# Optimizing a Trainium2 kernel written in Bass

```python
import jax, jax.numpy as jnp
from jax import lax
import numpy as np

D_MODEL = 2048
BATCH = 1
SEQ = 256
DEPTH = 1

N_META = 16
CHUNK = 64
MIX_WIDTH = D_MODEL
GLA_WIDTH = MIX_WIDTH // 2
POOL_WIDTH = MIX_WIDTH - GLA_WIDTH
GLA_HEADS = 4
GLA_DV = GLA_WIDTH // GLA_HEADS
GLA_DK = GLA_DV // 2
GLA_KW = GLA_HEADS * GLA_DK
GATE_RANK = 16
GATE_TAU = 16.0
POOL_WINDOWS = (2, 4, 8, 16)
POOL_GROUPS = len(POOL_WINDOWS)
POOL_GC = POOL_WIDTH // POOL_GROUPS
D_FF = 4 * D_MODEL
EPS = 1e-6
SPLIT_POINTS = (
    GLA_KW,
    2 * GLA_KW,
    2 * GLA_KW + GLA_WIDTH,
    2 * GLA_KW + 2 * GLA_WIDTH,
    2 * GLA_KW + 2 * GLA_WIDTH + GATE_RANK,
)
D_IN = 2 * GLA_KW + 2 * GLA_WIDTH + GATE_RANK + POOL_WIDTH


def rmsnorm(x, w):
    xf = x.astype(jnp.float32)
    y = xf * lax.rsqrt(jnp.mean(xf * xf, axis=-1, keepdims=True) + EPS)
    return (y * w.astype(jnp.float32)).astype(x.dtype)

def gla_chunked(q, k, v, logg):
    B, T, H, DK = q.shape
    DV = v.shape[-1]
    N = T // CHUNK

    def chunks(a):
        return a.reshape(B, N, CHUNK, H, a.shape[-1]).transpose(0, 3, 1, 2, 4)

    q, k, v, logg = chunks(q), chunks(k), chunks(v), chunks(logg)
    G = jnp.cumsum(logg, axis=3)
    G_last = G[:, :, :, -1:, :]
    q_dec = q * jnp.exp(G)
    k_inv = k * jnp.exp(-G)
    causal = jnp.tril(jnp.ones((CHUNK, CHUNK), dtype=bool))
    scores = jnp.einsum('bhncd,bhnsd->bhncs', q_dec, k_inv)
    scores = jnp.where(causal, scores, 0.0)
    o_intra = jnp.einsum('bhncs,bhnsv->bhncv', scores, v)
    k_to_end = k * jnp.exp(G_last - G)
    dS = jnp.einsum('bhncd,bhncv->bhndv', k_to_end, v)
    decay = jnp.exp(G_last[:, :, :, 0, :])

    def step(S, inp):
        dec, ds = inp
        return dec[..., None] * S + ds, S

    S0 = jnp.zeros((B, H, DK, DV), jnp.float32)
    _, S_prev = lax.scan(step, S0, (decay.transpose(2, 0, 1, 3), dS.transpose(2, 0, 1, 3, 4)))
    S_prev = S_prev.transpose(1, 2, 0, 3, 4)
    o_inter = jnp.einsum('bhncd,bhndv->bhncv', q_dec, S_prev)
    o = o_intra + o_inter
    return o.transpose(0, 2, 3, 1, 4).reshape(B, T, H, DV)

def multiscale_pool(pu, pool_w, pool_scale):
    B, L, _ = pu.shape
    xg = pu.astype(jnp.float32).reshape(B, L, POOL_GROUPS, POOL_GC)
    cs = jnp.pad(jnp.cumsum(xg, axis=1), ((0, 0), (1, 0), (0, 0), (0, 0)))
    t = jnp.arange(L)
    win = jnp.array(POOL_WINDOWS, dtype=jnp.int32)
    lo = jnp.maximum(t[:, None] + 1 - win[None, :], 0)
    g_idx = jnp.arange(POOL_GROUPS)[None, :]
    window_sum = cs[:, 1:] - cs[:, lo, g_idx]
    count = (t[:, None] + 1 - lo).astype(jnp.float32)[None, :, :, None]
    y = window_sum / count - xg
    y = jnp.einsum('blgc,gcd->blgd', y, pool_w.astype(jnp.float32))
    return y.reshape(B, L, POOL_WIDTH) * pool_scale.astype(jnp.float32)

def hybrid_layer(h, norm1_w, w_in, gate_w2, gate_b, gla_norm_w, pool_w, pool_scale,
                 w_out, norm2_w, mlp_w1, mlp_w2):
    B, L, _ = h.shape
    u = rmsnorm(h, norm1_w)
    proj = u @ w_in
    q, k, v, r, glr, pu = jnp.split(proj, SPLIT_POINTS, axis=-1)

    g_raw = (glr @ gate_w2 + gate_b).astype(jnp.float32)
    logg = jax.nn.log_sigmoid(g_raw) / GATE_TAU
    pad = (-N_META) % CHUNK

    def heads(a, d):
        a = a.astype(jnp.float32).reshape(B, L, GLA_HEADS, d)
        return jnp.pad(a, ((0, 0), (pad, 0), (0, 0), (0, 0)))

    o = gla_chunked(heads(q, GLA_DK) * (GLA_DK ** -0.5), heads(k, GLA_DK),
                    heads(v, GLA_DV), heads(logg, GLA_DK))[:, pad:]
    o = rmsnorm(o, gla_norm_w)
    gate_out = jax.nn.silu(r.astype(jnp.float32)).reshape(B, L, GLA_HEADS, GLA_DV)
    o_gla = (o * gate_out).reshape(B, L, GLA_WIDTH)

    o_pool = multiscale_pool(pu, pool_w, pool_scale)

    mixed = jnp.concatenate([o_gla, o_pool], axis=-1).astype(h.dtype)
    h = h + mixed @ w_out

    z = rmsnorm(h, norm2_w) @ mlp_w1
    h = h + jnp.square(jax.nn.relu(z)) @ mlp_w2
    return h

def first_inputs(seed: int = 0) -> dict:
    key = jax.random.key(seed)
    ks = jax.random.split(key, 16)
    f32 = jnp.float32
    nrm = lambda k, shape, s: jax.random.normal(k, shape, f32) * s
    return {
        "x": nrm(ks[0], (BATCH, SEQ, D_MODEL), 1.0),
        "meta_tokens": nrm(ks[1], (N_META, D_MODEL), 1.0),
        "norm1_w": 1.0 + nrm(ks[2], (DEPTH, D_MODEL), 0.02),
        "w_in": nrm(ks[3], (DEPTH, D_MODEL, D_IN), D_MODEL ** -0.5),
        "gate_w2": nrm(ks[4], (DEPTH, GATE_RANK, GLA_KW), GATE_RANK ** -0.5),
        "gate_b": nrm(ks[5], (DEPTH, GLA_KW), 0.1),
        "gla_norm_w": 1.0 + nrm(ks[6], (DEPTH, GLA_DV), 0.02),
        "pool_w": nrm(ks[7], (DEPTH, POOL_GROUPS, POOL_GC, POOL_GC), POOL_GC ** -0.5),
        "pool_scale": 1.0 + nrm(ks[8], (DEPTH, POOL_WIDTH), 0.1),
        "w_out": nrm(ks[9], (DEPTH, MIX_WIDTH, D_MODEL), MIX_WIDTH ** -0.5),
        "norm2_w": 1.0 + nrm(ks[10], (DEPTH, D_MODEL), 0.02),
        "mlp_w1": nrm(ks[11], (DEPTH, D_MODEL, D_FF), D_MODEL ** -0.5),
        "mlp_w2": nrm(ks[12], (DEPTH, D_FF, D_MODEL), D_FF ** -0.5),
        "final_norm_w": 1.0 + nrm(ks[13], (D_MODEL,), 0.02),
    }

def first_block(x, meta_tokens, norm1_w, w_in, gate_w2, gate_b, gla_norm_w, pool_w,
              pool_scale, w_out, norm2_w, mlp_w1, mlp_w2, final_norm_w):
    B = x.shape[0]
    meta = jnp.broadcast_to(meta_tokens[None].astype(x.dtype), (B, N_META, D_MODEL))
    h = jnp.concatenate([meta, x], axis=1)
    for i in range(DEPTH):
        h = hybrid_layer(h, norm1_w[i], w_in[i], gate_w2[i], gate_b[i], gla_norm_w[i],
                         pool_w[i], pool_scale[i], w_out[i], norm2_w[i], mlp_w1[i], mlp_w2[i])
    h = rmsnorm(h, final_norm_w)
    return h[:, N_META:]


HEAD_DIM = 128
N_HEADS_DSA = 8
N_HEADS_MOBA = 8
KV_LATENT = 256
IDX_HEADS = 16
IDX_DIM = 64
DSA_TOPK_MAX = 256
MOBA_BLOCK = 256
MOBA_TOPK_MAX = 3
N_MEM = 256
N_HEADS_MEM = 4
D_FF_2 = -(-8 * D_MODEL // (3 * 256)) * 256
ATTN_Q_BLOCK = 128
MOBA_Q_BLOCK = 64
DSA_WIDTH = N_HEADS_DSA * HEAD_DIM
MOBA_WIDTH = N_HEADS_MOBA * HEAD_DIM
MEM_WIDTH = N_HEADS_MEM * HEAD_DIM
SPLIT_SIZES = (DSA_WIDTH, KV_LATENT, IDX_HEADS * IDX_DIM, IDX_DIM, IDX_HEADS,
               MOBA_WIDTH, MOBA_WIDTH, MOBA_WIDTH, D_MODEL, D_MODEL)
IN_WIDTH = sum(SPLIT_SIZES)
ALPHA = (2.0 * DEPTH) ** 0.25
BETA = (8.0 * DEPTH) ** -0.25
LN_EPS = 1e-5


def layer_norm(x, g, b):
    xf = x.astype(jnp.float32)
    mu = xf.mean(-1, keepdims=True)
    var = jnp.square(xf - mu).mean(-1, keepdims=True)
    return ((xf - mu) * lax.rsqrt(var + LN_EPS) * g.astype(jnp.float32) + b.astype(jnp.float32)).astype(x.dtype)

def rms_norm(x, g):
    xf = x.astype(jnp.float32)
    return (xf * lax.rsqrt(jnp.mean(xf * xf, -1, keepdims=True) + LN_EPS) * g.astype(jnp.float32)).astype(x.dtype)

def alibi_slopes(n):
    return jnp.asarray([2.0 ** (-8.0 * (i + 1) / n) for i in range(n)], dtype=jnp.float32)

def dsa_attention(q, c_kv, q_idx, k_idx, w_idx, w_uk, w_uv):
    S = q.shape[0]
    topk = min(DSA_TOPK_MAX, S // 4)
    slopes = alibi_slopes(N_HEADS_DSA)
    q_lat = jnp.einsum('shd,hdc->shc', q, w_uk)
    key_pos = jnp.arange(S)
    idx_scale = IDX_DIM ** -0.5
    w_scale = IDX_HEADS ** -0.5

    def block(i):
        t0 = i * ATTN_Q_BLOCK
        qi = lax.dynamic_slice_in_dim(q_idx, t0, ATTN_Q_BLOCK, 0)
        wi = lax.dynamic_slice_in_dim(w_idx, t0, ATTN_Q_BLOCK, 0)
        ql = lax.dynamic_slice_in_dim(q_lat, t0, ATTN_Q_BLOCK, 0)
        qpos = t0 + jnp.arange(ATTN_Q_BLOCK)
        logits = jnp.einsum('thd,sd->ths', qi, k_idx, preferred_element_type=jnp.float32) * idx_scale
        score = jnp.einsum('th,ths->ts', wi.astype(jnp.float32) * w_scale, jax.nn.relu(logits))
        score = jnp.where(key_pos[None, :] <= qpos[:, None], score, -jnp.inf)
        _, sel = lax.top_k(score, topk)
        valid = sel <= qpos[:, None]
        c_sel = c_kv[sel]
        s = jnp.einsum('thc,tkc->thk', ql, c_sel, preferred_element_type=jnp.float32) * (HEAD_DIM ** -0.5)
        dist = (qpos[:, None] - sel).astype(jnp.float32)
        s = s - slopes[None, :, None] * dist[:, None, :]
        s = jnp.where(valid[:, None, :], s, -jnp.inf)
        p = jax.nn.softmax(s, axis=-1).astype(c_kv.dtype)
        return jnp.einsum('thk,tkc->thc', p, c_sel)

    o_lat = lax.map(block, jnp.arange(S // ATTN_Q_BLOCK)).reshape(S, N_HEADS_DSA, KV_LATENT)
    o = jnp.einsum('shc,hcd->shd', o_lat, w_uv)
    return o.reshape(S, DSA_WIDTH)

def moba_attention(q, k, v):
    S, H, Dh = q.shape
    n_blk = -(-S // MOBA_BLOCK)
    pad = n_blk * MOBA_BLOCK - S
    kb = jnp.pad(k, ((0, pad), (0, 0), (0, 0))).reshape(n_blk, MOBA_BLOCK, H, Dh).transpose(2, 0, 1, 3)
    vb = jnp.pad(v, ((0, pad), (0, 0), (0, 0))).reshape(n_blk, MOBA_BLOCK, H, Dh).transpose(2, 0, 1, 3)
    k_mean = kb.astype(jnp.float32).mean(axis=2)
    n_sel = min(MOBA_TOPK_MAX, n_blk - 1)
    n_past = n_sel * MOBA_BLOCK
    slopes = alibi_slopes(H)
    scale = Dh ** -0.5
    offs = jnp.arange(MOBA_BLOCK)
    blk_ids = jnp.arange(n_blk)
    head_ix = jnp.arange(H)[None, :, None]

    def block(i):
        t0 = i * MOBA_Q_BLOCK
        qi = lax.dynamic_slice_in_dim(q, t0, MOBA_Q_BLOCK, 0)
        qpos = t0 + jnp.arange(MOBA_Q_BLOCK)
        own = t0 // MOBA_BLOCK
        k_own = lax.dynamic_index_in_dim(kb, own, axis=1, keepdims=False)
        v_own = lax.dynamic_index_in_dim(vb, own, axis=1, keepdims=False)
        own_pos = own * MOBA_BLOCK + offs
        s_own = jnp.einsum('thd,hkd->thk', qi, k_own, preferred_element_type=jnp.float32) * scale
        s_own = s_own - slopes[None, :, None] * (qpos[:, None] - own_pos[None, :]).astype(jnp.float32)[:, None, :]
        s_own = jnp.where((own_pos[None, :] <= qpos[:, None])[:, None, :], s_own, -jnp.inf)
        if n_sel == 0:
            p = jax.nn.softmax(s_own, axis=-1).astype(v.dtype)
            return jnp.einsum('thk,hkd->thd', p, v_own)
        gate = jnp.einsum('thd,hnd->thn', qi.astype(jnp.float32), k_mean)
        gate = jnp.where(blk_ids[None, None, :] < own, gate, -jnp.inf)
        _, sel = lax.top_k(gate, n_sel)
        k_sel = kb[head_ix, sel]
        v_sel = vb[head_ix, sel].reshape(MOBA_Q_BLOCK, H, n_past, Dh)
        pos_sel = sel[..., None] * MOBA_BLOCK + offs
        s_sel = jnp.einsum('thd,thnkd->thnk', qi, k_sel, preferred_element_type=jnp.float32) * scale
        s_sel = s_sel - slopes[None, :, None, None] * (qpos[:, None, None, None] - pos_sel).astype(jnp.float32)
        s_sel = jnp.where((sel < own)[..., None], s_sel, -jnp.inf).reshape(MOBA_Q_BLOCK, H, n_past)
        s = jnp.concatenate([s_sel, s_own], axis=-1)
        p = jax.nn.softmax(s, axis=-1).astype(v.dtype)
        return (jnp.einsum('thk,thkd->thd', p[..., :n_past], v_sel)
                + jnp.einsum('thk,hkd->thd', p[..., n_past:], v_own))

    o = lax.map(block, jnp.arange(S // MOBA_Q_BLOCK))
    return o.reshape(S, H * Dh)

def hybrid_mixer(x, w_in, b_gate, kv_norm_g, idx_k_norm_g, idx_k_norm_b, w_uk, w_uv, w_o_dsa, w_o_moba, w_out):
    B, S, _ = x.shape
    points = np.cumsum(SPLIT_SIZES)[:-1].tolist()
    proj = x @ w_in
    q_dsa, c_kv, q_idx, k_idx, w_idx, q_m, k_m, v_m, ga, gb = jnp.split(proj, points, axis=-1)
    c_kv = rms_norm(c_kv, kv_norm_g)
    k_idx = layer_norm(k_idx, idx_k_norm_g, idx_k_norm_b)
    q_dsa = q_dsa.reshape(B, S, N_HEADS_DSA, HEAD_DIM)
    q_idx = q_idx.reshape(B, S, IDX_HEADS, IDX_DIM)
    o_a = jax.vmap(dsa_attention, in_axes=(0, 0, 0, 0, 0, None, None))(q_dsa, c_kv, q_idx, k_idx, w_idx, w_uk, w_uv)
    hm = (B, S, N_HEADS_MOBA, HEAD_DIM)
    o_b = jax.vmap(moba_attention)(q_m.reshape(hm), k_m.reshape(hm), v_m.reshape(hm))
    g_a = jax.nn.sigmoid(ga + b_gate[0])
    g_b = jax.nn.sigmoid(gb + b_gate[1])
    merged = g_a * (o_a @ w_o_dsa) + g_b * (o_b @ w_o_moba)
    return merged @ w_out

def mem_cross_attention(x, mem, w_q, w_kv, w_o):
    B, S, _ = x.shape
    q = (x @ w_q).reshape(B, S, N_HEADS_MEM, HEAD_DIM)
    k, v = jnp.split(mem @ w_kv, 2, axis=-1)
    k = k.reshape(B, N_MEM, N_HEADS_MEM, HEAD_DIM)
    v = v.reshape(B, N_MEM, N_HEADS_MEM, HEAD_DIM)
    s = jnp.einsum('bshd,bmhd->bhsm', q, k, preferred_element_type=jnp.float32) * (HEAD_DIM ** -0.5)
    p = jax.nn.softmax(s, axis=-1).astype(x.dtype)
    o = jnp.einsum('bhsm,bmhd->bshd', p, v).reshape(B, S, MEM_WIDTH)
    return o @ w_o

def swiglu(x, w_in, w_out):
    g, u = jnp.split(x @ w_in, 2, axis=-1)
    return (jax.nn.silu(g) * u) @ w_out

def second_inputs(seed: int = 0) -> dict:
    key = jax.random.key(seed)
    ks = jax.random.split(key, 20)
    f32 = jnp.float32

    def nrm(k, shape, scale):
        return jax.random.normal(k, shape, f32) * scale

    v_off = sum(SPLIT_SIZES[:7])
    col_scale = jnp.ones((IN_WIDTH,), f32).at[v_off:v_off + MOBA_WIDTH].set(BETA)
    kv_scale = jnp.ones((2 * MEM_WIDTH,), f32).at[MEM_WIDTH:].set(BETA)
    return {
        'x': nrm(ks[0], (BATCH, SEQ, D_MODEL), 1.0),
        'mem': nrm(ks[1], (BATCH, N_MEM, D_MODEL), 1.0),
        'w_in': nrm(ks[2], (DEPTH, D_MODEL, IN_WIDTH), D_MODEL ** -0.5) * col_scale,
        'b_gate': nrm(ks[3], (DEPTH, 2, D_MODEL), 0.02),
        'kv_norm_g': 1.0 + nrm(ks[4], (DEPTH, KV_LATENT), 0.02),
        'idx_k_norm_g': 1.0 + nrm(ks[5], (DEPTH, IDX_DIM), 0.02),
        'idx_k_norm_b': nrm(ks[6], (DEPTH, IDX_DIM), 0.02),
        'w_uk': nrm(ks[7], (DEPTH, N_HEADS_DSA, HEAD_DIM, KV_LATENT), HEAD_DIM ** -0.5),
        'w_uv': nrm(ks[8], (DEPTH, N_HEADS_DSA, KV_LATENT, HEAD_DIM), BETA * KV_LATENT ** -0.5),
        'w_o_dsa': nrm(ks[9], (DEPTH, DSA_WIDTH, D_MODEL), BETA * DSA_WIDTH ** -0.5),
        'w_o_moba': nrm(ks[10], (DEPTH, MOBA_WIDTH, D_MODEL), BETA * MOBA_WIDTH ** -0.5),
        'w_out': nrm(ks[11], (DEPTH, D_MODEL, D_MODEL), BETA * D_MODEL ** -0.5),
        'w_q_mem': nrm(ks[12], (DEPTH, D_MODEL, MEM_WIDTH), D_MODEL ** -0.5),
        'w_kv_mem': nrm(ks[13], (DEPTH, D_MODEL, 2 * MEM_WIDTH), D_MODEL ** -0.5) * kv_scale,
        'w_o_mem': nrm(ks[14], (DEPTH, MEM_WIDTH, D_MODEL), BETA * MEM_WIDTH ** -0.5),
        'w_ffn_in': nrm(ks[15], (DEPTH, D_MODEL, 2 * D_FF_2), BETA * D_MODEL ** -0.5),
        'w_ffn_out': nrm(ks[16], (DEPTH, D_FF_2, D_MODEL), BETA * D_FF_2 ** -0.5),
        'ln_g': 1.0 + nrm(ks[17], (DEPTH, 3, D_MODEL), 0.02),
        'ln_b': nrm(ks[18], (DEPTH, 3, D_MODEL), 0.02),
    }

def second_block(x, mem, w_in, b_gate, kv_norm_g, idx_k_norm_g, idx_k_norm_b, w_uk, w_uv, w_o_dsa, w_o_moba,
              w_out, w_q_mem, w_kv_mem, w_o_mem, w_ffn_in, w_ffn_out, ln_g, ln_b):
    for l in range(DEPTH):
        y = hybrid_mixer(x, w_in[l], b_gate[l], kv_norm_g[l], idx_k_norm_g[l], idx_k_norm_b[l], w_uk[l], w_uv[l],
                         w_o_dsa[l], w_o_moba[l], w_out[l])
        x = layer_norm(ALPHA * x + y, ln_g[l, 0], ln_b[l, 0])
        y = mem_cross_attention(x, mem, w_q_mem[l], w_kv_mem[l], w_o_mem[l])
        x = layer_norm(ALPHA * x + y, ln_g[l, 1], ln_b[l, 1])
        y = swiglu(x, w_ffn_in[l], w_ffn_out[l])
        x = layer_norm(ALPHA * x + y, ln_g[l, 2], ln_b[l, 2])
    return x


def setup_inputs(seed=0):
    out = dict(first_inputs(seed))
    for name, value in second_inputs(seed + 1).items():
        if name != "x":
            out[name + "_2"] = value
    return out


def reference(
    x, meta_tokens, norm1_w, w_in, gate_w2, gate_b, gla_norm_w, pool_w, pool_scale, w_out,
    norm2_w, mlp_w1, mlp_w2, final_norm_w, mem_2, w_in_2, b_gate_2, kv_norm_g_2, idx_k_norm_g_2,
    idx_k_norm_b_2, w_uk_2, w_uv_2, w_o_dsa_2, w_o_moba_2, w_out_2, w_q_mem_2, w_kv_mem_2,
    w_o_mem_2, w_ffn_in_2, w_ffn_out_2, ln_g_2, ln_b_2,
):
    x = first_block(
        x, meta_tokens, norm1_w, w_in, gate_w2, gate_b, gla_norm_w, pool_w, pool_scale, w_out,
        norm2_w, mlp_w1, mlp_w2, final_norm_w,
    )
    return second_block(
        x, mem_2, w_in_2, b_gate_2, kv_norm_g_2, idx_k_norm_g_2, idx_k_norm_b_2, w_uk_2, w_uv_2,
        w_o_dsa_2, w_o_moba_2, w_out_2, w_q_mem_2, w_kv_mem_2, w_o_mem_2, w_ffn_in_2,
        w_ffn_out_2, ln_g_2, ln_b_2,
    )


_drawn_inputs = setup_inputs


def setup_inputs(seed=0):
    import zlib

    import numpy as np

    out = dict(_drawn_inputs(seed))
    spreads = {}
    factors = {'norm1_w': 2.793,
     'gate_b': 3.238,
     'gla_norm_w': 6.375,
     'norm2_w': 3.283,
     'b_gate_2': 8.0,
     'kv_norm_g_2': 8.0,
     'idx_k_norm_g_2': 8.0,
     'idx_k_norm_b_2': 8.0}
    for name, (base, spread) in spreads.items():
        noise = np.random.default_rng([zlib.crc32(name.encode()), seed]).standard_normal(out[name].shape)
        drawn = base * np.exp(spread * noise) if base else spread * noise
        out[name] = __import__('jax').numpy.asarray(drawn.astype(out[name].dtype))
    for name, factor in factors.items():
        out[name] = (out[name] * factor).astype(out[name].dtype)
    return out
```

```python
from contextlib import ExitStack

import concourse.bass as bass
from concourse import mybir

F32 = mybir.dt.float32
F32R = mybir.dt.float32r
ACT = mybir.ActivationFunctionType
ALU = mybir.AluOpType
AX = mybir.AxisListType

P = 128
D = 2048
DC = D // P
SEQ = 256
META = 16
TOK = META + SEQ
X0 = META
GLA_H, GLA_DK, GLA_DV = 4, 128, 256
GLA_KW, GLA_W = GLA_H * GLA_DK, GLA_H * GLA_DV
CHUNK = 64
NCH = SEQ // CHUNK
GATE_RANK = 16
POOL_G, POOL_GC = 4, 256
D_FF = 8192
D_FF2 = 5632
H_DSA = 8
H_MOBA = 8
H_MEM = 4
IDX_H, IDX_D = 16, 64
TOPK = min(256, SEQ // 4)
EPS = 1e-6
LN_EPS = 1e-5
ALPHA = 2.0 ** 0.25
INV_SQRT_DH = 128 ** -0.5
NEG = -1e30
LOW = -1e38
TAKEN = -3e38

RAW = 4
CUT = 4
AHEAD = 3
BANKS = 4

C_Q, C_K, C_V, C_R, C_GLR = 0, GLA_KW, 2 * GLA_KW, 2 * GLA_KW + GLA_W, 2 * GLA_KW + 2 * GLA_W
C_PU = C_GLR + GATE_RANK
B_QD, B_CKV, B_QI, B_KI = 0, 1024, 1280, 2304
B_WI = B_KI + IDX_D
B_MOBA = B_WI + IDX_H
B_GATE = B_MOBA + 3 * 1024

V_N1, V_N2, V_FIN, V_GB, V_GLA, V_PS, V_KVN, V_BG = 0, 16, 32, 48, 52, 54, 62, 64
V_LG, V_LB, V_IG, V_IB = 96, 144, 192, 193

UP_GROUPS = 4
FF_GROUPS = 2
FF_CH = D_FF2 // P // FF_GROUPS

ALIBI = [2.0 ** (-8.0 * (i + 1) / H_MOBA) for i in range(H_MOBA)]


class Phase:

    def __init__(self, blocks, tiles):
        self.b0, self.t0 = Phase.b, Phase.t
        Phase.b += blocks
        Phase.t += tiles


def plan():
    Phase.b = Phase.t = 0
    ph = {}
    for name, blocks, tiles in (
        ("kv", 8, 8), ("glr", 2, 1), ("v", 8, 8), ("qk", 8, 8), ("r", 8, 8), ("pu", 8, 8),
        ("out", 16, 16), ("mlp", UP_GROUPS * 32, UP_GROUPS * 32),
        ("dsa", 20, 20), ("moba", 24, 24), ("gate", 32, 32), ("o", 16, 32), ("out2", 16, 16),
        ("qm", 4, 4), ("om", 4, 16), ("ffn", FF_GROUPS * (44 + 24), FF_GROUPS * (44 + 16)),
    ):
        ph[name] = Phase(blocks, tiles)
    ph["end"] = Phase(0, 0)
    steps, n = {}, 0
    for name, count in (
        ("vec", 2), ("memT", 8), ("xT", 16), ("n1", 1), ("vmT", 2), ("gate", 4),
        ("vT", 6), ("keT", 3), ("S", 16), ("sc", 2), ("o", 8), ("on", 2), ("pool", 8),
        ("n2", 1), ("nf", 1), ("ckv", 1), ("kmean", 1), ("kvar", 1), ("wT", 1), ("ckvT", 1),
        ("idx", 16), ("dsa", 5 * H_DSA), ("vmoT", 4), ("moba", 3 * H_MOBA),
        ("ln0", 2), ("mem", 3 * H_MEM), ("ln1", 2), ("ln2", 2), ("fin", 8),
    ):
        steps[name] = n
        n += count
    return ph, steps


def program(nc, A, out):
    ph, steps = plan()
    with ExitStack() as ctx:
        def sb(name, shape, dt=F32):
            return ctx.enter_context(nc.sbuf_tensor(name, shape, dt))

        def sem(name):
            return ctx.enter_context(nc.semaphore(name))

        raw = sb("raw", [P, RAW, 8, 256])
        w_hi = sb("w_hi", [P, CUT, 8, P], F32R)
        w_lo = sb("w_lo", [P, CUT, 8, P], F32R)
        xa = sb("xa", [P, DC, 2, TOK], F32R)
        h = sb("h", [P, DC, TOK])
        k_mem = sb("k_mem", [P, H_MEM, SEQ])
        v_mem = sb("v_mem", [P, 2, H_MEM * P])
        ident = sb("ident", [P, P])
        ones = sb("ones", [P, P])
        vec = sb("vec", [P, 194])
        ut = sb("ut", [P, 2, SEQ])
        rt = sb("rt", [P, 2, SEQ])
        acc = sb("acc", [P, TOK])
        mean = sb("mean", [P, TOK])
        rstd = sb("rstd", [P, TOK])
        rows = sb("rows", [P, 2, P])
        small = sb("small", [P, 32])
        top8 = sb("top8", [P, 2, 8])
        guard = nc.sbuf_tensor("xb", [P, FF_CH, 2, SEQ], F32R)
        xb = guard.__enter__()
        guard.__exit__(None, None, None)
        R = sb("region", [P, 20736])

        def reg(off, *shape, parts=P):
            size = 1
            for s in shape:
                size *= s
            v = R[0:parts, off:off + size]
            if len(shape) == 2:
                v = v.rearrange("p (a b) -> p a b", a=shape[0])
            if len(shape) == 3:
                v = v.rearrange("p (a b c) -> p a b c", a=shape[0], b=shape[1])
            return v

        ps = ctx.enter_context(nc.psum_tensor("ps", [P, 8, 512], F32))

        SQ = reg(8192, DC, TOK)
        meta_tok = reg(8192, D, parts=META)
        mem_tok = reg(12544, 2, D)
        x_tok = reg(16640, 2, D)
        vmT = reg(16640, H_MEM, SEQ)
        gs, gt = reg(0, GLA_H, TOK), reg(1088, GLA_H, TOK)
        e_pos, e_neg, e_end = reg(2176, GLA_H, TOK), reg(3264, GLA_H, TOK), reg(4352, GLA_H, TOK)
        q_dec, k_inv, k_end = reg(5440, GLA_H, TOK), reg(6528, GLA_H, TOK), reg(7616, GLA_H, TOK)
        vT = reg(8704, 8, TOK)
        r_silu = reg(10880, 8, SEQ)
        pu = reg(12928, 8, TOK)
        S = reg(15104, GLA_H, NCH, GLA_DV)
        reset = reg(15104, GLA_H, TOK)
        v_meta = reg(19200, 1024, parts=META)
        ke_meta = rt[0:META].rearrange("p a b -> p (a b)")
        glr = mean[0:GATE_RANK]
        gw2 = ut[0:GATE_RANK].rearrange("p a b -> p (a b)")
        v_tok = reg(0, 2, 1024)
        ke_tok = reg(3264, 2, 512)
        sc = reg(4352, 2, GLA_H, P)
        oT = reg(8704, 8, SEQ)
        o_sq = reg(15104, 8, SEQ)
        o_ss = reg(17152, GLA_H, SEQ)
        o_rs = reg(18176, GLA_H, SEQ)
        win_a, win_b = reg(0, 2, TOK), reg(544, 2, TOK)
        pool_y = reg(2176, 8, SEQ)
        pool_u = reg(15104, 8, SEQ)
        pool_w = reg(6528, 8, 256)
        qd, ckv, ki = reg(0, 8, SEQ), reg(2048, 2, SEQ), reg(2560, 2, SEQ)
        qi = reg(3072, 8, SEQ)
        kdup = reg(5120, SEQ)
        w_tok = reg(5376, 2, IDX_H)
        score, mbias = reg(5408, 2, SEQ), reg(5920, 2, SEQ)
        ckv_tok = reg(6944, 2, SEQ)
        uk, uv = reg(7456, H_DSA, 256), reg(9504, 2 * H_DSA, P)
        ql = reg(11552, 2, 512)
        sb_s = reg(12576, 2, 512)
        sb_pt = reg(13600, 2, 512)
        ol = reg(14624, 2, 512)
        sb_r = reg(15648, 2, 512)
        hb = reg(16672, 2, 512)
        csq = reg(17696, 2, SEQ)
        dist, distc = reg(18208, 2, SEQ), reg(18720, 2, SEQ)
        qm, km, vmo = reg(2048, 8, SEQ), reg(4096, 8, SEQ), reg(6144, 8, SEQ)
        vmo_tok = reg(8192, 2, 1024)
        gates = reg(8192, DC, 2, SEQ)
        m2 = reg(16384, 2, SEQ)
        qx = reg(0, H_MEM, SEQ)
        o_tok = reg(0, 2, D)

        loaded = [sem(f"loaded{i}") for i in range(RAW)]
        hi_made, lo_made = sem("hi_made"), sem("lo_made")
        piece_done = sem("piece_done")
        bank_free = [sem(f"bank_free{i}") for i in range(BANKS)]
        step_done = sem("step_done")
        side_free = [sem(f"side_free{i}") for i in range(BANKS)]
        rows_zero, rows_in = sem("rows_zero"), sem("rows_in")
        consts = sem("consts")
        mem_in, x_in, meta_in, gw_in = sem("mem_in"), sem("x_in"), sem("meta_in"), sem("gw_in")
        memhi = sem("memhi")
        sums = sem("sums")
        centered = sem("centered")
        squares = sem("squares")
        root = sem("root")
        normed = sem("normed")
        biased = sem("biased")
        xa_hi, xa_lo = sem("xa_hi"), sem("xa_lo")
        act_half, u_ready = sem("act_half"), sem("u_ready")
        xb_hi, xb_lo = sem("xb_hi"), sem("xb_lo")
        gate_z, gate_g, gate_e = sem("gate_z"), sem("gate_g"), sem("gate_e")
        sc_zero, sc_masked = sem("sc_zero"), sem("sc_masked")
        pool_in, uk_in, pool_ready = sem("pool_in"), sem("uk_in"), sem("pool_ready")
        pool_mv = sem("pool_mv")
        idx_relu, idx_acc = sem("idx_relu"), sem("idx_acc")
        kdup_ready, kdup_in = sem("kdup_ready"), sem("kdup_in")
        score_ready, score_cut, sel_ready, sel_cut = sem("score_ready"), sem("score_cut"), sem("sel_ready"), sem("sel_cut")
        dist_ready = sem("dist_ready")
        smax, sexp, pnorm = sem("smax"), sem("sexp"), sem("pnorm")
        out_done = sem("out_done")
        act_chain, dve_chain, pool_chain = sem("act_chain"), sem("dve_chain"), sem("pool_chain")

        block = ctx.enter_context(nc.Block())

        NORMS = {"n1": 0, "n2": 1, "nf": 2, "ln0": 3, "ln1": 4, "ln2": 5}
        LNS = {"ln0": 0, "ln1": 1, "ln2": 2}
        SUMS, SQS, MSQ = {}, {}, {}
        a = b = c = 0
        for name in ("n1", "on", "n2", "nf", "ckv", "kmean", "kvar", "ln0", "ln1", "ln2"):
            SUMS[name], SQS[name], MSQ[name] = a, b, c
            a += 2 if name in LNS else 1
            if name != "kmean":
                b += 1
                c += 1
        XA = {"n1": 0, "gla": 16, "pool": 24, "n2": 32, "nf": 48, "oa": 64, "ob": 72,
              "ln0": 80, "om": 96, "ln1": 100, "end": 116}
        XB = {"mlp": 0, "o": 64, "ffn": 80}
        UR = {"mlp": 0, "o": 64}
        HEADS = {"dsa": 0, "moba": H_DSA, "mem": H_DSA + H_MOBA}

        def step_bank(n):
            return ps[:, BANKS + n % BANKS, :]

        def tile_ps(ts, n):
            return ps[:, ts % BANKS, 0:n]

        def wait_tile_taken(eng, ts, td=0):
            eng.wait_ge(bank_free[ts % BANKS], td + (ts // BANKS + 1))

        def wait_tiles_taken(eng, end):
            for t in range(end - BANKS, end):
                wait_tile_taken(eng, t)

        def wait_step_taken(eng, n):
            eng.wait_ge(side_free[n % BANKS], n // BANKS + 1)

        def bank_for_step(eng, n):
            if n >= BANKS:
                wait_step_taken(eng, n - BANKS)

        @block.sync
        def _(sp):
            sp.dma_start(x_tok, A["x"][0].rearrange("(b p) n -> p b n", p=P)).then_inc(x_in, 16)

            def load(bs, bd, srcs):
                if not (isinstance(bd, int) and bs + bd < RAW):
                    sp.wait_ge(lo_made, bd * 2 + (2 * (bs - RAW) + 2))
                for dst, src in srcs:
                    sp.dma_start(dst, src).then_inc(loaded[bs % RAW], 32 // len(srcs))

            def halves(w):
                v = w.rearrange("(c p) n -> p c n", p=P)
                return v

            def pairs(b0, w, col, n_pairs, bd=0):
                v = halves(w)
                if n_pairs == 1:
                    for kb in range(2):
                        load(b0 + kb, bd, [(raw[:, (b0 + kb) % RAW], v[:, 8 * kb:8 * kb + 8, col:col + 256])])
                    return
                with sp.Fori(0, n_pairs // 2) as i:
                    for q in range(2):
                        for kb in range(2):
                            bs = b0 + 2 * q + kb
                            load(bs, bd + i * 4, [(raw[:, bs % RAW], v[:, 8 * kb:8 * kb + 8, bass.ds(i * 512 + (col + q * 256), 256)])])

            kvv = halves(A["w_kv_mem_2"][0])
            for b in range(8):
                q, kb = b // 2, b % 2
                load(b, 0, [(raw[:, b % RAW], kvv[:, 8 * kb:8 * kb + 8, 256 * q:256 * q + 256])])
            w_in = A["w_in"][0]
            pairs(ph["glr"].b0, w_in, C_GLR, 1)
            pairs(ph["v"].b0, w_in, C_V, 4)
            pairs(ph["qk"].b0, w_in, C_Q, 4)
            pairs(ph["r"].b0, w_in, C_R, 4)
            pairs(ph["pu"].b0, w_in, C_PU, 4)
            pairs(ph["out"].b0, A["w_out"][0], 0, 8)
            w1, w2 = halves(A["mlp_w1"][0]), halves(A["mlp_w2"][0])
            with sp.Fori(0, UP_GROUPS) as g:
                with sp.Fori(0, 4) as i:
                    for q in range(2):
                        for kb in range(2):
                            bs = ph["mlp"].b0 + 2 * q + kb
                            load(bs, g * 32 + i * 4, [(raw[:, bs % RAW], w1[:, 8 * kb:8 * kb + 8, bass.ds(g * 2048 + i * 512 + q * 256, 256)])])
                with sp.Fori(0, 4) as i:
                    for q in range(2):
                        for kb in range(2):
                            bs = ph["mlp"].b0 + 16 + 2 * q + kb
                            load(bs, g * 32 + i * 4, [(raw[:, bs % RAW], w2[:, bass.ds(g * 16 + 8 * kb, 8), bass.ds(i * 512 + q * 256, 256)])])
            w_in2 = A["w_in_2"][0]
            b = ph["dsa"].b0
            pairs(b, w_in2, B_CKV, 1)
            pairs(b + 2, w_in2, B_KI - IDX_D, 1)
            pairs(b + 4, w_in2, B_QI, 4)
            pairs(b + 12, w_in2, B_QD, 4)
            pairs(ph["moba"].b0, w_in2, B_MOBA, 12)
            pairs(ph["gate"].b0, w_in2, B_GATE, 16)
            woa, wob = halves(A["w_o_dsa_2"][0]), halves(A["w_o_moba_2"][0])
            with sp.Fori(0, 4) as i:
                for q in range(2):
                    for kb, v in enumerate((woa, wob)):
                        bs = ph["o"].b0 + 2 * q + kb
                        load(bs, i * 4, [(raw[:, bs % RAW], v[:, :, bass.ds(i * 512 + q * 256, 256)])])
            pairs(ph["out2"].b0, A["w_out_2"][0], 0, 8)
            pairs(ph["qm"].b0, A["w_q_mem_2"][0], 0, 2)
            wom = halves(A["w_o_mem_2"][0])
            for b in range(4):
                bs = ph["om"].b0 + b
                load(bs, 0, [(raw[:, bs % RAW].rearrange("p a b -> p (a b)").rearrange("p (c n) -> p c n", c=4),
                              wom[:, :, 512 * b:512 * b + 512])])
            wfi, wfo = halves(A["w_ffn_in_2"][0]), halves(A["w_ffn_out_2"][0])
            with sp.Fori(0, FF_GROUPS) as g:
                with sp.Fori(0, 11) as i:
                    for q in range(2):
                        for kb in range(2):
                            bs = ph["ffn"].b0 + 2 * q + kb
                            load(bs, g * 68 + i * 4,
                                 [(raw[:, bs % RAW, :, u * P:u * P + P],
                                   wfi[:, 8 * kb:8 * kb + 8, bass.ds(g * FF_CH * P + i * 256 + (u * D_FF2 + q * P), P)])
                                  for u in range(2)])
                with sp.Fori(0, 2) as i:
                    for q in range(4):
                        for kb, (c, n) in enumerate(((0, 8), (8, 8), (16, 6))):
                            bs = ph["ffn"].b0 + 44 + 3 * q + kb
                            load(bs, g * 68 + i * 12, [(raw[:, bs % RAW, 0:n], wfo[:, bass.ds(g * FF_CH + c, n), bass.ds(i * 1024 + q * 256, 256)])])
            o_v = out[0].rearrange("(b p) n -> p b n", p=P)
            for tb in range(2):
                for s in range(4):
                    wait_step_taken(sp, steps["fin"] + 4 * tb + s)
                sp.dma_start(o_v[:, tb], o_tok[:, tb]).then_inc(out_done, 16)
            sp.wait_ge(out_done, 32)

        @block.gpsimd
        def _(pool):
            chain = [0]

            def link(ins):
                chain[0] += 1
                ins.then_inc(pool_chain, 1)
                pool.wait_ge(pool_chain, chain[0])

            link(nc.gpsimd.memset(rows[:], 0.0))
            n_rows = 0
            for t, r0, src in (
                (0, V_N1, A["norm1_w"][0]), (0, V_N2, A["norm2_w"][0]), (0, V_FIN, A["final_norm_w"]),
                (0, V_GB, A["gate_b"][0]), (0, V_GLA, A["gla_norm_w"][0]), (0, V_PS, A["pool_scale"][0]),
                (0, V_KVN, A["kv_norm_g_2"][0]),
                (0, V_BG, A["b_gate_2"][0].rearrange("a n -> (a n)")),
                (1, V_LG - 96, A["ln_g_2"][0].rearrange("a n -> (a n)")),
                (1, V_LB - 96, A["ln_b_2"][0].rearrange("a n -> (a n)")),
            ):
                n = src.shape[0] // P
                pool.dma_start(rows[r0:r0 + n, t, :], src.rearrange("(c p) -> c p", p=P)).then_inc(rows_in, 16)
                n_rows += 1
            for r0, src in ((V_IG - 96, A["idx_k_norm_g_2"]), (V_IB - 96, A["idx_k_norm_b_2"])):
                pool.dma_start(rows[r0:r0 + 1, 1, IDX_D:2 * IDX_D], src).then_inc(rows_in, 16)
                n_rows += 1
            assert n_rows == 12
            pool.dma_start(mem_tok, A["mem_2"][0].rearrange("(b p) n -> p b n", p=P)).then_inc(mem_in, 16)
            pool.dma_start(meta_tok, A["meta_tokens"]).then_inc(meta_in, 16)
            pool.dma_start(gw2, A["gate_w2"][0]).then_inc(gw_in, 16)
            link(nc.gpsimd.memset(ident[:], 0.0))
            nc.gpsimd.affine_select(out=ident[:], in_=ident[:], compare_op=ALU.not_equal, fill=1.0, base=0,
                                    pattern=[[-1, P]], channel_multiplier=1).then_inc(consts, 1)
            nc.gpsimd.memset(ones[:], 1.0).then_inc(consts, 1)

            wait_step_taken(pool, steps["keT"] + 2)
            nc.gpsimd.memset(R[:, 4352:4352 + 1024], 0.0).then_inc(sc_zero, 1)
            for tb in range(2):
                wait_step_taken(pool, steps["sc"] + tb)
                nc.gpsimd.affine_select(out=sc[:, tb], in_=sc[:, tb], compare_op=ALU.is_ge, fill=0.0, base=0,
                                        pattern=[[0, GLA_H], [1, P]], channel_multiplier=-1).then_inc(sc_masked, 1)
            pool.dma_start(pool_w, A["pool_w"][0].rearrange("g (c p) d -> p (g c) d", p=P)).then_inc(pool_in, 16)

            pool.wait_ge(xa_lo, XA["nf"] + 16)
            for tb in range(2):
                link(nc.gpsimd.iota(dist[:, tb], pattern=[[1, SEQ]], base=-P * tb, channel_multiplier=-1,
                                    allow_small_or_imprecise_dtypes=True))
            nc.gpsimd.affine_select(out=distc[:], in_=dist[:], compare_op=ALU.is_ge, fill=-1e32, base=0,
                                    pattern=[[P, 2], [-1, SEQ]], channel_multiplier=1).then_inc(dist_ready, 1)
            pool.dma_start(uk, A["w_uk_2"][0].rearrange("h p c -> p h c")).then_inc(uk_in, 16)
            pool.dma_start(uv, A["w_uv_2"][0].rearrange("h (c p) d -> p (h c) d", p=P)).then_inc(uk_in, 16)
            pool.wait_ge(kdup_ready, 1)
            pool.dma_start(kdup[0:IDX_D], kdup[IDX_D:P]).then_inc(kdup_in, 16)
            pool.wait_ge(score_ready, 1)
            nc.gpsimd.affine_select(out=score[:], in_=score[:], compare_op=ALU.is_ge, fill=LOW, base=0,
                                    pattern=[[P, 2], [-1, SEQ]], channel_multiplier=1).then_inc(score_cut, 1)
            pool.wait_ge(sel_ready, 1)
            nc.gpsimd.affine_select(out=mbias[:], in_=mbias[:], compare_op=ALU.is_ge, fill=NEG, base=0,
                                    pattern=[[P, 2], [-1, SEQ]], channel_multiplier=1).then_inc(sel_cut, 1)

        @block.tensor
        def _(pe):
            def done(ins):
                ins.then_inc(step_done, 1)

            def pair(bs, bd, ts, td, rhs, n, blocks=(range(0, 8), range(8, 16)), ready=None, alone=False):
                for bi, chunks in enumerate(blocks):
                    for half in range(1 if alone else 2):
                        p = 2 * (bs + bi) + half
                        pe.wait_ge(lo_made, bd * 2 + (p + (2 if alone else 1)))
                        if bi == 0:
                            t = ts + half
                            if not (isinstance(td, int) and t + td < BANKS):
                                pe.wait_ge(bank_free[t % BANKS], _div4(td) + t // BANKS)
                        o = tile_ps(ts + half, n)
                        for ci, c in enumerate(chunks):
                            if ready is not None and half == 0:
                                ready(c)
                            hi, lo = w_hi[:, p % CUT, ci], w_lo[:, p % CUT, ci]
                            x_hi, x_lo = rhs(c)
                            first, last = bi == 0 and ci == 0, bi == len(blocks) - 1 and ci == len(chunks) - 1
                            nc.tensor.matmul(o, hi, x_hi, start=first, stop=False)
                            nc.tensor.matmul(o, hi, x_lo, start=False, stop=False)
                            ins = nc.tensor.matmul(o, lo, x_hi, start=False, stop=last)
                        ins.then_inc(piece_done, 2 if alone else 1)

            def _div4(td):
                return td if isinstance(td, int) and td == 0 else td

            def from_xa(n):
                return lambda c: (xa[:, c, 0, 0:n], xa[:, c, 1, 0:n])

            def from_xb(c):
                return xb[:, c, 0, :], xb[:, c, 1, :]

            def chunk_of_xa(base):
                def ready(c):
                    if c % 4 == 0:
                        pe.wait_ge(xa_lo, base + c + 4)
                return ready

            def run(phase, n_pairs, rhs, n, ready=None, skip=0):
                b0, t0 = phase.b0 + 2 * skip, phase.t0 + 2 * skip
                first = 0
                if ready is not None:
                    pair(b0, 0, t0, 0, rhs, n, ready=ready)
                    pair(b0 + 2, 0, t0 + 2, 0, rhs, n)
                    first = 1
                if n_pairs // 2 > first:
                    with pe.Fori(first, n_pairs // 2) as i:
                        for q in range(2):
                            pair(b0 + 2 * q, i * 4, t0 + 2 * q, i, rhs, n)

            pe.wait_ge(consts, 2)
            pe.wait_ge(rows_in, 12 * 16)
            for t in range(2):
                done(nc.tensor.transpose(step_bank(steps["vec"] + t)[:, 0:P], rows[:, t, :], ident[:]))
            pe.wait_ge(mem_in, 16)
            for s in range(8):
                n = steps["memT"] + s
                bank_for_step(pe, n)
                b = step_bank(n)
                for c in range(2):
                    for tb in range(2):
                        ins = nc.tensor.transpose(b[:, c * 256 + tb * P:c * 256 + tb * P + P],
                                                  mem_tok[:, tb, (2 * s + c) * P:(2 * s + c + 1) * P], ident[:])
                done(ins)
            pe.wait_ge(x_in, 16)
            pe.wait_ge(meta_in, 16)
            for c in range(DC):
                n = steps["xT"] + c
                bank_for_step(pe, n)
                b = step_bank(n)
                nc.tensor.transpose(b[:, 0:META], meta_tok[:, c * P:c * P + P], ident[0:META, 0:META])
                for tb in range(2):
                    ins = nc.tensor.transpose(b[:, X0 + tb * P:X0 + tb * P + P], x_tok[:, tb, c * P:c * P + P], ident[:])
                done(ins)

            for s in range(8):
                wait_step_taken(pe, steps["memT"] + s)
            for q in range(4):
                pair(2 * q, 0, 2 * q, 0, from_xb, SEQ)

            def ones_step(n, src, k, parts=slice(0, P)):
                bank_for_step(pe, n)
                pe.wait_ge(sums, k + 1)
                done(nc.tensor.matmul(step_bank(n)[:, 0:src.shape[-1]], ones[parts, :], src, start=True, stop=True))

            ones_step(steps["n1"], acc[:], SUMS["n1"])
            for tb in range(2):
                n = steps["vmT"] + tb
                bank_for_step(pe, n)
                wait_tiles_taken(pe, ph["kv"].t0 + 8)
                for j in range(H_MEM):
                    ins = nc.tensor.transpose(step_bank(n)[:, j * P:j * P + P], vmT[:, j, tb * P:tb * P + P], ident[:])
                done(ins)

            f = ph["glr"]
            pair(f.b0, 0, f.t0, 0, from_xa(TOK), TOK, ready=chunk_of_xa(XA["n1"]), alone=True)
            run(ph["v"], 4, from_xa(TOK), TOK)
            pe.wait_ge(gw_in, 16)
            wait_tile_taken(pe, ph["glr"].t0)
            for j in range(GLA_H):
                n = steps["gate"] + j
                bank_for_step(pe, n)
                done(nc.tensor.matmul(step_bank(n)[:, 0:TOK], gw2[:, j * P:j * P + P], glr, start=True, stop=True))
            run(ph["qk"], 4, from_xa(TOK), TOK)
            run(ph["r"], 4, from_xa(TOK), TOK)
            run(ph["pu"], 4, from_xa(TOK), TOK)

            wait_tiles_taken(pe, ph["r"].t0)
            for t in range(4):
                wait_tile_taken(pe, ph["qk"].t0 + t)
            n = steps["vT"]
            for tb in range(3):
                w = META if tb == 2 else P
                o = 0 if tb == 2 else X0 + tb * P
                for jh in range(2):
                    bank_for_step(pe, n)
                    for j in range(4):
                        ins = nc.tensor.transpose(step_bank(n)[0:w, j * P:j * P + P], vT[:, 4 * jh + j, o:o + w], ident[:])
                    done(ins)
                    n += 1
            for tb in range(3):
                w = META if tb == 2 else P
                o = 0 if tb == 2 else X0 + tb * P
                bank_for_step(pe, n)
                for j in range(GLA_H):
                    ins = nc.tensor.transpose(step_bank(n)[0:w, j * P:j * P + P], k_end[:, j, o:o + w], ident[:])
                done(ins)
                n += 1
            for s in range(6):
                wait_step_taken(pe, steps["vT"] + s)
            for s in range(3):
                wait_step_taken(pe, steps["keT"] + s)
            for j in range(GLA_H):
                for c in range(NCH):
                    n = steps["S"] + NCH * j + c
                    bank_for_step(pe, n)
                    o = step_bank(n)[:, 0:GLA_DV]
                    if c == 0:
                        ins = nc.tensor.matmul(o, ke_meta[:, j * P:j * P + P], v_meta[:, j * GLA_DV:(j + 1) * GLA_DV], start=True, stop=True)
                    else:
                        tb, r = (c - 1) // 2, CHUNK * ((c - 1) % 2)
                        ins = nc.tensor.matmul(o, ke_tok[r:r + CHUNK, tb, j * P:j * P + P],
                                               v_tok[r:r + CHUNK, tb, j * GLA_DV:(j + 1) * GLA_DV], start=True, stop=True)
                    done(ins)
            for tb in range(2):
                n = steps["sc"] + tb
                bank_for_step(pe, n)
                for j in range(GLA_H):
                    for r in (0, CHUNK):
                        o = X0 + tb * P + r
                        ins = nc.tensor.matmul(step_bank(n)[r:r + CHUNK, j * P + r:j * P + r + CHUNK],
                                               k_inv[:, j, o:o + CHUNK], q_dec[:, j, o:o + CHUNK], start=True, stop=True)
                done(ins)
            pe.wait_ge(sc_masked, 2)
            for s in range(16):
                wait_step_taken(pe, steps["S"] + s)
            for j in range(GLA_H):
                for vh in range(2):
                    n = steps["o"] + 2 * j + vh
                    bank_for_step(pe, n)
                    o = step_bank(n)
                    col = j * GLA_DV + vh * P
                    for tb in range(2):
                        nc.tensor.matmul(o[:, tb * P:tb * P + P], v_tok[:, tb, col:col + P], sc[:, tb, j], start=tb == 0, stop=False)
                    for c in range(NCH):
                        ins = nc.tensor.matmul(o[:, c * CHUNK:(c + 1) * CHUNK], S[:, j, c, vh * P:vh * P + P],
                                               q_dec[:, j, X0 + c * CHUNK:X0 + (c + 1) * CHUNK], start=False, stop=c == NCH - 1)
                    done(ins)
            pe.wait_ge(sums, SUMS["on"] + 1)
            for s in range(2):
                n = steps["on"] + s
                bank_for_step(pe, n)
                done(nc.tensor.matmul(step_bank(n), ones[:], R[:, 17152 + 512 * s:17152 + 512 * s + 512], start=True, stop=True))
            pe.wait_ge(pool_in, 16)
            pe.wait_ge(pool_ready, 1)
            for g in range(POOL_G):
                for dt in range(2):
                    n = steps["pool"] + 2 * g + dt
                    bank_for_step(pe, n)
                    for c in range(2):
                        ins = nc.tensor.matmul(step_bank(n)[:, 0:SEQ], pool_w[:, 2 * g + c, dt * P:dt * P + P], pool_y[:, 2 * g + c],
                                               start=c == 0, stop=c == 1)
                    done(ins)
            def ready_mix(c):
                if c == 0:
                    pe.wait_ge(xa_lo, XA["pool"])
                if c == 8:
                    pe.wait_ge(xa_lo, XA["pool"] + 8)

            run(ph["out"], 8, from_xa(SEQ), SEQ, ready=ready_mix)
            ones_step(steps["n2"], acc[:, 0:SEQ], SUMS["n2"])

            for q in range(0):
                pass
            pe.wait_ge(xa_lo, XA["n2"] + 16)
            with pe.Fori(0, UP_GROUPS) as g:
                with pe.Fori(0, 4) as i:
                    for q in range(2):
                        pair(ph["mlp"].b0 + 2 * q, g * 32 + i * 4, ph["mlp"].t0 + 2 * q, g * 8 + i, from_xa(SEQ), SEQ)

                def hidden(c):
                    pe.wait_ge(xb_lo, g * 16 + (XB["mlp"] + c + 1))

                pair(ph["mlp"].b0 + 16, g * 32, ph["mlp"].t0 + 16, g * 8, from_xb, SEQ, ready=hidden)
                pair(ph["mlp"].b0 + 18, g * 32, ph["mlp"].t0 + 18, g * 8, from_xb, SEQ)
                with pe.Fori(1, 4) as i:
                    for q in range(2):
                        pair(ph["mlp"].b0 + 16 + 2 * q, g * 32 + i * 4, ph["mlp"].t0 + 16 + 2 * q, g * 8 + i, from_xb, SEQ)
            ones_step(steps["nf"], acc[:, 0:SEQ], SUMS["nf"])

            run(ph["dsa"], 10, from_xa(SEQ), SEQ, ready=chunk_of_xa(XA["nf"]))
            ones_step(steps["ckv"], csq[:, 0], SUMS["ckv"])
            ones_step(steps["kmean"], ki[IDX_D:P, 0], SUMS["kmean"], slice(IDX_D, P))
            ones_step(steps["kvar"], csq[IDX_D:P, 1], SUMS["kvar"], slice(IDX_D, P))
            n = steps["wT"]
            bank_for_step(pe, n)
            for tb in range(2):
                ins = nc.tensor.transpose(step_bank(n)[:, tb * IDX_H:(tb + 1) * IDX_H], ki[0:IDX_H, 1, tb * P:tb * P + P],
                                          ident[0:IDX_H, 0:IDX_H])
            done(ins)
            n = steps["ckvT"]
            bank_for_step(pe, n)
            pe.wait_ge(normed, 16 * 3 + 2)
            for tb in range(2):
                for c in range(2):
                    ins = nc.tensor.transpose(step_bank(n)[:, tb * 256 + c * P:tb * 256 + c * P + P], ckv[:, c, tb * P:tb * P + P], ident[:])
            done(ins)
            pe.wait_ge(kdup_in, 16)
            for j in range(IDX_H):
                n = steps["idx"] + j
                bank_for_step(pe, n)
                r = IDX_D * (j % 2)
                for tb in range(2):
                    ins = nc.tensor.matmul(step_bank(n)[:, tb * SEQ:(tb + 1) * SEQ], qi[r:r + IDX_D, j // 2, tb * P:tb * P + P],
                                           kdup[r:r + IDX_D], start=True, stop=True)
                done(ins)

            def transpose_p(n, k):
                bank_for_step(pe, n)
                pe.wait_ge(pnorm, k + 1)
                s = sb_s[:, k % 2].rearrange("p (b n) -> p b n", b=2)
                for kb in range(2):
                    for tb in range(2):
                        ins = nc.tensor.transpose(step_bank(n)[:, kb * SEQ + tb * P:kb * SEQ + tb * P + P], s[:, tb, kb * P:kb * P + P], ident[:])
                done(ins)

            def pt(k, kb):
                return sb_pt[:, k % 2, kb * SEQ:(kb + 1) * SEQ]

            pe.wait_ge(uk_in, 32)
            wait_step_taken(pe, steps["ckvT"])
            for it in range(H_DSA + 1):
                if it < H_DSA:
                    n = steps["dsa"] + 5 * it
                    bank_for_step(pe, n)
                    for c in range(2):
                        ins = nc.tensor.matmul(step_bank(n)[:, c * SEQ:(c + 1) * SEQ], uk[:, it, c * P:c * P + P], qd[:, it], start=True, stop=True)
                    done(ins)
                    bank_for_step(pe, n + 1)
                    wait_step_taken(pe, n)
                    for tb in range(2):
                        for c in range(2):
                            ins = nc.tensor.matmul(step_bank(n + 1)[:, tb * SEQ:(tb + 1) * SEQ],
                                                   ql[:, it % 2, c * SEQ + tb * P:c * SEQ + tb * P + P], ckv[:, c], start=c == 0, stop=c == 1)
                    done(ins)
                    dsa_scores = n
                if it > 0:
                    pass
                if it < H_DSA:
                    k = HEADS["dsa"] + it
                    transpose_p(n + 2, k)
                    bank_for_step(pe, n + 3)
                    wait_step_taken(pe, n + 2)
                    for c in range(2):
                        for kb in range(2):
                            ins = nc.tensor.matmul(step_bank(n + 3)[:, c * SEQ:(c + 1) * SEQ], ckv_tok[:, kb, c * P:c * P + P], pt(k, kb),
                                                   start=kb == 0, stop=kb == 1)
                    done(ins)
                    bank_for_step(pe, n + 4)
                    wait_step_taken(pe, n + 3)
                    for c in range(2):
                        ins = nc.tensor.matmul(step_bank(n + 4)[:, 0:SEQ], uv[:, 2 * it + c], ol[:, it % 2, c * SEQ:(c + 1) * SEQ],
                                               start=c == 0, stop=c == 1)
                    done(ins)

            run(ph["moba"], 12, from_xa(SEQ), SEQ)
            wait_tiles_taken(pe, ph["moba"].t0 + 24)
            n = steps["vmoT"]
            for tb in range(2):
                for jh in range(2):
                    bank_for_step(pe, n)
                    for j in range(4):
                        ins = nc.tensor.transpose(step_bank(n)[:, j * P:j * P + P], vmo[:, 4 * jh + j, tb * P:tb * P + P], ident[:])
                    done(ins)
                    n += 1

            def attend(name, heads, q, k_src, v):
                for j in range(heads):
                    n = steps[name] + 3 * j
                    k = HEADS[name] + j
                    bank_for_step(pe, n)
                    for tb in range(2):
                        ins = nc.tensor.matmul(step_bank(n)[:, tb * SEQ:(tb + 1) * SEQ], q[:, j, tb * P:tb * P + P], k_src[:, j], start=True, stop=True)
                    done(ins)
                    transpose_p(n + 1, k)
                    bank_for_step(pe, n + 2)
                    wait_step_taken(pe, n + 1)
                    for kb in range(2):
                        ins = nc.tensor.matmul(step_bank(n + 2)[:, 0:SEQ], v[:, kb, j * P:j * P + P], pt(k, kb), start=kb == 0, stop=kb == 1)
                    done(ins)

            for s in range(4):
                wait_step_taken(pe, steps["vmoT"] + s)
            attend("moba", H_MOBA, qm, km, vmo_tok)
            run(ph["gate"], 16, from_xa(SEQ), SEQ)

            pe.wait_ge(xa_lo, XA["ob"] + 8)
            with pe.Fori(0, 4) as i:
                for q in range(2):
                    for kb in range(2):
                        pair(ph["o"].b0 + 2 * q + kb, i * 4, ph["o"].t0 + 4 * q + 2 * kb, i * 2, from_xa(SEQ), SEQ,
                             blocks=(range(8 * kb, 8 * kb + 8),))

            def merged(c):
                pe.wait_ge(xb_lo, XB["o"] + c + 1)

            f = ph["out2"]
            pair(f.b0, 0, f.t0, 0, from_xb, SEQ, ready=merged)
            pair(f.b0 + 2, 0, f.t0 + 2, 0, from_xb, SEQ)
            with pe.Fori(1, 4) as i:
                for q in range(2):
                    pair(f.b0 + 2 * q, i * 4, f.t0 + 2 * q, i, from_xb, SEQ)

            ones_step(steps["ln0"], acc[:, 0:SEQ], SUMS["ln0"])
            ones_step(steps["ln0"] + 1, acc[:, 0:SEQ], SUMS["ln0"] + 1)
            run(ph["qm"], 2, from_xa(SEQ), SEQ, ready=chunk_of_xa(XA["ln0"]))
            wait_tiles_taken(pe, ph["qm"].t0 + 4)
            for tb in range(2):
                wait_step_taken(pe, steps["vmT"] + tb)
            attend("mem", H_MEM, qx, k_mem, v_mem)

            pe.wait_ge(xa_lo, XA["om"] + 4)
            for b in range(4):
                bs = ph["om"].b0 + b
                for half in range(2):
                    p = 2 * bs + half
                    pe.wait_ge(lo_made, p + 1)
                    for q in range(2):
                        t = ph["om"].t0 + 4 * b + 2 * half + q
                        pe.wait_ge(bank_free[t % BANKS], t // BANKS)
                        o = tile_ps(t, SEQ)
                        for c in range(4):
                            hi, lo = w_hi[:, p % CUT, 2 * c + q], w_lo[:, p % CUT, 2 * c + q]
                            x_hi, x_lo = xa[:, c, 0, 0:SEQ], xa[:, c, 1, 0:SEQ]
                            nc.tensor.matmul(o, hi, x_hi, start=c == 0, stop=False)
                            nc.tensor.matmul(o, hi, x_lo, start=False, stop=False)
                            ins = nc.tensor.matmul(o, lo, x_hi, start=False, stop=c == 3)
                    ins.then_inc(piece_done, 1)
            ones_step(steps["ln1"], acc[:, 0:SEQ], SUMS["ln1"])
            ones_step(steps["ln1"] + 1, acc[:, 0:SEQ], SUMS["ln1"] + 1)

            pe.wait_ge(xa_lo, XA["ln1"] + 16)
            fb, ft = ph["ffn"].b0, ph["ffn"].t0
            with pe.Fori(0, FF_GROUPS) as g:
                with pe.Fori(0, 11) as i:
                    for q in range(2):
                        pair(fb + 2 * q, g * 68 + i * 4, ft + 2 * q, g * 15 + i, from_xa(SEQ), SEQ)

                def hidden2(c):
                    pe.wait_ge(xb_lo, g * FF_CH + (XB["ffn"] + c + 1))

                three = (range(0, 8), range(8, 16), range(16, 22))
                with pe.Fori(0, 2) as i:
                    for q in range(4):
                        pair(fb + 44 + 3 * q, g * 68 + i * 12, ft + 44 + 2 * q, g * 15 + i * 2, from_xb, SEQ,
                             blocks=three, ready=hidden2 if q == 0 else None)
            ones_step(steps["ln2"], acc[:, 0:SEQ], SUMS["ln2"])
            ones_step(steps["ln2"] + 1, acc[:, 0:SEQ], SUMS["ln2"] + 1)
            pe.wait_ge(biased, 16 * 3)
            for tb in range(2):
                for s in range(4):
                    n = steps["fin"] + 4 * tb + s
                    bank_for_step(pe, n)
                    for j in range(4):
                        ins = nc.tensor.transpose(step_bank(n)[:, j * P:j * P + P], h[:, 4 * s + j, X0 + tb * P:X0 + tb * P + P], ident[:])
                    done(ins)

        @block.scalar
        def _(act):
            chain = [0]

            def link(ins):
                chain[0] += 1
                ins.then_inc(act_chain, 1)
                act.wait_ge(act_chain, chain[0])

            def cut(ps_, pd):
                bs = ps_ // 2
                act.wait_ge(loaded[bs % RAW], pd * 4 + 32 * (bs // RAW + 1))
                if not (isinstance(pd, int) and ps_ + pd < CUT):
                    act.wait_ge(piece_done, pd + (ps_ - CUT + 1))
                nc.scalar.activation(w_hi[:, ps_ % CUT], raw[:, bs % RAW, :, (ps_ % 2) * P:(ps_ % 2) * P + P], ACT.Copy).then_inc(hi_made, 1)

            END = 2 * ph["end"].b0

            def body(b0, bd, t0, td, evac, n_pairs=2, per_pair=2, last=False):
                for q in range(n_pairs):
                    for k in range(2 * per_pair):
                        p = 2 * (b0 + per_pair * q) + k
                        if not (last and p + AHEAD >= END_STATIC[0]):
                            cut(p + AHEAD, bd * 2)
                        if k >= 2 * per_pair - 2:
                            t = 2 * q + k - (2 * per_pair - 2)
                            last_piece[:] = p, bd * 2
                            evac(t0 + t, td, t)

            END_STATIC = [1 << 30]

            last_piece = [0, 0]

            def complete():
                act.wait_ge(piece_done, last_piece[1] + (last_piece[0] + 1))

            def free(ins, ts):
                ins.then_inc(bank_free[ts % BANKS], 1)

            def take(n, ins_fn):
                act.wait_ge(step_done, n + 1)
                return ins_fn(step_bank(n)).then_inc(side_free[n % BANKS], 1)

            for t in range(2):
                w = 96 if t == 0 else 98
                take(steps["vec"] + t, lambda b: nc.scalar.activation(vec[:, 96 * t:96 * t + w], b[:, 0:w], ACT.Copy))
            for s in range(8):
                n = steps["memT"] + s
                act.wait_ge(step_done, n + 1)
                nc.scalar.activation(xb[:, 2 * s:2 * s + 2, 0, :], step_bank(n).rearrange("p (c n) -> p c n", c=2), ACT.Copy).then_inc(memhi, 1)
            for c in range(DC):
                take(steps["xT"] + c, lambda b: nc.scalar.activation(h[:, c, :], b[:, 0:TOK], ACT.Copy))
            for p in range(AHEAD):
                cut(p, 0)

            def norm_squares(name, n, off):
                if name == "n1":
                    wait_step_taken(act, steps["xT"] + 15)
                    wait_step_taken(act, steps["xT"] + 14)
                elif name in LNS:
                    act.wait_ge(centered, LNS[name] + 1)
                else:
                    wait_tiles_taken(act, ph[{"n2": "mlp", "nf": "dsa"}[name]].t0)
                for q in range(4):
                    ins = nc.scalar.activation(SQ[:, 4 * q:4 * q + 4, 0:n], h[:, 4 * q:4 * q + 4, off:off + n], ACT.Square)
                ins.then_inc(squares, 1)

            def norm_root(step, dst):
                wait_step_taken(act, step)
                nc.scalar.activation(dst, dst, ACT.Sqrt).then_inc(root, 1)

            def norm_cut(name, n, off, src):
                k = NORMS[name]
                for q in range(4):
                    act.wait_ge(normed, 16 * k + 4 * q + 4 + (2 if k > 2 else 0))
                    if name in LNS:
                        l = LNS[name]
                        for c in range(4 * q, 4 * q + 4):
                            ins = nc.scalar.activation(h[:, c, off:off + n], h[:, c, off:off + n], ACT.Identity,
                                                       bias=vec[:, V_LB + 16 * l + c:V_LB + 16 * l + c + 1]).then_inc(biased, 1)
                        act.wait_ge(biased, 16 * l + 4 * q + 4)
                    if name != "ln2":
                        nc.scalar.activation(xa[:, 4 * q:4 * q + 4, 0, 0:n], src[:, 4 * q:4 * q + 4, off:off + n] if src is h else src[:, 4 * q:4 * q + 4, 0:n],
                                             ACT.Copy).then_inc(xa_hi, 4)

            norm_squares("n1", TOK, 0)

            def ev_kv(ts, td, t):
                complete()
                dst = k_mem[:, ts] if ts < H_MEM else vmT[:, ts - H_MEM]
                free(nc.scalar.activation(dst, tile_ps(ts, SEQ), ACT.Copy), ts)

            act.wait_ge(consts, 2)
            for q in range(4):
                body(2 * q, 0, 2 * q, 0, ev_kv, n_pairs=1)
            norm_root(steps["n1"], rstd[:])
            norm_cut("n1", TOK, 0, SQ)
            for tb in range(2):
                take(steps["vmT"] + tb, lambda b: nc.scalar.activation(v_mem[:, tb], b, ACT.Copy))

            f = ph["glr"]
            for k in range(4):
                cut(2 * f.b0 + k + AHEAD, 0)
            last_piece[:] = 2 * f.b0 + 3, 0
            complete()
            free(nc.scalar.activation(glr, tile_ps(f.t0, TOK)[0:GATE_RANK], ACT.Copy), f.t0)

            def run(phase, n_pairs, evac, skip=0):
                b0, t0 = phase.b0 + 2 * skip, phase.t0 + 2 * skip
                with act.Fori(0, n_pairs // 2) as i:
                    body(b0, i * 4, t0, i, lambda ts, td, t: evac(ts, td, t, i))

            def copy_loop(buf, base=0, n=SEQ):
                def ev(ts, td, t, i):
                    complete()
                    free(nc.scalar.activation(buf[:, bass.ds(i * 4 + (base + t), 1), :], tile_ps(ts, n).unsqueeze(1), ACT.Copy), ts)
                return ev

            run(ph["v"], 4, copy_loop(vT, n=TOK))
            for j in range(GLA_H):
                take(steps["gate"] + j, lambda b: nc.scalar.activation(gs[:, j], b[:, 0:TOK], ACT.Identity, bias=vec[:, V_GB + j:V_GB + j + 1]))
            for j in range(GLA_H):
                wait_step_taken(act, steps["gate"] + j)
            link(nc.scalar.activation(gt[:], gs[:], ACT.Abs))
            link(nc.scalar.activation(gt[:], gt[:], ACT.Exp, scale=-1.0))
            nc.scalar.activation(gt[:], gt[:], ACT.Ln, bias=1.0).then_inc(gate_z, 1)
            act.wait_ge(gate_g, 1)
            nc.scalar.activation(e_pos[:], gs[:], ACT.Exp, scale=1.0 / 16).then_inc(gate_e, 1)
            nc.scalar.activation(e_neg[:], gs[:], ACT.Exp, scale=-1.0 / 16).then_inc(gate_e, 1)
            act.wait_ge(gate_g, 2)
            nc.scalar.activation(e_end[:], gt[:], ACT.Exp, scale=1.0 / 16).then_inc(gate_e, 1)

            def nothing(ts, td, t, i=None):
                pass

            run(ph["qk"], 4, nothing)

            def ev_r(ts, td, t, i):
                complete()
                wait_tile_taken(act, ts - 2, td)
                nc.scalar.activation(rt[:, t % 2], tile_ps(ts, TOK)[:, X0:TOK], ACT.Sigmoid).then_inc(act_half, 1)

            run(ph["r"], 4, ev_r)
            run(ph["pu"], 4, copy_loop(pu, n=TOK))

            n = steps["vT"]
            for tb in range(3):
                for jh in range(2):
                    w = META if tb == 2 else P
                    dst = v_meta[:, 512 * jh:512 * jh + 512] if tb == 2 else v_tok[:, tb, 512 * jh:512 * jh + 512]
                    take(n, lambda b: nc.scalar.activation(dst, b[0:w], ACT.Copy))
                    n += 1
            for tb in range(3):
                w = META if tb == 2 else P
                dst = ke_meta if tb == 2 else ke_tok[:, tb]
                take(n, lambda b: nc.scalar.activation(dst, b[0:w], ACT.Copy))
                n += 1
            act.wait_ge(sc_zero, 1)
            for tb in range(2):
                n = steps["sc"] + tb
                act.wait_ge(step_done, n + 1)
                b = step_bank(n).rearrange("p (j n) -> p j n", j=GLA_H)
                nc.scalar.activation(sc[0:CHUNK, tb, :, 0:CHUNK], b[0:CHUNK, :, 0:CHUNK], ACT.Copy)
                nc.scalar.activation(sc[CHUNK:P, tb, :, CHUNK:P], b[CHUNK:P, :, CHUNK:P], ACT.Copy).then_inc(side_free[n % BANKS], 1)
            for s in range(8):
                wait_step_taken(act, steps["o"] + s)
            nc.scalar.activation(o_sq[:], oT[:], ACT.Square).then_inc(squares, 1)
            wait_step_taken(act, steps["on"])
            norm_root(steps["on"] + 1, o_rs[:])
            act.wait_ge(gate_g, 3)
            nc.scalar.activation(xa[:, 0:8, 0, 0:SEQ], oT[:], ACT.Copy).then_inc(xa_hi, 8)
            for j in range(8):
                take(steps["pool"] + j, lambda b: nc.scalar.activation(pool_u[:, j], b[:, 0:SEQ], ACT.Copy, scale=vec[:, V_PS + j:V_PS + j + 1]))
            for j in range(4, 8):
                wait_step_taken(act, steps["pool"] + j)
            nc.scalar.activation(xa[:, 8:16, 0, 0:SEQ], pool_u[:], ACT.Copy).then_inc(xa_hi, 8)

            run(ph["out"], 8, nothing)
            norm_squares("n2", SEQ, X0)
            norm_root(steps["n2"], rstd[:, 0:SEQ])
            norm_cut("n2", SEQ, 0, SQ)

            with act.Fori(0, UP_GROUPS) as g:
                with act.Fori(0, 4) as i:
                    def ev_up(ts, td, t):
                        complete()
                        e = g * 16 + i * 4
                        free(nc.scalar.activation(rt[:, t % 2], tile_ps(ts, SEQ), ACT.Relu), ts)
                        act.wait_ge(u_ready, e + (UR["mlp"] + t + 1))
                        nc.scalar.activation(xb[:, bass.ds(i * 4 + t, 1), 0, :], ut[:, t % 2:t % 2 + 1, :], ACT.Copy).then_inc(xb_hi, 1)
                    body(ph["mlp"].b0, g * 32 + i * 4, ph["mlp"].t0, g * 8 + i, ev_up)
                with act.Fori(0, 4) as i:
                    body(ph["mlp"].b0 + 16, g * 32 + i * 4, ph["mlp"].t0 + 16, g * 8 + i, nothing)
            norm_squares("nf", SEQ, X0)
            norm_root(steps["nf"], rstd[:, 0:SEQ])
            norm_cut("nf", SEQ, X0, h)

            f = ph["dsa"]

            def ev_first(ts, td, t):
                dst = ckv[:, t] if t < 2 else ki[:, t - 2]
                complete()
                free(nc.scalar.activation(dst, tile_ps(ts, SEQ), ACT.Copy), ts)
            body(f.b0, 0, f.t0, 0, ev_first)
            for k, buf in ((1, qi), (3, qd)):
                with act.Fori(0, 2) as i:
                    ev = copy_loop(buf)
                    body(f.b0 + 4 * k, i * 4, f.t0 + 4 * k, i, lambda ts, td, t: ev(ts, td, t, i))
            nc.scalar.activation(csq[:], ckv[:], ACT.Square).then_inc(squares, 1)
            norm_root(steps["ckv"], rstd[:, 0:SEQ])
            act.wait_ge(gate_g, 4)
            nc.scalar.activation(csq[IDX_D:P, 1], kdup[IDX_D:P], ACT.Square).then_inc(squares, 1)
            norm_root(steps["kvar"], rstd[IDX_D:P, 0:SEQ])
            take(steps["ckvT"], lambda b: nc.scalar.activation(ckv_tok[:].rearrange("p a b -> p (a b)"), b, ACT.Copy))
            for j in range(IDX_H):
                n = steps["idx"] + j
                act.wait_ge(step_done, n + 1)
                if j >= 2:
                    act.wait_ge(idx_acc, j - 1)
                nc.scalar.activation(sb_r[:, j % 2], step_bank(n), ACT.Relu).then_inc(side_free[n % BANKS], 1)

            def exps(k, src, signal=None):
                act.wait_ge(smax, k + 1)
                s = sb_s[:, k % 2].rearrange("p (b n) -> p b n", b=2)
                for tb in range(2):
                    ins = nc.scalar.activation(s[:, tb], src[:, tb], ACT.Exp, bias=small[:, 2 + tb:3 + tb], scale=INV_SQRT_DH,
                                               accum_out=small[:, 4 + tb:5 + tb])
                ins.then_inc(sexp if signal is None else signal, 1)

            def both(v):
                return v.rearrange("p (b n) -> p b n", b=2)

            for it in range(H_DSA):
                n, k = steps["dsa"] + 5 * it, HEADS["dsa"] + it
                take(n, lambda b: nc.scalar.activation(ql[:, it % 2], b, ACT.Copy))
                exps(k, both(sb_s[:, k % 2]))
                take(n + 2, lambda b: nc.scalar.activation(sb_pt[:, k % 2], b, ACT.Copy))
                take(n + 3, lambda b: nc.scalar.activation(ol[:, it % 2], b, ACT.Copy))
                take(n + 4, lambda b: nc.scalar.activation(qd[:, it], b[:, 0:SEQ], ACT.Copy))

            f = ph["moba"]
            for k, buf in ((0, qm), (1, km), (2, vmo)):
                with act.Fori(0, 2) as i:
                    ev = copy_loop(buf)
                    body(f.b0 + 8 * k, i * 4, f.t0 + 8 * k, i, lambda ts, td, t: ev(ts, td, t, i))
            n = steps["vmoT"]
            for tb in range(2):
                for jh in range(2):
                    take(n, lambda b: nc.scalar.activation(vmo_tok[:, tb, 512 * jh:512 * jh + 512], b, ACT.Copy))
                    n += 1

            def attend(name, heads, q):
                for j in range(heads):
                    n, k = steps[name] + 3 * j, HEADS[name] + j
                    if name == "mem":
                        exps(k, both(step_bank(n)), side_free[n % BANKS])
                    else:
                        exps(k, both(sb_s[:, k % 2]))
                    take(n + 1, lambda b: nc.scalar.activation(sb_pt[:, k % 2], b, ACT.Copy))
                    take(n + 2, lambda b: nc.scalar.activation(q[:, j], b[:, 0:SEQ], ACT.Copy))

            attend("moba", H_MOBA, qm)

            f = ph["gate"]
            for k in range(2):
                with act.Fori(0, 4) as i:
                    def ev_gate(ts, td, t):
                        complete()
                        ins = nc.scalar.activation(gates[:, bass.ds(i * 4 + t, 1), k, :], tile_ps(ts, SEQ).unsqueeze(1), ACT.Sigmoid,
                                                   bias=vec[:, bass.ds(i * 4 + (V_BG + 16 * k + t), 1)])
                        free(ins, ts)
                    body(f.b0 + 16 * k, i * 4, f.t0 + 16 * k, i, ev_gate)
            for j in range(2):
                src = qd if j == 0 else qm
                for s in range(4, 8):
                    if j == 0:
                        wait_step_taken(act, steps["dsa"] + 5 * s + 4)
                    else:
                        wait_step_taken(act, steps["moba"] + 3 * s + 2)
                act.wait_ge(piece_done, 2 * ph["o"].b0)
                nc.scalar.activation(xa[:, 8 * j:8 * j + 8, 0, 0:SEQ], src[:], ACT.Copy).then_inc(xa_hi, 8)

            def copy_merged(e, slot, i, t):
                act.wait_ge(u_ready, e + (UR["o"] + t + 1))
                nc.scalar.activation(xb[:, bass.ds(i * 4 + t, 1), 0, :], ut[:, slot:slot + 1, :], ACT.Copy).then_inc(xb_hi, 1)

            with act.Fori(0, 4) as i:
                for q in range(2):
                    for k in range(4):
                        cut(2 * (ph["o"].b0 + 2 * q) + k + AHEAD, i * 8)
                        if k >= 2:
                            t = 2 * q + k - 2
                            copy_merged(i * 4, t % 2, i, t)
            run(ph["out2"], 8, nothing)
            norm_squares("ln0", SEQ, X0)
            norm_root(steps["ln0"] + 1, rstd[:, 0:SEQ])
            norm_cut("ln0", SEQ, X0, h)
            f = ph["qm"]
            def ev_qx(ts, td, t):
                complete()
                free(nc.scalar.activation(qx[:, t], tile_ps(ts, SEQ), ACT.Copy), ts)
            body(f.b0, 0, f.t0, 0, ev_qx)
            attend("mem", H_MEM, qx)
            for s in range(H_MEM):
                wait_step_taken(act, steps["mem"] + 3 * s + 2)
            nc.scalar.activation(xa[:, 0:4, 0, 0:SEQ], qx[:], ACT.Copy).then_inc(xa_hi, 4)
            for p in range(8):
                cut(2 * ph["om"].b0 + p + AHEAD, 0)
            norm_squares("ln1", SEQ, X0)
            norm_root(steps["ln1"] + 1, rstd[:, 0:SEQ])
            norm_cut("ln1", SEQ, X0, h)

            def ffn_group(g, last):
                with act.Fori(0, 11) as i:
                    def ev(ts, td, t):
                        complete()
                        if t % 2 == 0:
                            nc.scalar.activation(rt[:, (t // 2) % 2], tile_ps(ts, SEQ), ACT.Sigmoid).then_inc(act_half, 1)
                        else:
                            e = g * FF_CH + i * 2
                            wait_tile_taken(act, ts, td)
                            nc.scalar.activation(xb[:, bass.ds(i * 2 + t // 2, 1), 0, :], ut[:, t // 2:t // 2 + 1, :], ACT.Copy).then_inc(xb_hi, 1)
                    body(ph["ffn"].b0, g * 68 + i * 4, ph["ffn"].t0, g * 15 + i, ev)
                b1, t1 = ph["ffn"].b0 + 44, ph["ffn"].t0 + 44
                if not last:
                    with act.Fori(0, 2) as i:
                        body(b1, g * 68 + i * 12, t1, g * 15 + i * 2, nothing, n_pairs=4, per_pair=3)
                else:
                    body(b1, g * 68, t1, g * 15, nothing, n_pairs=4, per_pair=3)
                    END_STATIC[0] = 2 * (b1 + 12)
                    body(b1, g * 68 + 12, t1, g * 15 + 2, nothing, n_pairs=4, per_pair=3, last=True)

            for g in range(FF_GROUPS):
                ffn_group(g, g == FF_GROUPS - 1)
            norm_squares("ln2", SEQ, X0)
            norm_root(steps["ln2"] + 1, rstd[:, 0:SEQ])
            norm_cut("ln2", SEQ, X0, h)
            for tb in range(2):
                for s in range(4):
                    take(steps["fin"] + 4 * tb + s, lambda b: nc.scalar.activation(o_tok[:, tb, 512 * s:512 * s + 512], b, ACT.Copy))

        @block.vector
        def _(dve):
            chain = [0]

            def link(ins):
                chain[0] += 1
                ins.then_inc(dve_chain, 1)
                dve.wait_ge(dve_chain, chain[0])

            V = nc.vector

            def cut(ps_, pd):
                dve.wait_ge(hi_made, pd + (ps_ + 1))
                bs = ps_ // 2
                V.tensor_tensor(w_lo[:, ps_ % CUT], raw[:, bs % RAW, :, (ps_ % 2) * P:(ps_ % 2) * P + P],
                                w_hi[:, ps_ % CUT].bitcast(F32), ALU.subtract).then_inc(lo_made, 1)

            END_STATIC = [1 << 30]

            def body(b0, bd, t0, td, evac, n_pairs=2, per_pair=2, last=False):
                for q in range(n_pairs):
                    for k in range(2 * per_pair):
                        p = 2 * (b0 + per_pair * q) + k
                        if not (last and p + AHEAD >= END_STATIC[0]):
                            cut(p + AHEAD, bd * 2)
                        if k >= 2 * per_pair - 2:
                            t = 2 * q + k - (2 * per_pair - 2)
                            last_piece[:] = p, bd * 2
                            evac(t0 + t, td, t)

            last_piece = [0, 0]

            def complete():
                dve.wait_ge(piece_done, last_piece[1] + (last_piece[0] + 1))

            def free(ins, ts):
                ins.then_inc(bank_free[ts % BANKS], 1)

            def take(n, fn):
                dve.wait_ge(step_done, n + 1)
                return fn(step_bank(n)).then_inc(side_free[n % BANKS], 1)

            def nothing(ts, td, t, i=None):
                pass

            def run(phase, n_pairs, evac):
                with dve.Fori(0, n_pairs // 2) as i:
                    body(phase.b0, i * 4, phase.t0, i, lambda ts, td, t: evac(ts, td, t, i))

            for s in range(8):
                n = steps["memT"] + s
                dve.wait_ge(memhi, s + 1)
                V.tensor_tensor(xb[:, 2 * s:2 * s + 2, 1, :], step_bank(n).rearrange("p (c n) -> p c n", c=2),
                                xb[:, 2 * s:2 * s + 2, 0, :].bitcast(F32), ALU.subtract).then_inc(side_free[n % BANKS], 1)
            for p in range(AHEAD):
                cut(p, 0)

            def norm_stats(name, n, eps):
                dve.wait_ge(squares, SQS[name] + 1)
                V.tensor_reduce(acc[:, 0:n], SQ[:, :, 0:n].rearrange("p c n -> p n c"), AX.X, ALU.add).then_inc(sums, 1)

            def norm_rstd(name, step, dst, n, feats, eps):
                dve.wait_ge(step_done, step + 1)
                ins = V.tensor_scalar(dst, step_src(step, dst, n), 1.0 / feats, eps, ALU.mult, ALU.add)
                ins.then_inc(side_free[step % BANKS], 1)
                dve.wait_ge(root, MSQ[name] + 1)
                link(V.reciprocal(dst, dst))

            def step_src(step, dst, n):
                return step_bank(step)[P - dst.shape[0]:P, 0:n]

            def norm_apply(name, n, off, dst, wcol):
                k = NORMS[name]
                extra = 2 if k > 2 else 0

                def lows(q):
                    base = XA[name] + 4 * q
                    dve.wait_ge(xa_hi, base + 4)
                    src = dst[:, 4 * q:4 * q + 4, off if dst is h else 0:(off if dst is h else 0) + n]
                    V.tensor_tensor(xa[:, 4 * q:4 * q + 4, 1, 0:n], src, xa[:, 4 * q:4 * q + 4, 0, 0:n].bitcast(F32),
                                    ALU.subtract).then_inc(xa_lo, 4)

                o = off if dst is h else 0
                for q in range(4):
                    for c in range(4 * q, 4 * q + 4):
                        V.scalar_tensor_tensor(out=dst[:, c, o:o + n], in0=h[:, c, off:off + n], scalar=vec[:, wcol + c:wcol + c + 1],
                                               in1=rstd[:, 0:n], op0=ALU.mult, op1=ALU.mult).then_inc(normed, 1)
                    if q > 0 and name != "ln2":
                        lows(q - 1)
                if name != "ln2":
                    lows(3)

            norm_stats("n1", TOK, EPS)
            for q in range(4):
                body(2 * q, 0, 2 * q, 0, nothing, n_pairs=1)
            for t in range(2):
                wait_step_taken(dve, steps["vec"] + t)
            norm_rstd("n1", steps["n1"], rstd[:], TOK, D, EPS)
            norm_apply("n1", TOK, 0, SQ, V_N1)
            f = ph["glr"]
            for k in range(4):
                cut(2 * f.b0 + k + AHEAD, 0)
            run(ph["v"], 4, nothing)
            link(V.memset(reset[:], 1.0))
            link(V.memset(reset[:, :, 0:1], 0.0))
            link(V.memset(reset[:, :, X0:TOK].rearrange("p j (c n) -> p j c n", n=CHUNK)[:, :, :, 0:1], 0.0))
            dve.wait_ge(gate_z, 1)
            link(V.scalar_tensor_tensor(out=gt[:], in0=gs[:], scalar=0.0, in1=gt[:], op0=ALU.min, op1=ALU.subtract))

            def flat(off):
                return R[:, off:off + GLA_H * TOK]
            V.tensor_tensor_scan(flat(0), flat(15104), flat(1088), 0.0, ALU.mult, ALU.add).then_inc(gate_g, 1)
            dve.wait_ge(gate_g, 1)
            V.tensor_tensor(gt[:, :, 0:META], gs[:, :, META - 1:META].to_broadcast([P, GLA_H, META]), gs[:, :, 0:META], ALU.subtract)
            gx = gs[:, :, X0:TOK].rearrange("p j (c n) -> p j c n", n=CHUNK)
            V.tensor_tensor(gt[:, :, X0:TOK].rearrange("p j (c n) -> p j c n", n=CHUNK),
                            gx[:, :, :, CHUNK - 1:CHUNK].to_broadcast([P, GLA_H, NCH, CHUNK]), gx, ALU.subtract).then_inc(gate_g, 1)
            f = ph["qk"]

            def ev_q(ts, td, t):
                complete()
                ins = V.scalar_tensor_tensor(out=q_dec[:, t], in0=tile_ps(ts, TOK), scalar=GLA_DK ** -0.5, in1=e_pos[:, t],
                                             op0=ALU.mult, op1=ALU.mult)
                free(ins, ts)

            def ev_k(ts, td, t):
                complete()
                V.tensor_tensor(k_inv[:, t], tile_ps(ts, TOK), e_neg[:, t], ALU.mult)
                ins = V.tensor_tensor(k_end[:, t], tile_ps(ts, TOK), e_end[:, t], ALU.mult)
                free(ins, ts)

            dve.wait_ge(gate_e, 3)
            body(f.b0, 0, f.t0, 0, ev_q)
            body(f.b0 + 4, 0, f.t0 + 4, 0, ev_k)

            def ev_r(ts, td, t, i):
                dve.wait_ge(act_half, i * 4 + (t + 1))
                ins = V.tensor_tensor(r_silu[:, bass.ds(i * 4 + t, 1), :], tile_ps(ts, TOK)[:, X0:TOK].unsqueeze(1), rt[:, t % 2:t % 2 + 1, :], ALU.mult)
                free(ins, ts)

            run(ph["r"], 4, ev_r)
            run(ph["pu"], 4, nothing)

            for j in range(GLA_H):
                for c in range(NCH):
                    n = steps["S"] + NCH * j + c
                    if c == 0:
                        take(n, lambda b: V.tensor_copy(S[:, j, 0], b[:, 0:GLA_DV]))
                    else:
                        wait_step_taken(dve, n - 1)
                        last = X0 + c * CHUNK - 1
                        take(n, lambda b: V.scalar_tensor_tensor(out=S[:, j, c], in0=S[:, j, c - 1], scalar=e_pos[:, j, last:last + 1],
                                                                 in1=b[:, 0:GLA_DV], op0=ALU.mult, op1=ALU.add))
            for j in range(8):
                take(steps["o"] + j, lambda b: V.tensor_copy(oT[:, j], b[:, 0:SEQ]))
            dve.wait_ge(squares, SQS["on"] + 1)
            sq2 = o_sq[:].rearrange("p (j v) n -> p j v n", v=2)
            V.tensor_tensor(o_ss[:], sq2[:, :, 0], sq2[:, :, 1], ALU.add).then_inc(sums, 1)
            for s in range(2):
                n = steps["on"] + s
                dve.wait_ge(step_done, n + 1)
                ins = V.tensor_scalar(R[:, 18176 + 512 * s:18176 + 512 * s + 512], step_bank(n), 1.0 / GLA_DV, EPS, ALU.mult, ALU.add)
                ins.then_inc(side_free[n % BANKS], 1)
            for s in range(2):
                wait_step_taken(dve, steps["on"] + s)
            dve.wait_ge(root, MSQ["on"] + 1)
            link(V.reciprocal(o_rs[:], o_rs[:]))
            for j in range(8):
                ins = V.scalar_tensor_tensor(out=oT[:, j], in0=oT[:, j], scalar=vec[:, V_GLA + j % 2:V_GLA + j % 2 + 1],
                                             in1=o_rs[:, j // 2], op0=ALU.mult, op1=ALU.mult)
            link(ins)
            V.tensor_tensor(oT[:], oT[:], r_silu[:], ALU.mult).then_inc(gate_g, 1)
            dve.wait_ge(xa_hi, XA["gla"] + 8)
            V.tensor_tensor(xa[:, 0:8, 1, 0:SEQ], oT[:], xa[:, 0:8, 0, 0:SEQ].bitcast(F32), ALU.subtract).then_inc(xa_lo, 8)
            wait_tiles_taken(dve, ph["out"].t0)
            for g in range(POOL_G):
                src = pu[:, 2 * g:2 * g + 2]
                lo, bufs = 0, [win_a, win_b]
                for l in range(g + 1):
                    sh = 1 << l
                    dst = bufs[l % 2]
                    link(V.tensor_tensor(dst[:, :, lo + sh:TOK], src[:, :, lo + sh:TOK], src[:, :, lo:TOK - sh], ALU.add))
                    src, lo = dst, lo + sh
                link(V.scalar_tensor_tensor(out=pool_y[:, 2 * g:2 * g + 2], in0=src[:, :, X0:TOK], scalar=1.0 / (2 << g),
                                            in1=pu[:, 2 * g:2 * g + 2, X0:TOK], op0=ALU.mult, op1=ALU.subtract))
            V.memset(small[:, 8:9], 0.0).then_inc(pool_ready, 1)
            dve.wait_ge(xa_hi, XA["pool"] + 8)
            V.tensor_tensor(xa[:, 8:16, 1, 0:SEQ], pool_u[:], xa[:, 8:16, 0, 0:SEQ].bitcast(F32), ALU.subtract).then_inc(xa_lo, 8)

            def ev_add(scale=None):
                def ev(ts, td, t, i):
                    complete()
                    hc = h[:, bass.ds(i * 4 + t, 1), X0:TOK]
                    b = tile_ps(ts, SEQ).unsqueeze(1)
                    if scale is None:
                        ins = V.tensor_tensor(hc, b, hc, ALU.add)
                    else:
                        ins = V.scalar_tensor_tensor(out=hc, in0=hc, scalar=scale, in1=b, op0=ALU.mult, op1=ALU.add)
                    free(ins, ts)
                return ev

            run(ph["out"], 8, ev_add())
            norm_stats("n2", SEQ, EPS)
            norm_rstd("n2", steps["n2"], rstd[:, 0:SEQ], SEQ, D, EPS)
            norm_apply("n2", SEQ, X0, SQ, V_N2)

            with dve.Fori(0, UP_GROUPS) as g:
                with dve.Fori(0, 4) as i:
                    def ev_up(ts, td, t):
                        e = g * 16 + i * 4
                        wait_tile_taken(dve, ts, td)
                        V.tensor_tensor(ut[:, t % 2], rt[:, t % 2], rt[:, t % 2], ALU.mult).then_inc(u_ready, 1)
                        dve.wait_ge(xb_hi, e + (XB["mlp"] + t + 1))
                        c = bass.ds(i * 4 + t, 1)
                        V.tensor_tensor(xb[:, c, 1, :], ut[:, t % 2:t % 2 + 1, :], xb[:, c, 0, :].bitcast(F32), ALU.subtract).then_inc(xb_lo, 1)
                    body(ph["mlp"].b0, g * 32 + i * 4, ph["mlp"].t0, g * 8 + i, ev_up)
                with dve.Fori(0, 4) as i:
                    add = ev_add()
                    body(ph["mlp"].b0 + 16, g * 32 + i * 4, ph["mlp"].t0 + 16, g * 8 + i, lambda ts, td, t: add(ts, td, t, i))
            norm_stats("nf", SEQ, EPS)
            norm_rstd("nf", steps["nf"], rstd[:, 0:SEQ], SEQ, D, EPS)
            norm_apply("nf", SEQ, X0, h, V_FIN)

            run(ph["dsa"], 10, nothing)
            dve.wait_ge(squares, SQS["ckv"] + 1)
            V.tensor_tensor(csq[:, 0], csq[:, 0], csq[:, 1], ALU.add).then_inc(sums, 1)
            norm_rstd("ckv", steps["ckv"], rstd[:, 0:SEQ], SEQ, 256, LN_EPS)
            for c in range(2):
                V.scalar_tensor_tensor(out=ckv[:, c], in0=ckv[:, c], scalar=vec[:, V_KVN + c:V_KVN + c + 1], in1=rstd[:, 0:SEQ],
                                       op0=ALU.mult, op1=ALU.mult).then_inc(normed, 1)
            up = slice(IDX_D, P)
            V.memset(small[:, 8:9], 0.0).then_inc(sums, 1)
            take(steps["kmean"], lambda b: V.tensor_scalar(mean[up, 0:SEQ], b[up, 0:SEQ], 1.0 / IDX_D, None, ALU.mult))
            wait_step_taken(dve, steps["kmean"])
            V.tensor_tensor(kdup[up], ki[up, 0], mean[up, 0:SEQ], ALU.subtract).then_inc(gate_g, 1)
            dve.wait_ge(squares, SQS["kvar"] + 1)
            V.memset(small[:, 8:9], 0.0).then_inc(sums, 1)
            norm_rstd("kvar", steps["kvar"], rstd[up, 0:SEQ], SEQ, IDX_D, LN_EPS)
            link(V.scalar_tensor_tensor(out=kdup[up], in0=kdup[up], scalar=vec[up, V_IG:V_IG + 1], in1=rstd[up, 0:SEQ],
                                        op0=ALU.mult, op1=ALU.mult))
            V.tensor_scalar(kdup[up], kdup[up], vec[up, V_IB:V_IB + 1], None, ALU.add).then_inc(kdup_ready, 1)
            take(steps["wT"], lambda b: V.tensor_scalar(w_tok[:].rearrange("p a b -> p (a b)"), b[:, 0:2 * IDX_H],
                                                        IDX_D ** -0.5 * IDX_H ** -0.5, None, ALU.mult))
            wait_step_taken(dve, steps["wT"])
            for j in range(IDX_H):
                wait_step_taken(dve, steps["idx"] + j)
                r = sb_r[:, j % 2].rearrange("p (b n) -> p b n", b=2)
                if j > 0:
                    dve.wait_ge(idx_acc, j)
                for tb in range(2):
                    wcol = w_tok[:, tb, j:j + 1]
                    if j == 0:
                        ins = V.tensor_scalar(score[:, tb], r[:, tb], wcol, None, ALU.mult)
                    else:
                        ins = V.scalar_tensor_tensor(out=score[:, tb], in0=r[:, tb], scalar=wcol, in1=score[:, tb], op0=ALU.mult, op1=ALU.add)
                ins.then_inc(idx_acc, 1)
            dve.wait_ge(idx_acc, IDX_H)
            V.memset(small[:, 8:9], 0.0).then_inc(score_ready, 1)
            dve.wait_ge(score_cut, 1)
            for rnd in range(TOPK // 8):
                for tb in range(2):
                    ins = V.max(out=top8[:, tb], in_=score[:, tb])
                link(ins)
                for tb in range(2):
                    ins = V.match_replace(out=score[:, tb], in_to_replace=top8[:, tb], in_values=score[:, tb], imm_value=TAKEN)
                link(ins)
            V.tensor_scalar(mbias[:], score[:], TAKEN, NEG, ALU.not_equal, ALU.mult).then_inc(sel_ready, 1)
            dve.wait_ge(sel_cut, 1)
            dve.wait_ge(dist_ready, 1)

            def both(v):
                return v.rearrange("p (b n) -> p b n", b=2)

            def softmax(n, k, bias, slope):
                s = both(sb_s[:, k % 2])
                if bias is not None:
                    if slope is None:
                        take(n, lambda b: V.tensor_tensor(sb_s[:, k % 2], b, bias, ALU.add))
                    else:
                        take(n, lambda b: V.scalar_tensor_tensor(out=s, in0=bias, scalar=slope, in1=both(b), op0=ALU.mult, op1=ALU.add))
                    wait_step_taken(dve, n)
                    src = s
                else:
                    dve.wait_ge(step_done, n + 1)
                    src = both(step_bank(n))
                link(V.tensor_reduce(small[:, 0:2], src, AX.X, ALU.max, negate=True))
                V.tensor_scalar(small[:, 2:4], small[:, 0:2], INV_SQRT_DH, None, ALU.mult).then_inc(smax, 1)
                if bias is None:
                    wait_step_taken(dve, n)
                else:
                    dve.wait_ge(sexp, k + 1)
                link(V.reciprocal(small[:, 6:8], small[:, 4:6]))
                for tb in range(2):
                    ins = V.tensor_scalar(s[:, tb], s[:, tb], small[:, 6 + tb:7 + tb], None, ALU.mult)
                ins.then_inc(pnorm, 1)

            for it in range(H_DSA):
                link(V.scalar_tensor_tensor(out=hb[:, it % 2], in0=dist[:].rearrange("p a b -> p (a b)"), scalar=ALIBI[it] / INV_SQRT_DH,
                                            in1=mbias[:].rearrange("p a b -> p (a b)"), op0=ALU.mult, op1=ALU.add))
                softmax(steps["dsa"] + 5 * it + 1, HEADS["dsa"] + it, hb[:, it % 2], None)

            run(ph["moba"], 12, nothing)
            for j in range(H_MOBA):
                softmax(steps["moba"] + 3 * j, HEADS["moba"] + j, distc[:], ALIBI[j] / INV_SQRT_DH)
            run(ph["gate"], 16, nothing)
            for j in range(2):
                src = qd if j == 0 else qm
                base = XA["oa"] + 8 * j
                dve.wait_ge(xa_hi, base + 8)
                V.tensor_tensor(xa[:, 8 * j:8 * j + 8, 1, 0:SEQ], src[:], xa[:, 8 * j:8 * j + 8, 0, 0:SEQ].bitcast(F32),
                                ALU.subtract).then_inc(xa_lo, 8)

            t0 = ph["o"].t0
            with dve.Fori(0, 4) as i:
                for q in range(2):
                    for k in range(4):
                        cut(2 * (ph["o"].b0 + 2 * q) + k + AHEAD, i * 8)
                        if k >= 2:
                            t = 2 * q + k - 2
                            ta, tb_ = t0 + 4 * q + k - 2, t0 + 4 * q + k
                            c = bass.ds(i * 4 + t, 1)
                            last_piece[:] = 2 * (ph["o"].b0 + 2 * q) + k, i * 8
                            complete()
                            m = m2[:, 0:1, :]
                            ins = V.tensor_tensor(m, tile_ps(ta, SEQ).unsqueeze(1), gates[:, c, 0, :], ALU.mult)
                            free(ins, ta)
                            ins = V.tensor_tensor(m2[:, 1:2, :], tile_ps(tb_, SEQ).unsqueeze(1), gates[:, c, 1, :], ALU.mult)
                            free(ins, tb_)
                            wait_tile_taken(dve, ta, i * 2)
                            wait_tile_taken(dve, tb_, i * 2)
                            V.tensor_tensor(ut[:, t % 2:t % 2 + 1, :], m, m2[:, 1:2, :], ALU.add).then_inc(u_ready, 1)
                            dve.wait_ge(xb_hi, i * 4 + (XB["o"] + t + 1))
                            V.tensor_tensor(xb[:, c, 1, :], ut[:, t % 2:t % 2 + 1, :], xb[:, c, 0, :].bitcast(F32), ALU.subtract).then_inc(xb_lo, 1)

            def layer_norm(name, res):
                l = LNS[name]
                wait_tiles_taken(dve, res)
                V.tensor_reduce(acc[:, 0:SEQ], h[:, :, X0:TOK].rearrange("p c n -> p n c"), AX.X, ALU.add).then_inc(sums, 1)
                st = steps[name]
                take(st, lambda b: V.tensor_scalar(mean[:, 0:SEQ], b[:, 0:SEQ], 1.0 / D, None, ALU.mult))
                wait_step_taken(dve, st)
                for q in range(4):
                    ins = V.tensor_tensor(h[:, 4 * q:4 * q + 4, X0:TOK], h[:, 4 * q:4 * q + 4, X0:TOK],
                                          mean[:, 0:SEQ].unsqueeze(1).to_broadcast([P, 4, SEQ]), ALU.subtract)
                ins.then_inc(centered, 1)
                norm_stats(name, SEQ, LN_EPS)
                norm_rstd(name, st + 1, rstd[:, 0:SEQ], SEQ, D, LN_EPS)
                norm_apply(name, SEQ, X0, h, V_LG + 16 * l)

            run(ph["out2"], 8, ev_add(ALPHA))
            layer_norm("ln0", ph["qm"].t0)
            body(ph["qm"].b0, 0, ph["qm"].t0, 0, nothing)
            for j in range(H_MEM):
                softmax(steps["mem"] + 3 * j, HEADS["mem"] + j, None, None)
            dve.wait_ge(xa_hi, XA["om"] + 4)
            V.tensor_tensor(xa[:, 0:4, 1, 0:SEQ], qx[:], xa[:, 0:4, 0, 0:SEQ].bitcast(F32), ALU.subtract).then_inc(xa_lo, 4)
            for b in range(4):
                for half in range(2):
                    cut(2 * (ph["om"].b0 + b) + half + AHEAD, 0)
                    for q in range(2):
                        t = 4 * b + 2 * half + q
                        ts = ph["om"].t0 + t
                        last_piece[:] = 2 * (ph["om"].b0 + b) + half, 0
                        complete()
                        hc = h[:, 4 * b + 2 * q + half, X0:TOK]
                        ins = V.scalar_tensor_tensor(out=hc, in0=hc, scalar=ALPHA, in1=tile_ps(ts, SEQ), op0=ALU.mult, op1=ALU.add)
                        free(ins, ts)
            layer_norm("ln1", ph["ffn"].t0)

            def ffn_group(g, last):
                with dve.Fori(0, 11) as i:
                    def ev(ts, td, t):
                        if t % 2 == 0:
                            return
                        j = t // 2
                        e = g * FF_CH + i * 2
                        dve.wait_ge(act_half, e + (8 + j + 1))
                        ins = V.tensor_tensor(rt[:, j], tile_ps(ts - 1, SEQ), rt[:, j], ALU.mult)
                        free(ins, ts - 1)
                        complete()
                        wait_tile_taken(dve, ts - 1, td)
                        ins = V.tensor_tensor(ut[:, j], tile_ps(ts, SEQ), rt[:, j], ALU.mult)
                        free(ins, ts)
                        dve.wait_ge(xb_hi, e + (XB["ffn"] + j + 1))
                        c = bass.ds(i * 2 + j, 1)
                        V.tensor_tensor(xb[:, c, 1, :], ut[:, j:j + 1, :], xb[:, c, 0, :].bitcast(F32), ALU.subtract).then_inc(xb_lo, 1)
                    body(ph["ffn"].b0, g * 68 + i * 4, ph["ffn"].t0, g * 15 + i, ev)
                b1, t1 = ph["ffn"].b0 + 44, ph["ffn"].t0 + 44

                def add(ts, td, t, i):
                    complete()
                    hc = h[:, bass.ds(i * 8 + t, 1), X0:TOK]
                    b = tile_ps(ts, SEQ).unsqueeze(1)
                    if g > 0:
                        ins = V.tensor_tensor(hc, b, hc, ALU.add)
                    else:
                        ins = V.scalar_tensor_tensor(out=hc, in0=hc, scalar=ALPHA, in1=b, op0=ALU.mult, op1=ALU.add)
                    free(ins, ts)
                if not last:
                    with dve.Fori(0, 2) as i:
                        body(b1, g * 68 + i * 12, t1, g * 15 + i * 2, lambda ts, td, t: add(ts, td, t, i), n_pairs=4, per_pair=3)
                else:
                    body(b1, g * 68, t1, g * 15, lambda ts, td, t: add(ts, td, t, 0), n_pairs=4, per_pair=3)
                    END_STATIC[0] = 2 * (b1 + 12)
                    body(b1, g * 68 + 12, t1, g * 15 + 2, lambda ts, td, t: add(ts, td, t, 1), n_pairs=4, per_pair=3, last=True)

            for g in range(FF_GROUPS):
                ffn_group(g, g == FF_GROUPS - 1)
            layer_norm("ln2", ph["end"].t0)


INPUTS = ["x", "meta_tokens", "norm1_w", "w_in", "gate_w2", "gate_b", "gla_norm_w", "pool_w", "pool_scale", "w_out",
          "norm2_w", "mlp_w1", "mlp_w2", "final_norm_w", "mem_2", "w_in_2", "b_gate_2", "kv_norm_g_2", "idx_k_norm_g_2",
          "idx_k_norm_b_2", "w_uk_2", "w_uv_2", "w_o_dsa_2", "w_o_moba_2", "w_out_2", "w_q_mem_2", "w_kv_mem_2",
          "w_o_mem_2", "w_ffn_in_2", "w_ffn_out_2", "ln_g_2", "ln_b_2"]


def kernel(**inputs):
    import numpy as _np
    import concourse.bacc as _bacc
    from concourse import mybir as _mybir
    from concourse.bass_utils import run_bass_kernel_spmd as _run

    nc = _bacc.Bacc("TRN2", target_bir_lowering=False, num_devices=1, dynamic_dma_scratch_size=8192)
    arrays, args = {}, {}
    for name in INPUTS:
        a = _np.ascontiguousarray(inputs[name])
        arrays[f"in_{name}"] = a
        args[name] = nc.dram_tensor(f"in_{name}", a.shape, _mybir.dt.from_np(a.dtype), kind="ExternalInput").ap()
    o = nc.dram_tensor("out_0", (1, SEQ, D), F32, kind="ExternalOutput").ap()
    program(nc, args, o)
    r = _run(nc, [arrays], core_ids=[0])
    return r.results[0]["out_0"]
```

```python
from contextlib import ExitStack

import concourse.bass as bass
from concourse import mybir

F32 = mybir.dt.float32
F32R = mybir.dt.float32r
ACT = mybir.ActivationFunctionType
ALU = mybir.AluOpType
AX = mybir.AxisListType

P = 128
D = 2048
DC = D // P
SEQ = 256
META = 16
TOK = META + SEQ
X0 = META
GLA_H, GLA_DK, GLA_DV = 4, 128, 256
GLA_KW, GLA_W = GLA_H * GLA_DK, GLA_H * GLA_DV
CHUNK = 64
NCH = SEQ // CHUNK
GATE_RANK = 16
POOL_G, POOL_GC = 4, 256
D_FF = 8192
D_FF2 = 5632
H_DSA = 8
H_MOBA = 8
H_MEM = 4
IDX_H, IDX_D = 16, 64
TOPK = min(256, SEQ // 4)
EPS = 1e-6
LN_EPS = 1e-5
ALPHA = 2.0 ** 0.25
INV_SQRT_DH = 128 ** -0.5
NEG = -1e30
LOW = -1e38
TAKEN = -3e38

RAW = 4
CUT = 4
AHEAD = 3
BANKS = 4

C_Q, C_K, C_V, C_R, C_GLR = 0, GLA_KW, 2 * GLA_KW, 2 * GLA_KW + GLA_W, 2 * GLA_KW + 2 * GLA_W
C_PU = C_GLR + GATE_RANK
B_QD, B_CKV, B_QI, B_KI = 0, 1024, 1280, 2304
B_WI = B_KI + IDX_D
B_MOBA = B_WI + IDX_H
B_GATE = B_MOBA + 3 * 1024

V_N1, V_N2, V_FIN, V_GB, V_GLA, V_PS, V_KVN, V_BG = 0, 16, 32, 48, 52, 54, 62, 64
V_LG, V_LB, V_IG, V_IB = 96, 144, 192, 193

UP_GROUPS = 4
FF_GROUPS = 2
FF_CH = D_FF2 // P // FF_GROUPS

ALIBI = [2.0 ** (-8.0 * (i + 1) / H_MOBA) for i in range(H_MOBA)]


class Phase:

    def __init__(self, blocks, tiles):
        self.b0, self.t0 = Phase.b, Phase.t
        Phase.b += blocks
        Phase.t += tiles


MEM_ORDER = [("mem_" + w[0], int(w[1])) for w in "s0 s1 t0 s2 t1 o0 s3 t2 o1 t3 o2 o3".split()]


def plan():
    Phase.b = Phase.t = 0
    ph = {}
    for name, blocks, tiles in (
        ("kv", 8, 8), ("glr", 2, 1), ("v", 8, 8), ("qk", 8, 8), ("pu", 8, 8), ("r", 8, 8),
        ("out", 16, 16), ("mlp", UP_GROUPS * 32, UP_GROUPS * 32),
        ("dsa", 20, 20), ("moba", 24, 24), ("gate", 32, 32), ("o", 16, 32), ("out2", 16, 16),
        ("qm", 4, 4), ("om", 4, 16), ("ffn", FF_GROUPS * (44 + 24), FF_GROUPS * (44 + 16)),
    ):
        ph[name] = Phase(blocks, tiles)
    ph["end"] = Phase(0, 0)
    order = [(name, i) for name, count in (
        ("memT", 8), ("vec", 2), ("xT", 16), ("n1", 1), ("vmT", 2), ("gate", GLA_H), ("vT", 6), ("keT", 3), ("sc", 2),
    ) for i in range(count)]
    for j in range(GLA_H + 2):
        order += [("S", NCH * j + c) for c in range(NCH) if j < GLA_H]
        order += [("o", 2 * (j - 2) + v) for v in range(2) if j >= 2]
    order += [(name, i) for name, count in (
        ("on", 2), ("pool", 8), ("n2", 1), ("nf", 1), ("ckv", 1), ("wT", 1), ("kmean", 1), ("kvar", 1), ("ckvT", 1), ("idx", IDX_H),
    ) for i in range(count)]
    for beat in range(H_DSA + 2):
        order += dsa_beat(beat, 0) + dsa_beat(beat, 2)
    order += [("vmoT", i) for i in range(4)]
    for beat in range(H_MOBA + 1):
        order += head_beat("moba", H_MOBA, beat, 0) + head_beat("moba", H_MOBA, beat, 2)
    order += [("ln0", 0), ("ln0", 1)]
    order += MEM_ORDER
    order += [(name, i) for name, count in (("ln1", 2), ("ln2", 2), ("fin", 8)) for i in range(count)]
    return ph, {key: n for n, key in enumerate(order)}


def om_chunk(t):
    return 4 * (t // 4) + 2 * (t % 2) + (t // 2) % 2


def dsa_beat(beat, slot):
    if slot == 0:
        at = [("dsa_q", beat), ("dsa_l", beat - 2)]
    else:
        at = [("dsa_s", beat), ("dsa_t", beat - 1), ("dsa_o", beat - 2)]
    return [(name, j) for name, j in at if 0 <= j < H_DSA]


def head_beat(kind, heads, beat, slot):
    at = [(kind + "_s", beat), (kind + "_t", beat - 1)] if slot == 0 else [(kind + "_o", beat - 1)]
    return [(name, j) for name, j in at if 0 <= j < heads]


def program(nc, A, out):
    ph, steps = plan()
    with ExitStack() as ctx:
        def sb(name, shape, dt=F32):
            return ctx.enter_context(nc.sbuf_tensor(name, shape, dt))

        def sem(name):
            return ctx.enter_context(nc.semaphore(name))

        raw = sb("raw", [P, RAW, 8, 256])
        w_hi = sb("w_hi", [P, CUT, 8, P], F32R)
        w_lo = sb("w_lo", [P, CUT, 8, P], F32R)
        xa = sb("xa", [P, DC, 2, TOK], F32R)
        h = sb("h", [P, DC, TOK])
        k_mem = sb("k_mem", [P, H_MEM, SEQ])
        v_mem = sb("v_mem", [P, 2, H_MEM * P])
        ident = sb("ident", [P, P])
        ones = sb("ones", [P, P])
        vec = sb("vec", [P, 194])
        ut = sb("ut", [P, 2, SEQ])
        rt = sb("rt", [P, 2, SEQ])
        stat = sb("stat", [P, 2, TOK])
        acc, mean = stat[:, 0], stat[:, 1]
        shift = sb("shift", [P, SEQ])
        rstd = sb("rstd", [P, TOK])
        rows = sb("rows", [P, 2, P])
        small = sb("small", [P, 32])
        top8 = sb("top8", [P, 2, 8])
        guard = nc.sbuf_tensor("xb", [P, FF_CH, 2, SEQ], F32R)
        xb = guard.__enter__()
        guard.__exit__(None, None, None)
        R = sb("region", [P, 20736])

        def reg(off, *shape, parts=P):
            size = 1
            for s in shape:
                size *= s
            v = R[0:parts, off:off + size]
            if len(shape) == 2:
                v = v.rearrange("p (a b) -> p a b", a=shape[0])
            if len(shape) == 3:
                v = v.rearrange("p (a b c) -> p a b c", a=shape[0], b=shape[1])
            return v

        ps = ctx.enter_context(nc.psum_tensor("ps", [P, 8, 512], F32))

        SQ = reg(8192, DC, TOK)
        meta_tok = reg(8192, D, parts=META)
        mem_tok = reg(12544, 2, D)
        x_tok = reg(16640, 2, D)
        vmT = reg(16640, H_MEM, SEQ)
        gs, gt = reg(0, GLA_H, TOK), reg(1088, GLA_H, TOK)
        e_pos, e_neg, e_end = reg(2176, GLA_H, TOK), reg(3264, GLA_H, TOK), reg(4352, GLA_H, TOK)
        q_dec, k_inv, k_end = reg(5440, GLA_H, TOK), reg(6528, GLA_H, TOK), reg(7616, GLA_H, TOK)
        vT = reg(8704, 8, TOK)
        r_silu = reg(10880, 8, SEQ)
        pu = reg(12928, 8, TOK)
        S = reg(15104, GLA_H, NCH, GLA_DV)
        reset = reg(15104, GLA_H, TOK)
        v_meta = reg(19200, 1024, parts=META)
        ke_meta = rt[0:META].rearrange("p a b -> p (a b)")
        glr = mean[0:GATE_RANK]
        gw2 = ut[0:GATE_RANK].rearrange("p a b -> p (a b)")
        v_tok = reg(0, 2, 1024)
        ke_tok = reg(3264, 2, 512)
        sc = reg(4352, 2, GLA_H, P)
        oT = reg(8704, 8, SEQ)
        o_sq = reg(15104, 8, SEQ)
        o_ss = reg(17152, GLA_H, SEQ)
        o_rs = reg(18176, GLA_H, SEQ)
        win_a, win_b = reg(0, 2, TOK), reg(544, 2, TOK)
        pool_y = reg(2176, 8, SEQ)
        pool_u = reg(15104, 8, SEQ)
        pool_w = reg(6528, 8, 256)
        qd, ckv, ki = reg(0, 8, SEQ), reg(2048, 2, SEQ), reg(2560, 2, SEQ)
        qi = reg(3072, 8, SEQ)
        kdup = reg(5120, SEQ)
        w_tok = reg(5376, 2, IDX_H)
        score, mbias = reg(5408, 2, SEQ), reg(5920, 2, SEQ)
        ckv_tok = reg(6944, 2, SEQ)
        uk, uv = reg(7456, H_DSA, 256), reg(9504, 2 * H_DSA, P)
        ql = reg(11552, 2, 512)
        ol = reg(12576, 2, 512)
        sb_r = reg(13600, 2, 512)
        sb_s = reg(16384, 2, 512)
        sb_pt = reg(17408, 2, 512)
        dist, distc = reg(18432, 2, SEQ), reg(18944, 2, SEQ)
        csq = reg(19456, 2, SEQ)
        hb = reg(19968, 512)
        qm = reg(3072, 8, SEQ)
        h_flat = h[:].rearrange("p c n -> p (c n)")
        km = h_flat[:, 0:2048].rearrange("p (j n) -> p j n", j=8)
        vmo = h_flat[:, 2048:4096].rearrange("p (j n) -> p j n", j=8)
        vmo_tok = reg(6144, 2, 1024)
        gates = reg(8192, DC, 2, SEQ)
        m2 = reg(16384, 2, SEQ)
        qx = reg(0, H_MEM, SEQ)
        o_tok = reg(0, 2, D)

        loaded = [sem(f"loaded{i}") for i in range(RAW)]
        hi_made, lo_made = sem("hi_made"), sem("lo_made")
        piece_done = sem("piece_done")
        bank_free = [sem(f"bank_free{i}") for i in range(BANKS)]
        step_done = sem("step_done")
        side_free = [sem(f"side_free{i}") for i in range(BANKS)]
        rows_in = sem("rows_in")
        consts = sem("consts")
        mem_in = [sem(f"mem_in{s}") for s in range(4)]
        x_in, meta_in, gw_in = sem("x_in"), sem("meta_in"), sem("gw_in")
        memhi = sem("memhi")
        sums = sem("sums")
        squares = sem("squares")
        root = sem("root")
        normed = sem("normed")
        biased = sem("biased")
        xa_hi, xa_lo = sem("xa_hi"), sem("xa_lo")
        act_half, u_ready = sem("act_half"), sem("u_ready")
        xb_hi, xb_lo = sem("xb_hi"), sem("xb_lo")
        gate_z, gate_g, gate_e = sem("gate_z"), sem("gate_g"), sem("gate_e")
        sq_made = sem("sq_made")
        h_back = sem("h_back")
        shifted, delta, recentered = sem("shifted"), sem("delta"), sem("recentered")
        sq_added = sem("sq_added")
        gla_hi, gla_lo = sem("gla_hi"), sem("gla_lo")
        gate_one, gate_made = sem("gate_one"), sem("gate_made")
        kcentered = sem("kcentered")
        sc_zero, sc_masked = sem("sc_zero"), sem("sc_masked")
        pool_in, uk_in, pool_ready = sem("pool_in"), sem("uk_in"), sem("pool_ready")
        idx_acc = sem("idx_acc")
        kdup_ready, kdup_in = sem("kdup_ready"), sem("kdup_in")
        score_ready, score_cut, sel_ready, sel_cut = sem("score_ready"), sem("score_cut"), sem("sel_ready"), sem("sel_cut")
        dist_ready = sem("dist_ready")
        smax, sexp, pnorm = sem("smax"), sem("sexp"), sem("pnorm")
        out_done = sem("out_done")
        act_chain, dve_chain, pool_chain = sem("act_chain"), sem("dve_chain"), sem("pool_chain")

        block = ctx.enter_context(nc.Block())

        NORMS = {"n1": 0, "n2": 1, "nf": 2, "ln0": 3, "ln1": 4, "ln2": 5}
        LNS = {"ln0": 0, "ln1": 1, "ln2": 2}
        SUMS = {"n1": 0, "on": 1, "n2": 2, "nf": 3, "ckv": 4, "ln0": 5, "ln1": 7, "ln2": 9}
        SQS = {"n1": 0, "on": 4, "ckv": 5, "kvar": 6, "ln1": 7}
        ROOTS = {name: n for n, name in enumerate(("n1", "on", "n2", "nf", "ckv", "kvar", "ln0", "ln1", "ln2"))}
        SQN = {"n2": 0, "nf": 16, "ln0": 32, "ln2": 48}
        XA = {"n1": 0, "pool": 16, "n2": 24, "nf": 40, "oa": 56, "ln0": 72, "ln1": 88}
        XB = {"mlp": 0, "o": 64, "ffn": 80}
        UR = {"mlp": 0, "o": 64}
        HEADS = {"dsa": 0, "moba": H_DSA, "mem": H_DSA + H_MOBA}

        def step_bank(key):
            n = steps[key]
            return ps[:, BANKS + n % BANKS, :]

        def tile_ps(ts, n):
            return ps[:, ts % BANKS, 0:n]

        def wait_tile_taken(eng, ts, td=0):
            eng.wait_ge(bank_free[ts % BANKS], td + (ts // BANKS + 1))

        def wait_tiles_taken(eng, end):
            for t in range(end - BANKS, end):
                wait_tile_taken(eng, t)

        def wait_step_taken(eng, key):
            n = steps[key]
            eng.wait_ge(side_free[n % BANKS], n // BANKS + 1)

        def taken(ins, key):
            ins.then_inc(side_free[steps[key] % BANKS], 1)

        def bank_for_step(eng, key):
            n = steps[key] - BANKS
            if n >= 0:
                eng.wait_ge(side_free[n % BANKS], n // BANKS + 1)

        @block.sync
        def _(sp):
            mem_v, x_v = A["mem_2"][0].rearrange("(b p) n -> p b n", p=P), A["x"][0].rearrange("(b p) n -> p b n", p=P)
            for s in range(4):
                sp.dma_start(mem_tok[:, :, 512 * s:512 * s + 512], mem_v[:, :, 512 * s:512 * s + 512]).then_inc(mem_in[s], 16)

            def load(bs, bd, srcs):
                if not (isinstance(bd, int) and bs + bd < RAW):
                    sp.wait_ge(lo_made, bd * 2 + (2 * (bs - RAW) + 2))
                for dst, src in srcs:
                    sp.dma_start(dst, src).then_inc(loaded[bs % RAW], 32 // len(srcs))

            def halves(w):
                v = w.rearrange("(c p) n -> p c n", p=P)
                return v

            def pairs(b0, w, col, n_pairs, bd=0, halves_at=(0, 1)):
                v = halves(w)
                if n_pairs == 1:
                    for kb in range(2):
                        load(b0 + kb, bd, [(raw[:, (b0 + kb) % RAW], v[:, 8 * kb:8 * kb + 8, col:col + 256])])
                    return
                with sp.Fori(0, n_pairs // 2) as i:
                    for q in range(2):
                        for n, kb in enumerate(halves_at):
                            bs = b0 + 2 * q + n
                            load(bs, bd + i * 4, [(raw[:, bs % RAW], v[:, 8 * kb:8 * kb + 8, bass.ds(i * 512 + (col + q * 256), 256)])])

            kvv = halves(A["w_kv_mem_2"][0])
            for b in range(8):
                q, kb = b // 2, b % 2
                if b == 2:
                    sp.dma_start(x_tok, x_v).then_inc(x_in, 16)
                load(b, 0, [(raw[:, b % RAW], kvv[:, 8 * kb:8 * kb + 8, 256 * q:256 * q + 256])])
            w_in = A["w_in"][0]
            pairs(ph["glr"].b0, w_in, C_GLR, 1)
            pairs(ph["v"].b0, w_in, C_V, 4)
            pairs(ph["qk"].b0, w_in, C_Q, 4)
            pairs(ph["pu"].b0, w_in, C_PU, 4)
            pairs(ph["r"].b0, w_in, C_R, 4)
            wo = halves(A["w_out"][0])
            for q in range(8):
                for n, kb in enumerate((1, 0)):
                    b = ph["out"].b0 + 2 * q + n
                    load(b, 0, [(raw[:, b % RAW], wo[:, 8 * kb:8 * kb + 8, 256 * q:256 * q + 256])])
            w1, w2 = halves(A["mlp_w1"][0]), halves(A["mlp_w2"][0])
            with sp.Fori(0, UP_GROUPS) as g:
                with sp.Fori(0, 4) as i:
                    for q in range(2):
                        for kb in range(2):
                            bs = ph["mlp"].b0 + 2 * q + kb
                            load(bs, g * 32 + i * 4, [(raw[:, bs % RAW], w1[:, 8 * kb:8 * kb + 8, bass.ds(g * 2048 + i * 512 + q * 256, 256)])])
                with sp.Fori(0, 4) as i:
                    for q in range(2):
                        for kb in range(2):
                            bs = ph["mlp"].b0 + 16 + 2 * q + kb
                            load(bs, g * 32 + i * 4, [(raw[:, bs % RAW], w2[:, bass.ds(g * 16 + 8 * kb, 8), bass.ds(i * 512 + q * 256, 256)])])
            w_in2 = A["w_in_2"][0]
            b = ph["dsa"].b0
            pairs(b, w_in2, B_CKV, 1)
            pairs(b + 2, w_in2, B_KI - IDX_D, 1)
            pairs(b + 4, w_in2, B_QI, 4)
            pairs(b + 12, w_in2, B_QD, 4)
            pairs(ph["moba"].b0, w_in2, B_MOBA, 12)
            pairs(ph["gate"].b0, w_in2, B_GATE, 16)
            woa, wob = halves(A["w_o_dsa_2"][0]), halves(A["w_o_moba_2"][0])
            with sp.Fori(0, 4) as i:
                for q in range(2):
                    for kb, v in enumerate((woa, wob)):
                        bs = ph["o"].b0 + 2 * q + kb
                        load(bs, i * 4, [(raw[:, bs % RAW], v[:, :, bass.ds(i * 512 + q * 256, 256)])])
            pairs(ph["out2"].b0, A["w_out_2"][0], 0, 8)
            pairs(ph["qm"].b0, A["w_q_mem_2"][0], 0, 2)
            wom = halves(A["w_o_mem_2"][0])
            for b in range(4):
                bs = ph["om"].b0 + b
                load(bs, 0, [(raw[:, bs % RAW].rearrange("p a b -> p (a b)").rearrange("p (c n) -> p c n", c=4),
                              wom[:, :, 512 * b:512 * b + 512])])
            wfi, wfo = halves(A["w_ffn_in_2"][0]), halves(A["w_ffn_out_2"][0])
            with sp.Fori(0, FF_GROUPS) as g:
                with sp.Fori(0, 11) as i:
                    for q in range(2):
                        for kb in range(2):
                            bs = ph["ffn"].b0 + 2 * q + kb
                            load(bs, g * 68 + i * 4,
                                 [(raw[:, bs % RAW, :, u * P:u * P + P],
                                   wfi[:, 8 * kb:8 * kb + 8, bass.ds(g * FF_CH * P + i * 256 + (u * D_FF2 + q * P), P)])
                                  for u in range(2)])
                with sp.Fori(0, 2) as i:
                    for q in range(4):
                        for kb, (c, n) in enumerate(((0, 8), (8, 8), (16, 6))):
                            bs = ph["ffn"].b0 + 44 + 3 * q + kb
                            load(bs, g * 68 + i * 12, [(raw[:, bs % RAW, 0:n], wfo[:, bass.ds(g * FF_CH + c, n), bass.ds(i * 1024 + q * 256, 256)])])
            o_v = out[0].rearrange("(b p) n -> p b n", p=P)
            for s in range(4):
                for tb in range(2):
                    wait_step_taken(sp, ("fin", 2 * s + tb))
                sp.dma_start(o_v[:, :, 512 * s:512 * s + 512], o_tok[:, :, 512 * s:512 * s + 512]).then_inc(out_done, 16)
            sp.wait_ge(out_done, 64)

        @block.gpsimd
        def _(pool):
            chain = [0]

            def link(ins):
                chain[0] += 1
                ins.then_inc(pool_chain, 1)
                pool.wait_ge(pool_chain, chain[0])

            link(nc.gpsimd.memset(ident[:], 0.0))
            nc.gpsimd.affine_select(out=ident[:], in_=ident[:], compare_op=ALU.not_equal, fill=1.0, base=0,
                                    pattern=[[-1, P]], channel_multiplier=1).then_inc(consts, 1)
            nc.gpsimd.memset(ones[:], 1.0).then_inc(consts, 1)
            link(nc.gpsimd.memset(rows[:], 0.0))
            n_rows = 0
            for t, r0, src in (
                (0, V_N1, A["norm1_w"][0]), (0, V_N2, A["norm2_w"][0]), (0, V_FIN, A["final_norm_w"]),
                (0, V_GB, A["gate_b"][0]), (0, V_GLA, A["gla_norm_w"][0]), (0, V_PS, A["pool_scale"][0]),
                (0, V_KVN, A["kv_norm_g_2"][0]),
                (0, V_BG, A["b_gate_2"][0].rearrange("a n -> (a n)")),
                (1, V_LG - 96, A["ln_g_2"][0].rearrange("a n -> (a n)")),
                (1, V_LB - 96, A["ln_b_2"][0].rearrange("a n -> (a n)")),
            ):
                n = src.shape[0] // P
                pool.dma_start(rows[r0:r0 + n, t, :], src.rearrange("(c p) -> c p", p=P)).then_inc(rows_in, 16)
                n_rows += 1
            for r0, src in ((V_IG - 96, A["idx_k_norm_g_2"]), (V_IB - 96, A["idx_k_norm_b_2"])):
                pool.dma_start(rows[r0:r0 + 1, 1, IDX_D:2 * IDX_D], src).then_inc(rows_in, 16)
                n_rows += 1
            assert n_rows == 12
            pool.dma_start(meta_tok, A["meta_tokens"]).then_inc(meta_in, 16)
            pool.dma_start(gw2, A["gate_w2"][0]).then_inc(gw_in, 16)
            wait_step_taken(pool, ("keT", 2))
            nc.gpsimd.memset(R[:, 4352:4352 + 1024], 0.0).then_inc(sc_zero, 1)
            for tb in range(2):
                wait_step_taken(pool, ("sc", tb))
                nc.gpsimd.affine_select(out=sc[:, tb], in_=sc[:, tb], compare_op=ALU.is_ge, fill=0.0, base=0,
                                        pattern=[[0, GLA_H], [1, P]], channel_multiplier=-1).then_inc(sc_masked, 1)
            pool.dma_start(pool_w, A["pool_w"][0].rearrange("g (c p) d -> p (g c) d", p=P)).then_inc(pool_in, 16)

            pool.wait_ge(xa_lo, XA["nf"] + 16)
            for tb in range(2):
                link(nc.gpsimd.iota(dist[:, tb], pattern=[[1, SEQ]], base=-P * tb, channel_multiplier=-1,
                                    allow_small_or_imprecise_dtypes=True))
            nc.gpsimd.affine_select(out=distc[:], in_=dist[:], compare_op=ALU.is_ge, fill=-1e32, base=0,
                                    pattern=[[P, 2], [-1, SEQ]], channel_multiplier=1).then_inc(dist_ready, 1)
            pool.dma_start(uk, A["w_uk_2"][0].rearrange("h p c -> p h c")).then_inc(uk_in, 16)
            pool.dma_start(uv, A["w_uv_2"][0].rearrange("h (c p) d -> p (h c) d", p=P)).then_inc(uk_in, 16)
            pool.wait_ge(kdup_ready, 1)
            pool.dma_start(kdup[0:IDX_D], kdup[IDX_D:P]).then_inc(kdup_in, 16)
            pool.wait_ge(score_ready, 1)
            nc.gpsimd.affine_select(out=score[:], in_=score[:], compare_op=ALU.is_ge, fill=LOW, base=0,
                                    pattern=[[P, 2], [-1, SEQ]], channel_multiplier=1).then_inc(score_cut, 1)
            pool.wait_ge(sel_ready, 1)
            nc.gpsimd.affine_select(out=mbias[:], in_=mbias[:], compare_op=ALU.is_ge, fill=NEG, base=0,
                                    pattern=[[P, 2], [-1, SEQ]], channel_multiplier=1).then_inc(sel_cut, 1)

            for l in range(3):
                pool.wait_ge(delta, l + 1)
                for q in range(1, 4):
                    pool.wait_ge(recentered, 4 * l + q)
                    nc.gpsimd.tensor_tensor(h[:, 4 * q:4 * q + 4, X0:TOK], h[:, 4 * q:4 * q + 4, X0:TOK],
                                            mean[:, 0:SEQ].unsqueeze(1).to_broadcast([P, 4, SEQ]), ALU.subtract).then_inc(recentered, 1)

        @block.tensor
        def _(pe):
            side = [None]

            def slot():
                if side[0] is not None:
                    next(side[0], None)

            def finish():
                for _ in side[0]:
                    pass
                side[0] = None

            def done(ins):
                ins.then_inc(step_done, 1)

            def pair(bs, bd, ts, td, rhs, n, blocks=(range(0, 8), range(8, 16)), ready=None, alone=False):
                for bi, chunks in enumerate(blocks):
                    for half in range(1 if alone else 2):
                        p = 2 * (bs + bi) + half
                        pe.wait_ge(lo_made, bd * 2 + (p + (2 if alone else 1)))
                        if bi == 0:
                            t = ts + half
                            if not (isinstance(td, int) and t + td < BANKS):
                                pe.wait_ge(bank_free[t % BANKS], td + t // BANKS)
                        o = tile_ps(ts + half, n)
                        for ci, c in enumerate(chunks):
                            if ready is not None and half == 0:
                                ready(c)
                            hi, lo = w_hi[:, p % CUT, ci], w_lo[:, p % CUT, ci]
                            x_hi, x_lo = rhs(c)
                            first, last = bi == 0 and ci == 0, bi == len(blocks) - 1 and ci == len(chunks) - 1
                            nc.tensor.matmul(o, hi, x_hi, start=first, stop=False)
                            nc.tensor.matmul(o, hi, x_lo, start=False, stop=False)
                            ins = nc.tensor.matmul(o, lo, x_hi, start=False, stop=last)
                        ins.then_inc(piece_done, 2 if alone else 1)
                        slot()

            def from_tokens(c):
                return xa[:, c, 0, X0:TOK], xa[:, c, 1, X0:TOK]

            def from_xa(n):
                return lambda c: (xa[:, c, 0, 0:n], xa[:, c, 1, 0:n])

            def from_xb(c):
                return xb[:, c, 0, :], xb[:, c, 1, :]

            def chunk_of_xa(base):
                def ready(c):
                    if c % 4 == 0:
                        pe.wait_ge(xa_lo, base + c + 4)
                return ready

            def straight(phase, first, n_pairs, rhs, n, ready=None, blocks=(range(0, 8), range(8, 16))):
                for q in range(first, first + n_pairs):
                    pair(phase.b0 + 2 * q, 0, phase.t0 + 2 * q, 0, rhs, n, blocks=blocks, ready=ready if q == 0 else None)

            def run(phase, first, n_pairs, rhs, n, blocks=(range(0, 8), range(8, 16))):
                with pe.Fori(first // 2, (first + n_pairs) // 2) as i:
                    for q in range(2):
                        pair(phase.b0 + 2 * q, i * 4, phase.t0 + 2 * q, i, rhs, n, blocks=blocks)

            pe.wait_ge(consts, 2)

            for s in range(8):
                key = ("memT", s)
                pe.wait_ge(mem_in[s // 2], 16)
                bank_for_step(pe, key)
                b = step_bank(key)
                for c in range(2):
                    for tb in range(2):
                        ins = nc.tensor.transpose(b[:, c * 256 + tb * P:c * 256 + tb * P + P],
                                                  mem_tok[:, tb, (2 * s + c) * P:(2 * s + c + 1) * P], ident[:])
                done(ins)
            pe.wait_ge(rows_in, 12 * 16)
            for t in range(2):
                bank_for_step(pe, ("vec", t))
                done(nc.tensor.transpose(step_bank(("vec", t))[:, 0:P], rows[:, t, :], ident[:]))

            def tokens():
                pe.wait_ge(x_in, 16)
                pe.wait_ge(meta_in, 16)
                for c in range(DC):
                    key = ("xT", c)
                    bank_for_step(pe, key)
                    b = step_bank(key)
                    nc.tensor.transpose(b[:, 0:META], meta_tok[:, c * P:c * P + P], ident[0:META, 0:META])
                    for tb in range(2):
                        ins = nc.tensor.transpose(b[:, X0 + tb * P:X0 + tb * P + P], x_tok[:, tb, c * P:c * P + P], ident[:])
                    done(ins)
                    if c % 2:
                        yield

            def mem_chunk(c):
                wait_step_taken(pe, ("memT", c // 2))

            f = ph["kv"]
            straight(f, 0, 1, from_xb, SEQ, ready=mem_chunk)
            side[0] = tokens()
            straight(f, 1, 3, from_xb, SEQ)
            finish()

            def ones_step(key, src, k):
                bank_for_step(pe, key)
                pe.wait_ge(sums, k + 1)
                done(nc.tensor.matmul(step_bank(key)[:, 0:src.shape[-1]], ones[:], src, start=True, stop=True))

            def mean_step(name):
                ones_step((name, 0), mean[:, 0:SEQ], SUMS[name])

            def spread_step(name):
                key = (name, 1)
                bank_for_step(pe, key)
                pe.wait_ge(sums, SUMS[name] + 2)
                done(nc.tensor.matmul(step_bank(key), ones[:], stat[:, :, 0:SEQ], start=True, stop=True))

            ones_step(("n1", 0), acc[:], SUMS["n1"])
            wait_tiles_taken(pe, ph["kv"].t0 + 8)
            for tb in range(2):
                key = ("vmT", tb)
                bank_for_step(pe, key)
                for j in range(H_MEM):
                    ins = nc.tensor.transpose(step_bank(key)[:, j * P:j * P + P], vmT[:, j, tb * P:tb * P + P], ident[:])
                done(ins)

            f = ph["glr"]
            pair(f.b0, 0, f.t0, 0, from_xa(TOK), TOK, ready=chunk_of_xa(XA["n1"]), alone=True)

            def gate_side():
                yield
                pe.wait_ge(gw_in, 16)
                wait_tile_taken(pe, ph["glr"].t0)
                for j in range(GLA_H):
                    key = ("gate", j)
                    bank_for_step(pe, key)
                    done(nc.tensor.matmul(step_bank(key)[:, 0:TOK], gw2[:, j * P:j * P + P], glr, start=True, stop=True))

            side[0] = gate_side()
            straight(ph["v"], 0, 4, from_xa(TOK), TOK)
            finish()

            def token_part(tb):
                return (META, 0) if tb == 2 else (P, X0 + tb * P)

            def values_side():
                wait_tiles_taken(pe, ph["qk"].t0)
                for tb in range(3):
                    w, o = token_part(tb)
                    for jh in range(2):
                        yield
                        yield
                        key = ("vT", 2 * tb + jh)
                        bank_for_step(pe, key)
                        for j in range(4):
                            ins = nc.tensor.transpose(step_bank(key)[0:w, j * P:j * P + P], vT[:, 4 * jh + j, o:o + w], ident[:])
                        done(ins)

            side[0] = values_side()
            straight(ph["qk"], 0, 2, from_tokens, SEQ)
            straight(ph["qk"], 2, 2, from_xa(TOK), TOK)
            finish()

            def gla_side():
                wait_tiles_taken(pe, ph["pu"].t0)
                for tb in range(3):
                    w, o = token_part(tb)
                    key = ("keT", tb)
                    bank_for_step(pe, key)
                    for j in range(GLA_H):
                        ins = nc.tensor.transpose(step_bank(key)[0:w, j * P:j * P + P], k_end[:, j, o:o + w], ident[:])
                    done(ins)
                yield
                for tb in range(2):
                    key = ("sc", tb)
                    bank_for_step(pe, key)
                    for j in range(GLA_H):
                        for r in (0, CHUNK):
                            o = X0 + tb * P + r
                            ins = nc.tensor.matmul(step_bank(key)[r:r + CHUNK, j * P + r:j * P + r + CHUNK],
                                                   k_inv[:, j, o:o + CHUNK], q_dec[:, j, o:o + CHUNK], start=True, stop=True)
                    done(ins)
                yield
                for s in range(6):
                    wait_step_taken(pe, ("vT", s))
                for s in range(3):
                    wait_step_taken(pe, ("keT", s))
                for jj in range(GLA_H + 2):
                    for c in range(NCH):
                        if jj < GLA_H:
                            j = jj
                            key = ("S", NCH * j + c)
                            bank_for_step(pe, key)
                            o = step_bank(key)[:, 0:GLA_DV]
                            if c == 0:
                                ins = nc.tensor.matmul(o, ke_meta[:, j * P:j * P + P], v_meta[:, j * GLA_DV:(j + 1) * GLA_DV], start=True, stop=True)
                            else:
                                tb, r = (c - 1) // 2, CHUNK * ((c - 1) % 2)
                                ins = nc.tensor.matmul(o, ke_tok[r:r + CHUNK, tb, j * P:j * P + P],
                                                       v_tok[r:r + CHUNK, tb, j * GLA_DV:(j + 1) * GLA_DV], start=True, stop=True)
                            done(ins)
                            if c % 2:
                                yield
                    if jj >= 2:
                        j = jj - 2
                        if j == 0:
                            pe.wait_ge(sc_masked, 2)
                        for c in range(NCH):
                            wait_step_taken(pe, ("S", NCH * j + c))
                        for vh in range(2):
                            key = ("o", 2 * j + vh)
                            bank_for_step(pe, key)
                            o = step_bank(key)
                            col = j * GLA_DV + vh * P
                            for tb in range(2):
                                nc.tensor.matmul(o[:, tb * P:tb * P + P], v_tok[:, tb, col:col + P], sc[:, tb, j], start=tb == 0, stop=False)
                            for c in range(NCH):
                                ins = nc.tensor.matmul(o[:, c * CHUNK:(c + 1) * CHUNK], S[:, j, c, vh * P:vh * P + P],
                                                       q_dec[:, j, X0 + c * CHUNK:X0 + (c + 1) * CHUNK], start=False, stop=c == NCH - 1)
                            done(ins)
                            if j >= 2:
                                yield

            side[0] = gla_side()
            straight(ph["pu"], 0, 4, from_xa(TOK), TOK)
            finish()

            def pool_side():
                yield
                yield
                pe.wait_ge(sums, SUMS["on"] + 1)
                for s in range(2):
                    key = ("on", s)
                    bank_for_step(pe, key)
                    done(nc.tensor.matmul(step_bank(key), ones[:], R[:, 17152 + 512 * s:17152 + 512 * s + 512], start=True, stop=True))
                pe.wait_ge(pool_in, 16)
                for g in range(POOL_G):
                    for _ in range((2, 2, 5, 2)[g]):
                        yield
                    pe.wait_ge(pool_ready, g + 1)
                    for dt in range(2):
                        key = ("pool", 2 * g + dt)
                        bank_for_step(pe, key)
                        for c in range(2):
                            ins = nc.tensor.matmul(step_bank(key)[:, 0:SEQ], pool_w[:, 2 * g + c, dt * P:dt * P + P], pool_y[:, 2 * g + c],
                                                   start=c == 0, stop=c == 1)
                        done(ins)

            side[0] = pool_side()
            straight(ph["r"], 0, 4, from_tokens, SEQ)
            finish()

            def ready_mix(c):
                if c % 4 == 0 and c >= 8:
                    pe.wait_ge(xa_lo, XA["pool"] + c - 4)
                if c % 4 == 0 and c < 8:
                    pe.wait_ge(gla_lo, c // 4 + 1)

            pool_first = (range(8, 16), range(0, 8))
            straight(ph["out"], 0, 2, from_xa(SEQ), SEQ, ready=ready_mix, blocks=pool_first)
            run(ph["out"], 2, 6, from_xa(SEQ), SEQ, blocks=pool_first)
            ones_step(("n2", 0), acc[:, 0:SEQ], SUMS["n2"])

            def mlp_down(g):
                def hidden(c):
                    pe.wait_ge(xb_lo, g * 16 + (XB["mlp"] + c + 1))

                pair(ph["mlp"].b0 + 16, g * 32, ph["mlp"].t0 + 16, g * 8, from_xb, SEQ, ready=hidden)
                pair(ph["mlp"].b0 + 18, g * 32, ph["mlp"].t0 + 18, g * 8, from_xb, SEQ)
                with pe.Fori(1, 4) as i:
                    for q in range(2):
                        pair(ph["mlp"].b0 + 16 + 2 * q, g * 32 + i * 4, ph["mlp"].t0 + 16 + 2 * q, g * 8 + i, from_xb, SEQ)

            f = ph["mlp"]
            straight(f, 0, 2, from_xa(SEQ), SEQ, ready=chunk_of_xa(XA["n2"]))
            run(f, 2, 6, from_xa(SEQ), SEQ)
            mlp_down(0)
            with pe.Fori(1, UP_GROUPS) as g:
                with pe.Fori(0, 4) as i:
                    for q in range(2):
                        pair(f.b0 + 2 * q, g * 32 + i * 4, f.t0 + 2 * q, g * 8 + i, from_xa(SEQ), SEQ)
                mlp_down(g)
            ones_step(("nf", 0), acc[:, 0:SEQ], SUMS["nf"])

            def latent_side():
                for _ in range(8):
                    yield
                ones_step(("ckv", 0), csq[:, 0], SUMS["ckv"])
                wait_tile_taken(pe, ph["dsa"].t0 + 3)
                key = ("wT", 0)
                bank_for_step(pe, key)
                for tb in range(2):
                    ins = nc.tensor.transpose(step_bank(key)[:, tb * IDX_H:(tb + 1) * IDX_H], ki[0:IDX_H, 1, tb * P:tb * P + P],
                                              ident[0:IDX_H, 0:IDX_H])
                done(ins)
                wait_tile_taken(pe, ph["dsa"].t0 + 2)
                key = ("kmean", 0)
                bank_for_step(pe, key)
                done(nc.tensor.matmul(step_bank(key)[:, 0:SEQ], ones[IDX_D:P, :], ki[IDX_D:P, 0], start=True, stop=True))
                for _ in range(4):
                    yield
                key = ("kvar", 0)
                bank_for_step(pe, key)
                pe.wait_ge(squares, SQS["kvar"] + 1)
                done(nc.tensor.matmul(step_bank(key)[:, 0:SEQ], ones[IDX_D:P, :], csq[IDX_D:P, 1], start=True, stop=True))
                yield
                key = ("ckvT", 0)
                bank_for_step(pe, key)
                pe.wait_ge(normed, 16 * 3 + 2)
                for tb in range(2):
                    for c in range(2):
                        ins = nc.tensor.transpose(step_bank(key)[:, tb * 256 + c * P:tb * 256 + c * P + P], ckv[:, c, tb * P:tb * P + P], ident[:])
                done(ins)

            def index_side():
                wait_tiles_taken(pe, ph["dsa"].t0 + 12)
                pe.wait_ge(kdup_in, 16)
                for j in range(IDX_H):
                    key = ("idx", j)
                    bank_for_step(pe, key)
                    r = IDX_D * (j % 2)
                    for tb in range(2):
                        ins = nc.tensor.matmul(step_bank(key)[:, tb * SEQ:(tb + 1) * SEQ], qi[r:r + IDX_D, j // 2, tb * P:tb * P + P],
                                               kdup[r:r + IDX_D], start=True, stop=True)
                    done(ins)
                    yield

            side[0] = latent_side()
            f = ph["dsa"]
            straight(f, 0, 6, from_xa(SEQ), SEQ, ready=chunk_of_xa(XA["nf"]))
            finish()
            side[0] = index_side()
            straight(f, 6, 4, from_xa(SEQ), SEQ)
            finish()

            def transpose_p(key, k):
                bank_for_step(pe, key)
                pe.wait_ge(pnorm, k + 1)
                s = sb_s[:, k % 2].rearrange("p (b n) -> p b n", b=2)
                for kb in range(2):
                    for tb in range(2):
                        ins = nc.tensor.transpose(step_bank(key)[:, kb * SEQ + tb * P:kb * SEQ + tb * P + P], s[:, tb, kb * P:kb * P + P], ident[:])
                done(ins)

            def pt(k, kb):
                return sb_pt[:, k % 2, kb * SEQ:(kb + 1) * SEQ]

            def dsa_side():
                for _ in range(8):
                    yield
                pe.wait_ge(uk_in, 32)
                wait_tiles_taken(pe, ph["moba"].t0)
                wait_step_taken(pe, ("ckvT", 0))
                for beat in range(H_DSA + 2):
                    for half in (0, 2):
                        for key in dsa_beat(beat, half):
                            name, j = key
                            k = HEADS["dsa"] + j
                            if name == "dsa_t":
                                transpose_p(key, k)
                                continue
                            bank_for_step(pe, key)
                            b = step_bank(key)
                            if name == "dsa_q":
                                for c in range(2):
                                    ins = nc.tensor.matmul(b[:, c * SEQ:(c + 1) * SEQ], uk[:, j, c * P:c * P + P], qd[:, j], start=True, stop=True)
                            elif name == "dsa_s":
                                wait_step_taken(pe, ("dsa_q", j))
                                for tb in range(2):
                                    for c in range(2):
                                        ins = nc.tensor.matmul(b[:, tb * SEQ:(tb + 1) * SEQ],
                                                               ql[:, j % 2, c * SEQ + tb * P:c * SEQ + tb * P + P], ckv[:, c], start=c == 0, stop=c == 1)
                            elif name == "dsa_l":
                                wait_step_taken(pe, ("dsa_t", j))
                                for c in range(2):
                                    for kb in range(2):
                                        ins = nc.tensor.matmul(b[:, c * SEQ:(c + 1) * SEQ], ckv_tok[:, kb, c * P:c * P + P], pt(k, kb),
                                                               start=kb == 0, stop=kb == 1)
                            else:
                                wait_step_taken(pe, ("dsa_l", j))
                                for c in range(2):
                                    ins = nc.tensor.matmul(b[:, 0:SEQ], uv[:, 2 * j + c], ol[:, j % 2, c * SEQ:(c + 1) * SEQ],
                                                           start=c == 0, stop=c == 1)
                            done(ins)
                        yield
                        yield

            side[0] = dsa_side()
            straight(ph["moba"], 0, 12, from_xa(SEQ), SEQ)
            finish()

            def head_side(kind, heads, q, keys, v):
                for beat in range(heads + 1):
                    for half in (0, 2):
                        for key in head_beat(kind, heads, beat, half):
                            name, j = key
                            k = HEADS[kind] + j
                            if name == kind + "_t":
                                transpose_p(key, k)
                                continue
                            bank_for_step(pe, key)
                            b = step_bank(key)
                            if name == kind + "_s":
                                for tb in range(2):
                                    ins = nc.tensor.matmul(b[:, tb * SEQ:(tb + 1) * SEQ], q[:, j, tb * P:tb * P + P], keys[:, j], start=True, stop=True)
                            else:
                                wait_step_taken(pe, (kind + "_t", j))
                                for kb in range(2):
                                    ins = nc.tensor.matmul(b[:, 0:SEQ], v[:, kb, j * P:j * P + P], pt(k, kb), start=kb == 0, stop=kb == 1)
                            done(ins)
                        yield
                        yield

            def moba_side():
                wait_tiles_taken(pe, ph["moba"].t0 + 24)
                for tb in range(2):
                    for jh in range(2):
                        key = ("vmoT", 2 * tb + jh)
                        bank_for_step(pe, key)
                        for j in range(4):
                            ins = nc.tensor.transpose(step_bank(key)[:, j * P:j * P + P], vmo[:, 4 * jh + j, tb * P:tb * P + P], ident[:])
                        done(ins)
                    yield
                for s in range(4):
                    wait_step_taken(pe, ("vmoT", s))
                yield from head_side("moba", H_MOBA, qm, km, vmo_tok)

            side[0] = moba_side()
            straight(ph["gate"], 0, 10, from_xa(SEQ), SEQ)
            finish()
            run(ph["gate"], 10, 6, from_xa(SEQ), SEQ)

            def map_pair(b, q, bd, td, ready=None):
                for kb in range(2):
                    pair(ph["o"].b0 + b + 2 * q + kb, bd, ph["o"].t0 + 2 * b + 4 * q + 2 * kb, td, from_xa(SEQ), SEQ,
                         blocks=(range(8 * kb, 8 * kb + 8),), ready=ready)

            map_pair(0, 0, 0, 0, ready=chunk_of_xa(XA["oa"]))
            map_pair(0, 1, 0, 0)
            with pe.Fori(1, 4) as i:
                for q in range(2):
                    map_pair(0, q, i * 4, i * 2)

            def merged(c):
                pe.wait_ge(xb_lo, XB["o"] + c + 1)

            f = ph["out2"]
            straight(f, 0, 2, from_xb, SEQ, ready=merged)

            run(f, 2, 2, from_xb, SEQ)
            mean_step("ln0")
            run(f, 4, 4, from_xb, SEQ)
            spread_step("ln0")
            straight(ph["qm"], 0, 1, from_xa(SEQ), SEQ, ready=chunk_of_xa(XA["ln0"]))

            def mem_side():
                yield
                for tb in range(2):
                    wait_step_taken(pe, ("vmT", tb))
                for key in MEM_ORDER:
                    j = key[1]
                    k = HEADS["mem"] + j
                    b = step_bank(key)
                    if key[0] == "mem_t":
                        transpose_p(key, k)
                        continue
                    if key[0] == "mem_s":
                        wait_tile_taken(pe, ph["qm"].t0 + j)
                    else:
                        wait_step_taken(pe, ("mem_t", j))
                    bank_for_step(pe, key)
                    for i in range(2):
                        if key[0] == "mem_s":
                            ins = nc.tensor.matmul(b[:, i * SEQ:(i + 1) * SEQ], qx[:, j, i * P:i * P + P], k_mem[:, j], start=True, stop=True)
                        else:
                            ins = nc.tensor.matmul(b[:, 0:SEQ], v_mem[:, i, j * P:j * P + P], pt(k, i), start=i == 0, stop=i == 1)
                    done(ins)
                    if key[0] == "mem_s" and j < 2:
                        yield

            side[0] = mem_side()
            straight(ph["qm"], 1, 1, from_xa(SEQ), SEQ)
            finish()

            for b in range(4):
                bs = ph["om"].b0 + b
                for half in range(2):
                    p = 2 * bs + half
                    pe.wait_ge(lo_made, p + 1)
                    for q in range(2):
                        t = ph["om"].t0 + 4 * b + 2 * half + q
                        pe.wait_ge(bank_free[t % BANKS], t // BANKS)
                        o = tile_ps(t, SEQ)
                        for c in range(4):
                            if t == ph["om"].t0:
                                wait_step_taken(pe, ("mem_o", c))
                            hi, lo = w_hi[:, p % CUT, 2 * c + q], w_lo[:, p % CUT, 2 * c + q]
                            x_hi, x_lo = xa[:, c, 0, 0:SEQ], xa[:, c, 1, 0:SEQ]
                            nc.tensor.matmul(o, hi, x_hi, start=c == 0, stop=False)
                            nc.tensor.matmul(o, hi, x_lo, start=False, stop=False)
                            ins = nc.tensor.matmul(o, lo, x_hi, start=False, stop=c == 3)
                    ins.then_inc(piece_done, 1)
            mean_step("ln1")
            spread_step("ln1")

            fb, ft = ph["ffn"].b0, ph["ffn"].t0
            three = (range(0, 8), range(8, 16), range(16, 22))

            def ffn_up(g, i, ready=None):
                for q in range(2):
                    pair(fb + 2 * q, g * 68 + i * 4, ft + 2 * q, g * 15 + i, from_xa(SEQ), SEQ, ready=ready if q == 0 else None)

            def ffn_down(g, i):
                def hidden(c):
                    pe.wait_ge(xb_lo, XB["ffn"] + g * FF_CH + c + 1)
                for q in range(4):
                    pair(fb + 44 + 3 * q, g * 68 + i * 12, ft + 44 + 2 * q, g * 15 + i * 2, from_xb, SEQ,
                         blocks=three, ready=hidden if q == 0 and i == 0 else None)

            for g in range(FF_GROUPS):
                if g == 0:
                    ffn_up(0, 0, ready=chunk_of_xa(XA["ln1"]))
                with pe.Fori(1 if g == 0 else 0, 11) as i:
                    ffn_up(g, i)
                ffn_down(g, 0)
                if g == FF_GROUPS - 1:
                    mean_step("ln2")
                ffn_down(g, 1)
            spread_step("ln2")
            for s in range(4):
                pe.wait_ge(biased, 16 * 2 + 4 * s + 4)
                for tb in range(2):
                    key = ("fin", 2 * s + tb)
                    bank_for_step(pe, key)
                    for j in range(4):
                        ins = nc.tensor.transpose(step_bank(key)[:, j * P:j * P + P], h[:, 4 * s + j, X0 + tb * P:X0 + tb * P + P], ident[:])
                    done(ins)

        @block.scalar
        def _(act):
            chain = [0]

            def link(ins):
                chain[0] += 1
                ins.then_inc(act_chain, 1)
                act.wait_ge(act_chain, chain[0])

            side = [None]

            def slot():
                if side[0] is not None:
                    next(side[0], None)

            def finish():
                for _ in side[0]:
                    pass
                side[0] = None

            def slots(n):
                for _ in range(n):
                    yield

            def copy(dst, src, **kw):
                return nc.scalar.activation(dst, src, ACT.Copy, **kw)

            pieces_end = [1 << 30]

            def cut(ps_, pd):
                bs = ps_ // 2
                act.wait_ge(loaded[bs % RAW], pd * 4 + 32 * (bs // RAW + 1))
                if not (isinstance(pd, int) and ps_ + pd < CUT):
                    act.wait_ge(piece_done, pd + (ps_ - CUT + 1))
                copy(w_hi[:, ps_ % CUT], raw[:, bs % RAW, :, (ps_ % 2) * P:(ps_ % 2) * P + P]).then_inc(hi_made, 1)

            last_piece = [0, 0]

            def complete():
                act.wait_ge(piece_done, last_piece[1] + (last_piece[0] + 1))

            def body(b0, bd, t0, td, evac, n_pairs=2, per_pair=2):
                for q in range(n_pairs):
                    for k in range(2 * per_pair):
                        p = 2 * (b0 + per_pair * q) + k
                        if p + AHEAD < pieces_end[0]:
                            cut(p + AHEAD, bd * 2)
                        if k >= 2 * per_pair - 2:
                            t = 2 * q + k - (2 * per_pair - 2)
                            last_piece[:] = p, bd * 2
                            evac(t0 + t, td, t)
                        slot()

            def straight(phase, first, n_pairs, evac):
                for q in range(first, first + n_pairs):
                    body(phase.b0 + 2 * q, 0, phase.t0 + 2 * q, 0,
                         lambda ts, td, t: evac(ts, td, (2 * q) % 4 + t, q // 2), n_pairs=1)

            def run(phase, first, n_pairs, evac):
                with act.Fori(first // 2, (first + n_pairs) // 2) as i:
                    body(phase.b0, i * 4, phase.t0, i, lambda ts, td, t: evac(ts, td, t, i))

            def free(ins, ts):
                ins.then_inc(bank_free[ts % BANKS], 1)

            def take(key, ins_fn):
                act.wait_ge(step_done, steps[key] + 1)
                taken(ins_fn(step_bank(key)), key)

            def nothing(ts, td, t, i=None):
                pass

            def copy_to(buf, n=SEQ, base=0):
                def ev(ts, td, t, i):
                    complete()
                    free(copy(buf[:, bass.ds(i * 4 + (base + t), 1), :], tile_ps(ts, n).unsqueeze(1)), ts)
                return ev

            for s in range(8):
                key = ("memT", s)
                act.wait_ge(step_done, steps[key] + 1)
                copy(xb[:, 2 * s:2 * s + 2, 0, :], step_bank(key).rearrange("p (c n) -> p c n", c=2)).then_inc(memhi, 1)
                if s < AHEAD:
                    cut(s, 0)
            for t in range(2):
                w = 96 if t == 0 else 98
                take(("vec", t), lambda b: copy(vec[:, 96 * t:96 * t + w], b[:, 0:w]))

            def tokens_side():
                yield
                for c in range(DC):
                    take(("xT", c), lambda b: copy(h[:, c, :], b[:, 0:TOK]))
                    if c % 2:
                        yield
                for c in range(DC - 4, DC):
                    wait_step_taken(act, ("xT", c))
                for q in range(4):
                    ins = nc.scalar.activation(SQ[:, 4 * q:4 * q + 4, :], h[:, 4 * q:4 * q + 4, :], ACT.Square)
                    ins.then_inc(squares, 1)
                    yield

            def norm_root(key, dst):
                wait_step_taken(act, key)
                nc.scalar.activation(dst, dst, ACT.Sqrt).then_inc(root, 1)

            def norm_cut(name, n, off, src):
                k = NORMS[name]
                for q in range(4):
                    act.wait_ge(normed, 16 * k + 4 * q + 4 + (2 if k > 2 else 0))
                    rows_q = src[:, 4 * q:4 * q + 4, off:off + n] if src is h else src[:, 4 * q:4 * q + 4, 0:n]
                    if name in LNS:
                        l = LNS[name]
                        for c in range(4 * q, 4 * q + 4):
                            nc.scalar.activation(h[:, c, off:off + n], h[:, c, off:off + n], ACT.Identity,
                                                 bias=vec[:, V_LB + 16 * l + c:V_LB + 16 * l + c + 1]).then_inc(biased, 1)
                        act.wait_ge(biased, 16 * l + 4 * q + 4)
                    if name != "ln2":
                        copy(xa[:, 4 * q:4 * q + 4, 0, 0:n], rows_q).then_inc(xa_hi, 4)

            def ev_kv(ts, td, t, i):
                complete()
                j = 4 * i + t
                free(copy(k_mem[:, j] if j < H_MEM else vmT[:, j - H_MEM], tile_ps(ts, SEQ)), ts)

            side[0] = None
            straight(ph["kv"], 0, 1, ev_kv)
            side[0] = tokens_side()
            straight(ph["kv"], 1, 3, ev_kv)
            finish()
            norm_root(("n1", 0), rstd[:])
            norm_cut("n1", TOK, 0, SQ)
            for tb in range(2):
                take(("vmT", tb), lambda b: copy(v_mem[:, tb], b))

            f = ph["glr"]
            for k in range(4):
                cut(2 * f.b0 + k + AHEAD, 0)
            last_piece[:] = 2 * f.b0 + 3, 0
            complete()
            free(copy(glr, tile_ps(f.t0, TOK)[0:GATE_RANK]), f.t0)

            def gate_side():
                yield from slots(2)
                for j in range(GLA_H):
                    take(("gate", j), lambda b: nc.scalar.activation(gs[:, j], b[:, 0:TOK], ACT.Identity, bias=vec[:, V_GB + j:V_GB + j + 1]))
                yield
                for j in range(GLA_H):
                    wait_step_taken(act, ("gate", j))
                link(nc.scalar.activation(gt[:], gs[:], ACT.Abs))
                yield
                link(nc.scalar.activation(gt[:], gt[:], ACT.Exp, scale=-1.0))
                yield
                nc.scalar.activation(gt[:], gt[:], ACT.Ln, bias=1.0).then_inc(gate_z, 1)
                yield from slots(3)
                act.wait_ge(gate_g, 1)
                nc.scalar.activation(e_pos[:], gs[:], ACT.Exp, scale=1.0 / 16).then_inc(gate_e, 1)
                yield
                nc.scalar.activation(e_neg[:], gs[:], ACT.Exp, scale=-1.0 / 16).then_inc(gate_e, 1)
                yield
                act.wait_ge(gate_g, 2)
                nc.scalar.activation(e_end[:], gt[:], ACT.Exp, scale=1.0 / 16).then_inc(gate_e, 1)

            side[0] = gate_side()
            straight(ph["v"], 0, 4, copy_to(vT, n=TOK))
            finish()

            def values_side():
                yield
                for tb in range(3):
                    for jh in range(2):
                        yield
                        yield
                        w = META if tb == 2 else P
                        dst = v_meta[:, 512 * jh:512 * jh + 512] if tb == 2 else v_tok[:, tb, 512 * jh:512 * jh + 512]
                        take(("vT", 2 * tb + jh), lambda b: copy(dst, b[0:w]))

            side[0] = values_side()
            straight(ph["qk"], 0, 4, nothing)
            finish()

            def gla_side():
                yield
                for tb in range(3):
                    w = META if tb == 2 else P
                    dst = ke_meta if tb == 2 else ke_tok[:, tb]
                    take(("keT", tb), lambda b: copy(dst, b[0:w]))
                yield
                act.wait_ge(sc_zero, 1)
                for tb in range(2):
                    key = ("sc", tb)
                    act.wait_ge(step_done, steps[key] + 1)
                    b = step_bank(key).rearrange("p (j n) -> p j n", j=GLA_H)
                    copy(sc[0:CHUNK, tb, :, 0:CHUNK], b[0:CHUNK, :, 0:CHUNK])
                    taken(copy(sc[CHUNK:P, tb, :, CHUNK:P], b[CHUNK:P, :, CHUNK:P]), key)

            side[0] = gla_side()
            straight(ph["pu"], 0, 4, copy_to(pu, n=TOK))
            finish()

            def pool_side():
                for s in range(8):
                    wait_step_taken(act, ("o", s))
                nc.scalar.activation(o_sq[:], oT[:], ACT.Square).then_inc(squares, 1)
                yield from slots(4)
                wait_step_taken(act, ("on", 0))
                norm_root(("on", 1), o_rs[:])
                for g in range(POOL_G):
                    yield from slots((1, 2, 5, 2)[g])
                    for j in (2 * g, 2 * g + 1):
                        take(("pool", j), lambda b: copy(pool_u[:, j], b[:, 0:SEQ], scale=vec[:, V_PS + j:V_PS + j + 1]))

            def ev_r(ts, td, t, i):
                complete()
                wait_tile_taken(act, ts - 2, td)
                nc.scalar.activation(rt[:, t % 2], tile_ps(ts, SEQ), ACT.Sigmoid).then_inc(act_half, 1)

            side[0] = pool_side()
            straight(ph["r"], 0, 4, ev_r)
            finish()
            for q in range(2):
                wait_step_taken(act, ("pool", 4 * q + 2))
                wait_step_taken(act, ("pool", 4 * q + 3))
                copy(xa[:, 8 + 4 * q:12 + 4 * q, 0, 0:SEQ], pool_u[:, 4 * q:4 * q + 4]).then_inc(xa_hi, 4)
            for q in range(2):
                act.wait_ge(gate_g, 3 + q)
                copy(xa[:, 4 * q:4 * q + 4, 0, 0:SEQ], oT[:, 4 * q:4 * q + 4]).then_inc(gla_hi, 1)

            def square(n, src):
                if n >= 2:
                    act.wait_ge(sq_added, n - 1)
                nc.scalar.activation(rt[:, n % 2], src, ACT.Square).then_inc(sq_made, 1)

            def ev_square(n0):
                def ev(ts, td, t, i):
                    j = 4 * i + t
                    wait_tile_taken(act, ts, td)
                    square(n0 + j, h[:, j, X0:TOK])
                return ev

            straight(ph["out"], 0, 8, ev_square(SQN["n2"]))
            norm_root(("n2", 0), rstd[:, 0:SEQ])
            norm_cut("n2", SEQ, 0, SQ)

            def ev_up(g):
                def ev(ts, td, t, i):
                    complete()
                    free(nc.scalar.activation(rt[:, t % 2], tile_ps(ts, SEQ), ACT.Relu), ts)
                    act.wait_ge(u_ready, g * 16 + i * 4 + (UR["mlp"] + t + 1))
                    copy(xb[:, bass.ds(i * 4 + t, 1), 0, :], ut[:, t % 2:t % 2 + 1, :]).then_inc(xb_hi, 1)
                return ev

            f = ph["mlp"]
            with act.Fori(0, UP_GROUPS - 1) as g:
                with act.Fori(0, 4) as i:
                    body(f.b0, g * 32 + i * 4, f.t0, g * 8 + i, lambda ts, td, t: ev_up(g)(ts, td, t, i))
                with act.Fori(0, 4) as i:
                    body(f.b0 + 16, g * 32 + i * 4, f.t0 + 16, g * 8 + i, nothing)
            g = UP_GROUPS - 1
            with act.Fori(0, 4) as i:
                body(f.b0, g * 32 + i * 4, f.t0, g * 8 + i, lambda ts, td, t: ev_up(g)(ts, td, t, i))
            for q in range(8):
                body(f.b0 + 16 + 32 * g + 2 * q, 0, f.t0 + 16 + 32 * g + 2 * q, 0,
                     lambda ts, td, t: ev_square(SQN["nf"])(ts, td, (2 * q) % 4 + t, q // 2), n_pairs=1)
            norm_root(("nf", 0), rstd[:, 0:SEQ])
            norm_cut("nf", SEQ, X0, h)

            def latent_side():
                yield from slots(4)
                for t in range(2):
                    wait_tile_taken(act, ph["dsa"].t0 + t)
                nc.scalar.activation(csq[:], ckv[:], ACT.Square).then_inc(squares, 1)
                yield from slots(6)
                norm_root(("ckv", 0), rstd[:, 0:SEQ])
                yield
                act.wait_ge(kcentered, 1)
                act.wait_ge(normed, 16 * 3 + 1)
                nc.scalar.activation(csq[IDX_D:P, 1], kdup[IDX_D:P], ACT.Square).then_inc(squares, 1)
                yield from slots(3)
                norm_root(("kvar", 0), rstd[IDX_D:P, 0:SEQ])
                take(("ckvT", 0), lambda b: copy(ckv_tok[:].rearrange("p a b -> p (a b)"), b))

            def ev_dsa(ts, td, t, i):
                complete()
                j = 4 * i + t
                dst = ckv[:, j] if j < 2 else ki[:, j - 2] if j < 4 else qi[:, j - 4] if j < 12 else qd[:, j - 12]
                free(copy(dst, tile_ps(ts, SEQ)), ts)

            def index_side():
                for j in range(IDX_H):
                    yield
                    key = ("idx", j)
                    if j >= 2:
                        act.wait_ge(idx_acc, j - 1)
                    take(key, lambda b: nc.scalar.activation(sb_r[:, j % 2], b, ACT.Relu))

            side[0] = latent_side()
            straight(ph["dsa"], 0, 6, ev_dsa)
            finish()
            side[0] = index_side()
            straight(ph["dsa"], 6, 4, ev_dsa)
            finish()

            def exps(k, src, signal=None):
                act.wait_ge(smax, k + 1)
                s = sb_s[:, k % 2].rearrange("p (b n) -> p b n", b=2)
                for tb in range(2):
                    c = 16 * (k % 2) + tb
                    ins = nc.scalar.activation(s[:, tb], src[:, tb], ACT.Exp, bias=small[:, c + 2:c + 3], scale=INV_SQRT_DH,
                                               accum_out=small[:, c + 4:c + 5])
                ins.then_inc(sexp if signal is None else signal, 1)

            def both(v):
                return v.rearrange("p (b n) -> p b n", b=2)

            def dsa_side():
                yield from slots(8)
                for beat in range(H_DSA + 2):
                    if 0 <= beat - 1 < H_DSA:
                        exps(HEADS["dsa"] + beat - 1, both(sb_s[:, (beat - 1) % 2]))
                    yield
                    for name, j in dsa_beat(beat, 0):
                        take((name, j), lambda b: copy((ql if name == "dsa_q" else ol)[:, j % 2], b))
                    yield
                    yield
                    for name, j in dsa_beat(beat, 2):
                        if name == "dsa_t":
                            take((name, j), lambda b: copy(sb_pt[:, j % 2], b))
                        if name == "dsa_o":
                            take((name, j), lambda b: copy(qd[:, j], b[:, 0:SEQ]))
                    yield

            def ev_moba(ts, td, t, i):
                complete()
                j = 4 * i + t
                free(copy((qm, km, vmo)[j // 8][:, j % 8], tile_ps(ts, SEQ)), ts)

            side[0] = dsa_side()
            straight(ph["moba"], 0, 12, ev_moba)
            finish()

            def head_side(kind, heads, q):
                for beat in range(heads + 1):
                    yield
                    for name, j in head_beat(kind, heads, beat, 0):
                        if name == kind + "_t":
                            take((name, j), lambda b: copy(sb_pt[:, (HEADS[kind] + j) % 2], b))
                    yield
                    if beat < heads:
                        k = HEADS[kind] + beat
                        exps(k, both(sb_s[:, k % 2]))
                    yield
                    for name, j in head_beat(kind, heads, beat, 2):
                        take((name, j), lambda b: copy(q[:, j], b[:, 0:SEQ]))
                    yield

            def moba_side():
                for tb in range(2):
                    yield
                    for jh in range(2):
                        take(("vmoT", 2 * tb + jh), lambda b: copy(vmo_tok[:, tb, 512 * jh:512 * jh + 512], b))
                yield from head_side("moba", H_MOBA, qm)

            def ev_gate(k):
                def ev(ts, td, t, i):
                    complete()
                    free(nc.scalar.activation(gates[:, bass.ds(i * 4 + (t - 16 * k), 1), k, :], tile_ps(ts, SEQ).unsqueeze(1), ACT.Exp,
                                              bias=vec[:, bass.ds(i * 4 + (V_BG + t), 1)], scale=-1.0), ts)
                return ev

            side[0] = moba_side()
            straight(ph["gate"], 0, 8, ev_gate(0))
            straight(ph["gate"], 8, 2, ev_gate(1))
            finish()
            run(ph["gate"], 10, 6, ev_gate(1))
            act.wait_ge(h_back, 1)
            act.wait_ge(piece_done, 2 * ph["o"].b0)
            for j in range(2):
                src = qd if j == 0 else qm
                for q in range(2):
                    copy(xa[:, 8 * j + 4 * q:8 * j + 4 * q + 4, 0, 0:SEQ], src[:, 4 * q:4 * q + 4]).then_inc(xa_hi, 4)

            with act.Fori(0, 4) as i:
                for q in range(2):
                    for k in range(4):
                        cut(2 * (ph["o"].b0 + 2 * q) + k + AHEAD, i * 8)
                        if k >= 2:
                            t = 2 * q + k - 2
                            act.wait_ge(u_ready, i * 4 + (UR["o"] + t + 1))
                            copy(xb[:, bass.ds(i * 4 + t, 1), 0, :], ut[:, t % 2:t % 2 + 1, :]).then_inc(xb_hi, 1)

            def ln_squares(n0, j, k0):
                if j >= 8:
                    for m in range(2):
                        act.wait_ge(shifted, k0 + 2 * (j - 8) + m + 1)
                        square(n0 + 2 * (j - 8) + m, h[:, j - 8 + 8 * m, X0:TOK])

            straight(ph["out2"], 0, 8, lambda ts, td, t, i: ln_squares(SQN["ln0"], 4 * i + t, 0))
            norm_root(("ln0", 1), rstd[:, 0:SEQ])
            norm_cut("ln0", SEQ, X0, h)

            def ev_qx(ts, td, t, i):
                complete()
                free(copy(qx[:, t], tile_ps(ts, SEQ)), ts)

            def mem_side():
                yield
                for key in MEM_ORDER:
                    j = key[1]
                    k = HEADS["mem"] + j
                    if key[0] == "mem_s":
                        yield
                        exps(k, both(step_bank(key)), side_free[steps[key] % BANKS])
                    elif key[0] == "mem_t":
                        take(key, lambda b: copy(sb_pt[:, k % 2], b))
                    else:
                        act.wait_ge(step_done, steps[key] + 1)
                        copy(xa[:, j, 0, 0:SEQ], step_bank(key)[:, 0:SEQ]).then_inc(memhi, 1)

            straight(ph["qm"], 0, 1, ev_qx)
            side[0] = mem_side()
            straight(ph["qm"], 1, 1, ev_qx)
            finish()
            for p in range(8):
                cut(2 * ph["om"].b0 + p + AHEAD, 0)
            for q in range(4):
                act.wait_ge(shifted, 16 + q + 1)
                nc.scalar.activation(SQ[:, 4 * q:4 * q + 4, 0:SEQ], h[:, 4 * q:4 * q + 4, X0:TOK], ACT.Square).then_inc(squares, 1)
            norm_root(("ln1", 1), rstd[:, 0:SEQ])
            norm_cut("ln1", SEQ, X0, h)

            b1, t1 = ph["ffn"].b0 + 44, ph["ffn"].t0 + 44
            for g in range(FF_GROUPS):
                with act.Fori(0, 11) as i:
                    def ev(ts, td, t):
                        complete()
                        if t % 2 == 0:
                            nc.scalar.activation(rt[:, (t // 2) % 2], tile_ps(ts, SEQ), ACT.Sigmoid).then_inc(act_half, 1)
                        else:
                            wait_tile_taken(act, ts, td)
                            copy(xb[:, bass.ds(i * 2 + t // 2, 1), 0, :], ut[:, t // 2:t // 2 + 1, :]).then_inc(xb_hi, 1)
                    body(ph["ffn"].b0, g * 68 + i * 4, ph["ffn"].t0, g * 15 + i, ev)
                if g < FF_GROUPS - 1:
                    with act.Fori(0, 2) as i:
                        body(b1, g * 68 + i * 12, t1, g * 15 + i * 2, nothing, n_pairs=4, per_pair=3)
                else:
                    pieces_end[0] = 2 * ph["end"].b0
                    for q in range(8):
                        body(b1 + g * 68 + 3 * q, 0, t1 + g * 60 + 2 * q, 0,
                             lambda ts, td, t: ln_squares(SQN["ln2"], 2 * q + t, 16 + 4), n_pairs=1, per_pair=3)
            norm_root(("ln2", 1), rstd[:, 0:SEQ])
            norm_cut("ln2", SEQ, X0, h)
            for s in range(4):
                for tb in range(2):
                    take(("fin", 2 * s + tb), lambda b: copy(o_tok[:, tb, 512 * s:512 * s + 512], b))

        @block.vector
        def _(dve):
            chain = [0]

            def link(ins):
                chain[0] += 1
                ins.then_inc(dve_chain, 1)
                dve.wait_ge(dve_chain, chain[0])

            V = nc.vector
            side = [None]

            def slot():
                if side[0] is not None:
                    next(side[0], None)

            def finish():
                for _ in side[0]:
                    pass
                side[0] = None

            def slots(n):
                for _ in range(n):
                    yield

            pieces_end = [1 << 30]

            def cut(ps_, pd):
                dve.wait_ge(hi_made, pd + (ps_ + 1))
                bs = ps_ // 2
                V.tensor_tensor(w_lo[:, ps_ % CUT], raw[:, bs % RAW, :, (ps_ % 2) * P:(ps_ % 2) * P + P],
                                w_hi[:, ps_ % CUT].bitcast(F32), ALU.subtract).then_inc(lo_made, 1)

            last_piece = [0, 0]

            def complete():
                dve.wait_ge(piece_done, last_piece[1] + (last_piece[0] + 1))

            def body(b0, bd, t0, td, evac, n_pairs=2, per_pair=2):
                for q in range(n_pairs):
                    for k in range(2 * per_pair):
                        p = 2 * (b0 + per_pair * q) + k
                        if p + AHEAD < pieces_end[0]:
                            cut(p + AHEAD, bd * 2)
                        if k >= 2 * per_pair - 2:
                            t = 2 * q + k - (2 * per_pair - 2)
                            last_piece[:] = p, bd * 2
                            evac(t0 + t, td, t)
                        slot()

            def straight(phase, first, n_pairs, evac):
                for q in range(first, first + n_pairs):
                    body(phase.b0 + 2 * q, 0, phase.t0 + 2 * q, 0,
                         lambda ts, td, t: evac(ts, td, (2 * q) % 4 + t, q // 2), n_pairs=1)

            def run(phase, first, n_pairs, evac):
                with dve.Fori(first // 2, (first + n_pairs) // 2) as i:
                    body(phase.b0, i * 4, phase.t0, i, lambda ts, td, t: evac(ts, td, t, i))

            def free(ins, ts):
                ins.then_inc(bank_free[ts % BANKS], 1)

            def take(key, fn):
                dve.wait_ge(step_done, steps[key] + 1)
                taken(fn(step_bank(key)), key)

            def nothing(ts, td, t, i=None):
                pass

            for s in range(8):
                key = ("memT", s)
                dve.wait_ge(memhi, s + 1)
                taken(V.tensor_tensor(xb[:, 2 * s:2 * s + 2, 1, :], step_bank(key).rearrange("p (c n) -> p c n", c=2),
                                      xb[:, 2 * s:2 * s + 2, 0, :].bitcast(F32), ALU.subtract), key)
                if s < AHEAD:
                    cut(s, 0)

            def norm_rstd(name, key, dst, n, feats, eps):
                dve.wait_ge(step_done, steps[key] + 1)
                taken(V.tensor_scalar(dst, step_bank(key)[P - dst.shape[0]:P, 0:n], 1.0 / feats, eps, ALU.mult, ALU.add), key)
                dve.wait_ge(root, ROOTS[name] + 1)
                link(V.reciprocal(dst, dst))

            def norm_apply(name, n, off, dst, wcol):
                def lows(q):
                    base = XA[name] + 4 * q
                    dve.wait_ge(xa_hi, base + 4)
                    V.tensor_tensor(xa[:, 4 * q:4 * q + 4, 1, 0:n], dst[:, 4 * q:4 * q + 4, o:o + n],
                                    xa[:, 4 * q:4 * q + 4, 0, 0:n].bitcast(F32), ALU.subtract).then_inc(xa_lo, 4)

                o = off if dst is h else 0
                for q in range(4):
                    if name in LNS:
                        dve.wait_ge(recentered, 4 * LNS[name] + q + 1)
                    for c in range(4 * q, 4 * q + 4):
                        V.scalar_tensor_tensor(out=dst[:, c, o:o + n], in0=h[:, c, off:off + n], scalar=vec[:, wcol + c:wcol + c + 1],
                                               in1=rstd[:, 0:n], op0=ALU.mult, op1=ALU.mult).then_inc(normed, 1)
                    if q > 0 and name != "ln2":
                        lows(q - 1)
                if name != "ln2":
                    lows(3)

            def norm1_side():
                yield from slots(9)
                dve.wait_ge(squares, 4)
                V.tensor_reduce(acc[:], SQ.rearrange("p c n -> p n c"), AX.X, ALU.add).then_inc(sums, 1)

            straight(ph["kv"], 0, 1, nothing)
            side[0] = norm1_side()
            straight(ph["kv"], 1, 3, nothing)
            finish()
            for t in range(2):
                wait_step_taken(dve, ("vec", t))
            V.tensor_scalar(vec[:, V_BG:V_BG + 32], vec[:, V_BG:V_BG + 32], -1.0, None, ALU.mult)
            norm_rstd("n1", ("n1", 0), rstd[:], TOK, D, EPS)
            norm_apply("n1", TOK, 0, SQ, V_N1)
            f = ph["glr"]
            for k in range(4):
                cut(2 * f.b0 + k + AHEAD, 0)

            def gate_side():
                link(V.memset(reset[:], 1.0))
                link(V.memset(reset[:, :, 0:1], 0.0))
                link(V.memset(reset[:, :, X0:TOK].rearrange("p j (c n) -> p j c n", n=CHUNK)[:, :, :, 0:1], 0.0))
                yield from slots(6)
                dve.wait_ge(gate_z, 1)
                link(V.scalar_tensor_tensor(out=gt[:], in0=gs[:], scalar=0.0, in1=gt[:], op0=ALU.min, op1=ALU.subtract))
                yield

                def flat(off):
                    return R[:, off:off + GLA_H * TOK]
                V.tensor_tensor_scan(flat(0), flat(15104), flat(1088), 0.0, ALU.mult, ALU.add).then_inc(gate_g, 1)
                yield
                dve.wait_ge(gate_g, 1)
                V.tensor_tensor(gt[:, :, 0:META], gs[:, :, META - 1:META].to_broadcast([P, GLA_H, META]), gs[:, :, 0:META], ALU.subtract)
                gx = gs[:, :, X0:TOK].rearrange("p j (c n) -> p j c n", n=CHUNK)
                V.tensor_tensor(gt[:, :, X0:TOK].rearrange("p j (c n) -> p j c n", n=CHUNK),
                                gx[:, :, :, CHUNK - 1:CHUNK].to_broadcast([P, GLA_H, NCH, CHUNK]), gx, ALU.subtract).then_inc(gate_g, 1)

            side[0] = gate_side()
            straight(ph["v"], 0, 4, nothing)
            finish()

            def ev_qk(ts, td, t, i):
                complete()
                if i == 0:
                    free(V.scalar_tensor_tensor(out=q_dec[:, t, X0:TOK], in0=tile_ps(ts, SEQ), scalar=GLA_DK ** -0.5, in1=e_pos[:, t, X0:TOK],
                                                op0=ALU.mult, op1=ALU.mult), ts)
                else:
                    V.tensor_tensor(k_inv[:, t], tile_ps(ts, TOK), e_neg[:, t], ALU.mult)
                    free(V.tensor_tensor(k_end[:, t], tile_ps(ts, TOK), e_end[:, t], ALU.mult), ts)

            dve.wait_ge(gate_e, 3)
            straight(ph["qk"], 0, 4, ev_qk)

            def gla_side():
                yield from slots(3)
                for jj in range(GLA_H + 2):
                    for c in range(NCH):
                        if jj < GLA_H:
                            key = ("S", NCH * jj + c)
                            if c == 0:
                                take(key, lambda b: V.tensor_copy(S[:, jj, 0], b[:, 0:GLA_DV]))
                            else:
                                wait_step_taken(dve, ("S", NCH * jj + c - 1))
                                end = X0 + c * CHUNK - 1
                                take(key, lambda b: V.scalar_tensor_tensor(out=S[:, jj, c], in0=S[:, jj, c - 1], scalar=e_pos[:, jj, end:end + 1],
                                                                           in1=b[:, 0:GLA_DV], op0=ALU.mult, op1=ALU.add))
                            if c % 2:
                                yield
                    if jj >= 2:
                        for vh in range(2):
                            j = 2 * (jj - 2) + vh
                            take(("o", j), lambda b: V.tensor_copy(oT[:, j], b[:, 0:SEQ]))
                            if jj >= 4:
                                yield

            side[0] = gla_side()
            straight(ph["pu"], 0, 4, nothing)
            finish()

            def window(g):
                src = pu[:, 2 * g:2 * g + 2]
                if g > 0:
                    dve.wait_ge(pool_ready, g)
                lo, bufs = 0, [win_a, win_b]
                for l in range(g + 1):
                    sh = 1 << l
                    dst = bufs[l % 2]
                    link(V.tensor_tensor(dst[:, :, lo + sh:TOK], src[:, :, lo + sh:TOK], src[:, :, lo:TOK - sh], ALU.add))
                    src, lo = dst, lo + sh
                V.scalar_tensor_tensor(out=pool_y[:, 2 * g:2 * g + 2], in0=src[:, :, X0:TOK], scalar=1.0 / (2 << g),
                                       in1=pu[:, 2 * g:2 * g + 2, X0:TOK], op0=ALU.mult, op1=ALU.subtract).then_inc(pool_ready, 1)

            def gla_gate(q):
                wait_tile_taken(dve, ph["r"].t0 + 4 * q + 2)
                wait_tile_taken(dve, ph["r"].t0 + 4 * q + 3)
                V.tensor_tensor(oT[:, 4 * q:4 * q + 4], oT[:, 4 * q:4 * q + 4], r_silu[:, 4 * q:4 * q + 4], ALU.mult).then_inc(gate_g, 1)

            def gla_low(q):
                dve.wait_ge(gla_hi, q + 1)
                V.tensor_tensor(xa[:, 4 * q:4 * q + 4, 1, 0:SEQ], oT[:, 4 * q:4 * q + 4], xa[:, 4 * q:4 * q + 4, 0, 0:SEQ].bitcast(F32),
                                ALU.subtract).then_inc(gla_lo, 1)

            def pool_side():
                yield
                dve.wait_ge(squares, SQS["on"] + 1)
                sq2 = o_sq.rearrange("p (j v) n -> p j v n", v=2)
                V.tensor_tensor(o_ss[:], sq2[:, :, 0], sq2[:, :, 1], ALU.add).then_inc(sums, 1)
                yield
                wait_tiles_taken(dve, ph["r"].t0)
                window(0)
                yield
                for s in range(2):
                    take(("on", s), lambda b: V.tensor_scalar(R[:, 18176 + 512 * s:18176 + 512 * s + 512], b, 1.0 / GLA_DV, EPS, ALU.mult, ALU.add))
                yield
                window(1)
                yield
                dve.wait_ge(root, ROOTS["on"] + 1)
                link(V.reciprocal(o_rs[:], o_rs[:]))
                for half in range(2):
                    yield
                    for j in range(4 * half, 4 * half + 4):
                        ins = V.scalar_tensor_tensor(out=oT[:, j], in0=oT[:, j], scalar=vec[:, V_GLA + j % 2:V_GLA + j % 2 + 1],
                                                     in1=o_rs[:, j // 2], op0=ALU.mult, op1=ALU.mult)
                    link(ins)
                yield
                gla_gate(0)
                yield
                window(2)
                yield
                yield
                window(3)

            def ev_r(ts, td, t, i):
                dve.wait_ge(act_half, i * 4 + (t + 1))
                free(V.tensor_tensor(r_silu[:, bass.ds(i * 4 + t, 1), :], tile_ps(ts, SEQ).unsqueeze(1), rt[:, t % 2:t % 2 + 1, :], ALU.mult), ts)

            side[0] = pool_side()
            straight(ph["r"], 0, 4, ev_r)
            finish()
            gla_gate(1)
            for q in range(2):
                dve.wait_ge(xa_hi, XA["pool"] + 4 * q + 4)
                V.tensor_tensor(xa[:, 8 + 4 * q:12 + 4 * q, 1, 0:SEQ], pool_u[:, 4 * q:4 * q + 4],
                                xa[:, 8 + 4 * q:12 + 4 * q, 0, 0:SEQ].bitcast(F32), ALU.subtract).then_inc(xa_lo, 4)
            gla_low(0)
            gla_low(1)

            def add_square(n, first):
                dve.wait_ge(sq_made, n + 1)
                if n > 0:
                    dve.wait_ge(sq_added, n)
                if first:
                    V.tensor_copy(acc[:, 0:SEQ], rt[:, n % 2]).then_inc(sq_added, 1)
                else:
                    V.tensor_tensor(acc[:, 0:SEQ], acc[:, 0:SEQ], rt[:, n % 2], ALU.add).then_inc(sq_added, 1)

            def residual(ts, td, chunk, scale=None):
                complete()
                hc = h[:, chunk, X0:TOK]
                b = tile_ps(ts, SEQ).unsqueeze(1)
                if scale is None:
                    free(V.tensor_tensor(hc, b, hc, ALU.add), ts)
                else:
                    free(V.scalar_tensor_tensor(out=hc, in0=hc, scalar=scale, in1=b, op0=ALU.mult, op1=ALU.add), ts)

            def ev_squares(n0):
                def ev(ts, td, t, i):
                    j = 4 * i + t
                    residual(ts, td, slice(j, j + 1))
                    if j > 0:
                        add_square(n0 + j - 1, j == 1)
                return ev

            def last_square(n):
                dve.wait_ge(sq_made, n + 1)
                dve.wait_ge(sq_added, n)
                link(V.tensor_tensor(acc[:, 0:SEQ], acc[:, 0:SEQ], rt[:, n % 2], ALU.add))
                V.tensor_copy(small[:, 9:10], acc[:, 0:1]).then_inc(sq_added, 1)
                V.tensor_copy(small[:, 10:11], acc[:, 0:1]).then_inc(sums, 1)

            straight(ph["out"], 0, 8, ev_squares(SQN["n2"]))
            last_square(SQN["n2"] + 15)
            norm_rstd("n2", ("n2", 0), rstd[:, 0:SEQ], SEQ, D, EPS)
            norm_apply("n2", SEQ, X0, SQ, V_N2)

            def ev_up(g):
                def ev(ts, td, t, i):
                    wait_tile_taken(dve, ts, td)
                    V.tensor_tensor(ut[:, t % 2], rt[:, t % 2], rt[:, t % 2], ALU.mult).then_inc(u_ready, 1)
                    dve.wait_ge(xb_hi, g * 16 + i * 4 + (XB["mlp"] + t + 1))
                    c = bass.ds(i * 4 + t, 1)
                    V.tensor_tensor(xb[:, c, 1, :], ut[:, t % 2:t % 2 + 1, :], xb[:, c, 0, :].bitcast(F32), ALU.subtract).then_inc(xb_lo, 1)
                return ev

            f = ph["mlp"]
            with dve.Fori(0, UP_GROUPS - 1) as g:
                with dve.Fori(0, 4) as i:
                    body(f.b0, g * 32 + i * 4, f.t0, g * 8 + i, lambda ts, td, t: ev_up(g)(ts, td, t, i))
                with dve.Fori(0, 4) as i:
                    body(f.b0 + 16, g * 32 + i * 4, f.t0 + 16, g * 8 + i, lambda ts, td, t: residual(ts, td, bass.ds(i * 4 + t, 1)))
            g = UP_GROUPS - 1
            with dve.Fori(0, 4) as i:
                body(f.b0, g * 32 + i * 4, f.t0, g * 8 + i, lambda ts, td, t: ev_up(g)(ts, td, t, i))
            for q in range(8):
                body(f.b0 + 16 + 32 * g + 2 * q, 0, f.t0 + 16 + 32 * g + 2 * q, 0,
                     lambda ts, td, t: ev_squares(SQN["nf"])(ts, td, (2 * q) % 4 + t, q // 2), n_pairs=1)
            last_square(SQN["nf"] + 15)
            norm_rstd("nf", ("nf", 0), rstd[:, 0:SEQ], SEQ, D, EPS)
            norm_apply("nf", SEQ, X0, h, V_FIN)

            up = slice(IDX_D, P)

            def latent_side():
                yield from slots(5)
                dve.wait_ge(squares, SQS["ckv"] + 1)
                V.tensor_tensor(csq[:, 0], csq[:, 0], csq[:, 1], ALU.add).then_inc(sums, 1)
                yield from slots(4)
                key = ("ckv", 0)
                take(key, lambda b: V.tensor_scalar(rstd[:, 0:SEQ], b[:, 0:SEQ], 1.0 / 256, LN_EPS, ALU.mult, ALU.add))
                take(("wT", 0), lambda b: V.tensor_scalar(w_tok[:].rearrange("p a b -> p (a b)"), b[:, 0:2 * IDX_H],
                                                          IDX_D ** -0.5 * IDX_H ** -0.5, None, ALU.mult))
                take(("kmean", 0), lambda b: V.tensor_scalar(mean[up, 0:SEQ], b[up, 0:SEQ], 1.0 / IDX_D, None, ALU.mult))
                wait_step_taken(dve, ("kmean", 0))
                V.tensor_tensor(kdup[up], ki[up, 0], mean[up, 0:SEQ], ALU.subtract).then_inc(kcentered, 1)
                yield from slots(2)
                dve.wait_ge(root, ROOTS["ckv"] + 1)
                link(V.reciprocal(rstd[:, 0:SEQ], rstd[:, 0:SEQ]))
                for c in range(2):
                    V.scalar_tensor_tensor(out=ckv[:, c], in0=ckv[:, c], scalar=vec[:, V_KVN + c:V_KVN + c + 1], in1=rstd[:, 0:SEQ],
                                           op0=ALU.mult, op1=ALU.mult).then_inc(normed, 1)
                yield from slots(3)
                dve.wait_ge(normed, 16 * 3 + 2)
                take(("kvar", 0), lambda b: V.tensor_scalar(rstd[up, 0:SEQ], b[up, 0:SEQ], 1.0 / IDX_D, LN_EPS, ALU.mult, ALU.add))
                yield from slots(2)
                dve.wait_ge(root, ROOTS["kvar"] + 1)
                link(V.reciprocal(rstd[up, 0:SEQ], rstd[up, 0:SEQ]))
                link(V.scalar_tensor_tensor(out=kdup[up], in0=kdup[up], scalar=vec[up, V_IG:V_IG + 1], in1=rstd[up, 0:SEQ],
                                            op0=ALU.mult, op1=ALU.mult))
                V.tensor_scalar(kdup[up], kdup[up], vec[up, V_IB:V_IB + 1], None, ALU.add).then_inc(kdup_ready, 1)

            side[0] = latent_side()
            straight(ph["dsa"], 0, 6, nothing)
            finish()

            def index_side():
                for j in range(IDX_H):
                    yield
                    wait_step_taken(dve, ("idx", j))
                    rr = sb_r[:, j % 2].rearrange("p (b n) -> p b n", b=2)
                    if j > 0:
                        dve.wait_ge(idx_acc, j)
                    for tb in range(2):
                        wcol = w_tok[:, tb, j:j + 1]
                        if j == 0:
                            ins = V.tensor_scalar(score[:, tb], rr[:, tb], wcol, None, ALU.mult)
                        else:
                            ins = V.scalar_tensor_tensor(out=score[:, tb], in0=rr[:, tb], scalar=wcol, in1=score[:, tb], op0=ALU.mult, op1=ALU.add)
                    ins.then_inc(idx_acc, 1)

            side[0] = index_side()
            straight(ph["dsa"], 6, 4, nothing)
            finish()

            def both(v):
                return v.rearrange("p (b n) -> p b n", b=2)

            def softmax_max(key, k, bias, slope):
                s = both(sb_s[:, k % 2])
                if bias is not None:
                    if slope is None:
                        take(key, lambda b: V.tensor_tensor(sb_s[:, k % 2], b, bias, ALU.add))
                    else:
                        take(key, lambda b: V.scalar_tensor_tensor(out=s, in0=bias, scalar=slope, in1=both(b), op0=ALU.mult, op1=ALU.add))
                    wait_step_taken(dve, key)
                    src = s
                else:
                    dve.wait_ge(step_done, steps[key] + 1)
                    src = both(step_bank(key))
                sm = small[:, 16 * (k % 2):16 * (k % 2) + 8]
                link(V.tensor_reduce(sm[:, 0:2], src, AX.X, ALU.max, negate=True))
                V.tensor_scalar(sm[:, 2:4], sm[:, 0:2], INV_SQRT_DH, None, ALU.mult).then_inc(smax, 1)

            def softmax_norm(key, k, in_bank=False):
                s = both(sb_s[:, k % 2])
                if in_bank:
                    wait_step_taken(dve, key)
                else:
                    dve.wait_ge(sexp, k + 1)
                sm = small[:, 16 * (k % 2):16 * (k % 2) + 8]
                link(V.reciprocal(sm[:, 6:8], sm[:, 4:6]))
                for tb in range(2):
                    ins = V.tensor_scalar(s[:, tb], s[:, tb], sm[:, 6 + tb:7 + tb], None, ALU.mult)
                ins.then_inc(pnorm, 1)

            def dsa_side():
                dve.wait_ge(idx_acc, IDX_H)
                V.tensor_copy(small[:, 9:10], score[:, 0, 0:1]).then_inc(score_ready, 1)
                yield from slots(2)
                dve.wait_ge(score_cut, 1)
                for rnd in range(TOPK // 8):
                    for tb in range(2):
                        ins = V.max(out=top8[:, tb], in_=score[:, tb])
                    link(ins)
                    for tb in range(2):
                        ins = V.match_replace(out=score[:, tb], in_to_replace=top8[:, tb], in_values=score[:, tb], imm_value=TAKEN)
                    link(ins)
                    if rnd not in (0, 4):
                        yield
                V.tensor_scalar(mbias[:], score[:], TAKEN, NEG, ALU.not_equal, ALU.mult).then_inc(sel_ready, 1)
                dve.wait_ge(dist_ready, 1)
                for beat in range(H_DSA + 2):
                    yield
                    if 0 <= beat - 1 < H_DSA:
                        softmax_norm(("dsa_s", beat - 1), HEADS["dsa"] + beat - 1, False)
                    yield
                    yield
                    if beat < H_DSA:
                        if beat == 0:
                            dve.wait_ge(sel_cut, 1)
                        link(V.scalar_tensor_tensor(out=hb[:], in0=dist[:].rearrange("p a b -> p (a b)"), scalar=ALIBI[beat] / INV_SQRT_DH,
                                                    in1=mbias[:].rearrange("p a b -> p (a b)"), op0=ALU.mult, op1=ALU.add))
                        softmax_max(("dsa_s", beat), HEADS["dsa"] + beat, hb[:], None)
                    yield

            side[0] = dsa_side()
            straight(ph["moba"], 0, 12, nothing)
            finish()

            def head_side(kind, heads):
                for beat in range(heads + 1):
                    yield
                    if beat < heads:
                        k = HEADS[kind] + beat
                        key = (kind + "_s", beat)
                        softmax_max(key, k, distc[:], ALIBI[beat] / INV_SQRT_DH)
                    yield
                    yield
                    if beat < heads:
                        softmax_norm(key, k)
                    yield

            def moba_side():
                yield from slots(2)
                yield from head_side("moba", H_MOBA)

            def ev_gate(k):
                def ev(ts, td, t, i):
                    wait_tile_taken(dve, ts, td)
                    c = gates[:, bass.ds(i * 4 + (t - 16 * k), 1), k, :]
                    V.tensor_scalar(c, c, 1.0, None, ALU.add).then_inc(gate_one, 1)
                    dve.wait_ge(gate_one, i * 4 + (t + 1))
                    V.reciprocal(c, c).then_inc(gate_made, 1)
                return ev

            side[0] = moba_side()
            straight(ph["gate"], 0, 8, ev_gate(0))
            straight(ph["gate"], 8, 2, ev_gate(1))
            finish()
            for j in range(4, 8):
                wait_step_taken(dve, ("moba_o", j))
            for q in range(4):
                ins = V.tensor_tensor(h[:, 4 * q:4 * q + 4, X0:TOK], xa[:, 4 * q:4 * q + 4, 0, 0:SEQ].bitcast(F32),
                                      xa[:, 4 * q:4 * q + 4, 1, 0:SEQ].bitcast(F32), ALU.add)
            ins.then_inc(h_back, 1)
            straight(ph["gate"], 10, 6, ev_gate(1))
            for j in range(2):
                src = qd if j == 0 else qm
                for q in range(2):
                    c = 8 * j + 4 * q
                    dve.wait_ge(xa_hi, XA["oa"] + c + 4)
                    V.tensor_tensor(xa[:, c:c + 4, 1, 0:SEQ], src[:, 4 * q:4 * q + 4], xa[:, c:c + 4, 0, 0:SEQ].bitcast(F32),
                                    ALU.subtract).then_inc(xa_lo, 4)

            t0 = ph["o"].t0
            dve.wait_ge(gate_made, 32)
            with dve.Fori(0, 4) as i:
                for q in range(2):
                    for k in range(4):
                        cut(2 * (ph["o"].b0 + 2 * q) + k + AHEAD, i * 8)
                        if k >= 2:
                            t = 2 * q + k - 2
                            ta, tb_ = t0 + 4 * q + k - 2, t0 + 4 * q + k
                            c = bass.ds(i * 4 + t, 1)
                            last_piece[:] = 2 * (ph["o"].b0 + 2 * q) + k, i * 8
                            complete()
                            m = m2[:, 0:1, :]
                            free(V.tensor_tensor(m, tile_ps(ta, SEQ).unsqueeze(1), gates[:, c, 0, :], ALU.mult), ta)
                            free(V.tensor_tensor(m2[:, 1:2, :], tile_ps(tb_, SEQ).unsqueeze(1), gates[:, c, 1, :], ALU.mult), tb_)
                            wait_tile_taken(dve, ta, i * 2)
                            wait_tile_taken(dve, tb_, i * 2)
                            V.tensor_tensor(ut[:, t % 2:t % 2 + 1, :], m, m2[:, 1:2, :], ALU.add).then_inc(u_ready, 1)
                            dve.wait_ge(xb_hi, i * 4 + (XB["o"] + t + 1))
                            V.tensor_tensor(xb[:, c, 1, :], ut[:, t % 2:t % 2 + 1, :], xb[:, c, 0, :].bitcast(F32), ALU.subtract).then_inc(xb_lo, 1)

            def sum_rows(name, j, last_of_sum):
                hc = h[:, j, X0:TOK]
                ins = V.tensor_copy(mean[:, 0:SEQ], hc) if j == 0 else V.tensor_tensor(mean[:, 0:SEQ], mean[:, 0:SEQ], hc, ALU.add)
                if last_of_sum:
                    ins.then_inc(sums, 1)
                    dve.wait_ge(sums, SUMS[name] + 1)
                else:
                    link(ins)

            def take_shift(name, feats):
                take((name, 0), lambda b: V.tensor_scalar(shift[:], b[:, 0:SEQ], 1.0 / feats, None, ALU.mult))
                wait_step_taken(dve, (name, 0))

            def ln_tile(name, ts, td, j, scale):
                residual(ts, td, slice(j, j + 1), scale)
                wait_tile_taken(dve, ts, td)
                if j == 8:
                    take_shift(name, D // 2)
                sum_rows(name, j, j == 7)
                n0 = SQN[name]
                if j >= 8:
                    for m in (j - 8, j):
                        V.tensor_tensor(h[:, m, X0:TOK], h[:, m, X0:TOK], shift[:], ALU.subtract).then_inc(shifted, 1)
                    if j > 8:
                        for m in range(2):
                            n = 2 * (j - 9) + m
                            add_square(n0 + n, n == 0)
                if j == 15:
                    add_square(n0 + 14, False)
                    last_square(n0 + 15)

            def layer_norm(name):
                l = LNS[name]
                key = (name, 1)
                b = step_bank(key)
                dve.wait_ge(step_done, steps[key] + 1)
                link(V.scalar_tensor_tensor(out=mean[:, 0:SEQ], in0=b[:, SEQ:2 * SEQ], scalar=1.0 / D, in1=shift[:], op0=ALU.mult, op1=ALU.subtract))
                V.tensor_copy(small[:, 9:10], mean[:, 0:1]).then_inc(delta, 1)
                link(V.tensor_tensor(shift[:], mean[:, 0:SEQ], mean[:, 0:SEQ], ALU.mult))
                link(V.tensor_scalar(shift[:], shift[:], LN_EPS, None, ALU.subtract))
                taken(V.scalar_tensor_tensor(out=rstd[:, 0:SEQ], in0=b[:, 0:SEQ], scalar=1.0 / D, in1=shift[:], op0=ALU.mult, op1=ALU.subtract), key)
                V.tensor_tensor(h[:, 0:4, X0:TOK], h[:, 0:4, X0:TOK], mean[:, 0:SEQ].unsqueeze(1).to_broadcast([P, 4, SEQ]),
                                ALU.subtract).then_inc(recentered, 1)
                dve.wait_ge(root, ROOTS[name] + 1)
                link(V.reciprocal(rstd[:, 0:SEQ], rstd[:, 0:SEQ]))
                norm_apply(name, SEQ, X0, h, V_LG + 16 * l)

            straight(ph["out2"], 0, 8, lambda ts, td, t, i: ln_tile("ln0", ts, td, 4 * i + t, ALPHA))
            layer_norm("ln0")

            def mem_side():
                def mem_low(j):
                    dve.wait_ge(memhi, 8 + j + 1)
                    taken(V.tensor_tensor(xa[:, j, 1, 0:SEQ], step_bank(("mem_o", j))[:, 0:SEQ], xa[:, j, 0, 0:SEQ].bitcast(F32),
                                          ALU.subtract), ("mem_o", j))

                yield
                for j in range(2):
                    yield
                    softmax_max(("mem_s", j), HEADS["mem"] + j, None, None)
                for j in range(H_MEM):
                    softmax_norm(("mem_s", j), HEADS["mem"] + j, True)
                    if j > 0:
                        mem_low(j - 1)
                    if j + 2 < H_MEM:
                        softmax_max(("mem_s", j + 2), HEADS["mem"] + j + 2, None, None)
                mem_low(H_MEM - 1)

            straight(ph["qm"], 0, 1, nothing)
            side[0] = mem_side()
            straight(ph["qm"], 1, 1, nothing)
            finish()
            for b in range(4):
                for half in range(2):
                    cut(2 * (ph["om"].b0 + b) + half + AHEAD, 0)
                    for q in range(2):
                        t = 4 * b + 2 * half + q
                        ts = ph["om"].t0 + t
                        last_piece[:] = 2 * (ph["om"].b0 + b) + half, 0
                        c = om_chunk(t)
                        residual(ts, 0, slice(c, c + 1), ALPHA)
            wait_tiles_taken(dve, ph["ffn"].t0)
            V.tensor_reduce(mean[:, 0:SEQ], h[:, :, X0:TOK].rearrange("p c n -> p n c"), AX.X, ALU.add).then_inc(sums, 1)
            take_shift("ln1", D)
            for q in range(4):
                V.tensor_tensor(h[:, 4 * q:4 * q + 4, X0:TOK], h[:, 4 * q:4 * q + 4, X0:TOK],
                                shift[:].unsqueeze(1).to_broadcast([P, 4, SEQ]), ALU.subtract).then_inc(shifted, 1)
            dve.wait_ge(squares, SQS["ln1"] + 4)
            V.tensor_reduce(acc[:, 0:SEQ], SQ[:, :, 0:SEQ].rearrange("p c n -> p n c"), AX.X, ALU.add).then_inc(sums, 1)
            layer_norm("ln1")

            b1, t1 = ph["ffn"].b0 + 44, ph["ffn"].t0 + 44
            for g in range(FF_GROUPS):
                with dve.Fori(0, 11) as i:
                    def ev(ts, td, t):
                        if t % 2 == 0:
                            return
                        j = t // 2
                        e = g * FF_CH + i * 2
                        dve.wait_ge(act_half, e + (8 + j + 1))
                        free(V.tensor_tensor(rt[:, j], tile_ps(ts - 1, SEQ), rt[:, j], ALU.mult), ts - 1)
                        complete()
                        wait_tile_taken(dve, ts - 1, td)
                        free(V.tensor_tensor(ut[:, j], tile_ps(ts, SEQ), rt[:, j], ALU.mult), ts)
                        dve.wait_ge(xb_hi, e + (XB["ffn"] + j + 1))
                        c = bass.ds(i * 2 + j, 1)
                        V.tensor_tensor(xb[:, c, 1, :], ut[:, j:j + 1, :], xb[:, c, 0, :].bitcast(F32), ALU.subtract).then_inc(xb_lo, 1)
                    body(ph["ffn"].b0, g * 68 + i * 4, ph["ffn"].t0, g * 15 + i, ev)
                if g < FF_GROUPS - 1:
                    with dve.Fori(0, 2) as i:
                        body(b1, g * 68 + i * 12, t1, g * 15 + i * 2,
                             lambda ts, td, t: residual(ts, td, bass.ds(i * 8 + t, 1), ALPHA if g == 0 else None), n_pairs=4, per_pair=3)
                else:
                    pieces_end[0] = 2 * ph["end"].b0
                    for q in range(8):
                        body(b1 + g * 68 + 3 * q, 0, t1 + g * 60 + 2 * q, 0,
                             lambda ts, td, t: ln_tile("ln2", ts, td, 2 * q + t, None), n_pairs=1, per_pair=3)
            layer_norm("ln2")


INPUTS = ["x", "meta_tokens", "norm1_w", "w_in", "gate_w2", "gate_b", "gla_norm_w", "pool_w", "pool_scale", "w_out",
          "norm2_w", "mlp_w1", "mlp_w2", "final_norm_w", "mem_2", "w_in_2", "b_gate_2", "kv_norm_g_2", "idx_k_norm_g_2",
          "idx_k_norm_b_2", "w_uk_2", "w_uv_2", "w_o_dsa_2", "w_o_moba_2", "w_out_2", "w_q_mem_2", "w_kv_mem_2",
          "w_o_mem_2", "w_ffn_in_2", "w_ffn_out_2", "ln_g_2", "ln_b_2"]


def kernel(**inputs):
    import numpy as _np
    import concourse.bacc as _bacc
    from concourse import mybir as _mybir
    from concourse.bass_utils import run_bass_kernel_spmd as _run

    nc = _bacc.Bacc("TRN2", target_bir_lowering=False, num_devices=1, dynamic_dma_scratch_size=8192)
    arrays, args = {}, {}
    for name in INPUTS:
        a = _np.ascontiguousarray(inputs[name])
        arrays[f"in_{name}"] = a
        args[name] = nc.dram_tensor(f"in_{name}", a.shape, _mybir.dt.from_np(a.dtype), kind="ExternalInput").ap()
    o = nc.dram_tensor("out_0", (1, SEQ, D), F32, kind="ExternalOutput").ap()
    program(nc, args, o)
    r = _run(nc, [arrays], core_ids=[0])
    return r.results[0]["out_0"]
```
